# Optimizing a Trainium2 kernel written in Bass

```python
import jax, jax.numpy as jnp
from jax import lax
import numpy as np

D_MODEL = 1024
BATCH = 1
SEQ = 1024
DEPTH = 2
DEC_BATCH = 8
DEC_SEQ = 16
PAST_LEN = 128

CHUNK = 64
Q_BLOCK = 128
N_MIXERS = 2
N_MLA = (DEPTH + 1) // 2
N_SB = DEPTH // 2
MLA_HEADS = 8
MLA_NOPE = 128
MLA_ROPE = 64
MLA_V = 128
MLA_Q_LORA = 512
MLA_KV_LORA = 256
MLA_IN = MLA_Q_LORA + MLA_KV_LORA + MLA_ROPE
ROPE_THETA = 10000.0
SB_HEADS = 16
SB_HEAD_DIM = 64
SB_WIDTH = SB_HEADS * SB_HEAD_DIM
D_FF = 4 * D_MODEL
EPS = 1e-6

kernel_name = 'hybrid_mla_stickbreaking_streaming_step'

def rmsnorm(x, g):
    xf = x.astype(jnp.float32)
    y = xf * lax.rsqrt(jnp.mean(xf * xf, axis=-1, keepdims=True) + EPS)
    return (y * g.astype(jnp.float32)).astype(x.dtype)

def rope_tables(pos):
    inv = ROPE_THETA ** (-jnp.arange(0, MLA_ROPE, 2, dtype=jnp.float32) / MLA_ROPE)
    ang = pos.astype(jnp.float32)[:, None] * inv[None, :]
    return jnp.cos(ang), jnp.sin(ang)

def apply_rope(x, cos, sin):
    half = x.shape[-1] // 2
    x1 = x[..., :half].astype(jnp.float32)
    x2 = x[..., half:].astype(jnp.float32)
    return jnp.concatenate([x1 * cos - x2 * sin, x2 * cos + x1 * sin], axis=-1).astype(x.dtype)

def mla_attend(q_nope, q_rope, q_pos, k_nope, k_rope, v, k_pos):
    scale = (MLA_NOPE + MLA_ROPE) ** -0.5
    s = (jnp.einsum('bqhd,bkhd->bhqk', q_nope, k_nope, preferred_element_type=jnp.float32)
         + jnp.einsum('bqhr,bkr->bhqk', q_rope, k_rope, preferred_element_type=jnp.float32)) * scale
    mask = (k_pos[None, :] // CHUNK) <= (q_pos[:, None] // CHUNK)
    s = jnp.where(mask[None, None], s, -jnp.inf)
    p = jax.nn.softmax(s, axis=-1)
    return jnp.einsum('bhqk,bkhd->bqhd', p.astype(v.dtype), v)

def sb_attend(q, q_pos, k, v, k_pos):
    z = jnp.einsum('bqhd,bkhd->bhqk', q, k, preferred_element_type=jnp.float32) * (SB_HEAD_DIM ** -0.5)
    mask = (k_pos[None, :] < q_pos[:, None])[None, None]
    log_keep = jnp.where(mask, jax.nn.log_sigmoid(-z), 0.0)
    suffix = lax.cumsum(log_keep, axis=3, reverse=True) - log_keep
    a = jnp.where(mask, jnp.exp(jax.nn.log_sigmoid(z) + suffix), 0.0)
    return jnp.einsum('bhqk,bkhd->bqhd', a.astype(v.dtype), v)

def attend_queries(attend, q_parts, q_pos, kv_args):
    B, S = q_parts[0].shape[:2]
    if S >= Q_BLOCK and S % Q_BLOCK == 0:
        nb = S // Q_BLOCK
        qb = tuple(q.reshape((B, nb, Q_BLOCK) + q.shape[2:]).swapaxes(0, 1) for q in q_parts)
        pb = q_pos.reshape(nb, Q_BLOCK)
        out = lax.map(lambda xs: attend(*xs[0], xs[1], *kv_args), (qb, pb))
        return out.swapaxes(0, 1).reshape((B, S) + out.shape[3:])
    return attend(*q_parts, q_pos, *kv_args)

def mla_mixer(h, q_pos, past_ckv, past_krope, w_in, g_q, w_qb, g_kv, w_kvb, w_o):
    B, S, _ = h.shape
    a = h @ w_in
    c_q = rmsnorm(a[..., :MLA_Q_LORA], g_q)
    c_kv = rmsnorm(a[..., MLA_Q_LORA:MLA_Q_LORA + MLA_KV_LORA], g_kv)
    cos, sin = rope_tables(q_pos)
    k_rope = apply_rope(a[..., MLA_Q_LORA + MLA_KV_LORA:], cos, sin)
    q = (c_q @ w_qb).reshape(B, S, MLA_HEADS, MLA_NOPE + MLA_ROPE)
    q_nope = q[..., :MLA_NOPE]
    q_rope = apply_rope(q[..., MLA_NOPE:], cos[:, None, :], sin[:, None, :])
    if past_ckv is None:
        ckv_all, kr_all, k_pos = c_kv, k_rope, q_pos
    else:
        ckv_all = jnp.concatenate([past_ckv, c_kv], axis=1)
        kr_all = jnp.concatenate([past_krope, k_rope], axis=1)
        k_pos = jnp.arange(past_ckv.shape[1] + S, dtype=jnp.int32)
    T = ckv_all.shape[1]
    kv = (ckv_all @ w_kvb).reshape(B, T, MLA_HEADS, MLA_NOPE + MLA_V)
    k_nope, v = kv[..., :MLA_NOPE], kv[..., MLA_NOPE:]
    out = attend_queries(mla_attend, (q_nope, q_rope), q_pos, (k_nope, kr_all, v, k_pos))
    return out.reshape(B, S, MLA_HEADS * MLA_V) @ w_o, c_kv, k_rope

def sb_mixer(h, q_pos, past_k, past_v, w_in, w_o):
    B, S, _ = h.shape
    qkv = (h @ w_in).reshape(B, S, 3, SB_HEADS, SB_HEAD_DIM)
    q, k, v = qkv[:, :, 0], qkv[:, :, 1], qkv[:, :, 2]
    if past_k is None:
        k_all, v_all, k_pos = k, v, q_pos
    else:
        k_all = jnp.concatenate([past_k, k], axis=1)
        v_all = jnp.concatenate([past_v, v], axis=1)
        k_pos = jnp.arange(past_k.shape[1] + S, dtype=jnp.int32)
    out = attend_queries(sb_attend, (q,), q_pos, (k_all, v_all, k_pos))
    return out.reshape(B, S, SB_WIDTH) @ w_o, k, v

def run_trunk(x, q_pos, caches, weights):
    (norm_mix, norm_mlp, norm_final, mla_w_in, mla_g_q, mla_w_qb, mla_g_kv, mla_w_kvb, mla_w_o,
     sb_w_in, sb_w_o, mlp_w_up, mlp_w_down) = weights
    ckv_l, kr_l, k_l, v_l = [], [], [], []
    for i in range(DEPTH):
        j = i // N_MIXERS
        h = rmsnorm(x, norm_mix[i])
        if i % N_MIXERS == 0:
            pc = caches[0][j] if caches is not None else None
            pk = caches[1][j] if caches is not None else None
            out, c, kr = mla_mixer(h, q_pos, pc, pk, mla_w_in[j], mla_g_q[j], mla_w_qb[j],
                                   mla_g_kv[j], mla_w_kvb[j], mla_w_o[j])
            ckv_l.append(c)
            kr_l.append(kr)
        else:
            pk = caches[2][j] if caches is not None else None
            pv = caches[3][j] if caches is not None else None
            out, k, v = sb_mixer(h, q_pos, pk, pv, sb_w_in[j], sb_w_o[j])
            k_l.append(k)
            v_l.append(v)
        x = x + out
        h = rmsnorm(x, norm_mlp[i])
        x = x + jnp.square(jax.nn.relu(h @ mlp_w_up[i])) @ mlp_w_down[i]
    y = rmsnorm(x, norm_final)
    return y, jnp.stack(ckv_l), jnp.stack(kr_l), jnp.stack(k_l), jnp.stack(v_l)

def setup_inputs(seed: int = 0) -> dict:
    key = jax.random.key(seed)
    ks = jax.random.split(key, 24)
    f32 = jnp.float32

    def w(k, shape, fan_in):
        return jax.random.normal(k, shape, f32) * (fan_in ** -0.5)

    def gain(k, shape):
        return 1.0 + 0.1 * jax.random.normal(k, shape, f32)

    return {
        'x_prompt': jax.random.normal(ks[0], (BATCH, SEQ, D_MODEL), f32),
        'x_sample': jax.random.normal(ks[1], (DEC_BATCH, DEC_SEQ, D_MODEL), f32),
        'cache_mla_ckv': jax.random.normal(ks[2], (N_MLA, DEC_BATCH, PAST_LEN, MLA_KV_LORA), f32),
        'cache_mla_krope': jax.random.normal(ks[3], (N_MLA, DEC_BATCH, PAST_LEN, MLA_ROPE), f32),
        'cache_sb_k': jax.random.normal(ks[4], (N_SB, DEC_BATCH, PAST_LEN, SB_HEADS, SB_HEAD_DIM), f32),
        'cache_sb_v': jax.random.normal(ks[5], (N_SB, DEC_BATCH, PAST_LEN, SB_HEADS, SB_HEAD_DIM), f32),
        'norm_mix': gain(ks[6], (DEPTH, D_MODEL)),
        'norm_mlp': gain(ks[7], (DEPTH, D_MODEL)),
        'norm_final': gain(ks[8], (D_MODEL,)),
        'mla_w_in': w(ks[9], (N_MLA, D_MODEL, MLA_IN), D_MODEL),
        'mla_g_q': gain(ks[10], (N_MLA, MLA_Q_LORA)),
        'mla_w_qb': w(ks[11], (N_MLA, MLA_Q_LORA, MLA_HEADS * (MLA_NOPE + MLA_ROPE)), MLA_Q_LORA),
        'mla_g_kv': gain(ks[12], (N_MLA, MLA_KV_LORA)),
        'mla_w_kvb': w(ks[13], (N_MLA, MLA_KV_LORA, MLA_HEADS * (MLA_NOPE + MLA_V)), MLA_KV_LORA),
        'mla_w_o': w(ks[14], (N_MLA, MLA_HEADS * MLA_V, D_MODEL), MLA_HEADS * MLA_V),
        'sb_w_in': w(ks[15], (N_SB, D_MODEL, 3 * SB_WIDTH), D_MODEL),
        'sb_w_o': w(ks[16], (N_SB, SB_WIDTH, D_MODEL), SB_WIDTH),
        'mlp_w_up': w(ks[17], (DEPTH, D_MODEL, D_FF), D_MODEL),
        'mlp_w_down': w(ks[18], (DEPTH, D_FF, D_MODEL), D_FF),
    }

def reference(x_prompt, x_sample, cache_mla_ckv, cache_mla_krope, cache_sb_k, cache_sb_v,
              norm_mix, norm_mlp, norm_final, mla_w_in, mla_g_q, mla_w_qb, mla_g_kv, mla_w_kvb,
              mla_w_o, sb_w_in, sb_w_o, mlp_w_up, mlp_w_down):
    weights = (norm_mix, norm_mlp, norm_final, mla_w_in, mla_g_q, mla_w_qb, mla_g_kv, mla_w_kvb,
               mla_w_o, sb_w_in, sb_w_o, mlp_w_up, mlp_w_down)
    past = cache_mla_ckv.shape[2]
    s_new = x_sample.shape[1]
    p_pos = jnp.arange(x_prompt.shape[1], dtype=jnp.int32)
    s_pos = past + jnp.arange(s_new, dtype=jnp.int32)
    y_prompt, p_ckv, p_kr, p_k, p_v = run_trunk(x_prompt, p_pos, None, weights)
    y_sample, s_ckv, s_kr, s_k, s_v = run_trunk(
        x_sample, s_pos, (cache_mla_ckv, cache_mla_krope, cache_sb_k, cache_sb_v), weights)
    return (y_prompt, y_sample, p_ckv, p_kr, p_k, p_v, s_ckv, s_kr, s_k, s_v)


_drawn_inputs = setup_inputs


def setup_inputs(seed=0):
    import zlib

    import numpy as np

    out = dict(_drawn_inputs(seed))
    spreads = {}
    factors = {'mla_g_q': 3.319}
    for name, (base, spread) in spreads.items():
        noise = np.random.default_rng([zlib.crc32(name.encode()), seed]).standard_normal(out[name].shape)
        drawn = base * np.exp(spread * noise) if base else spread * noise
        out[name] = __import__('jax').numpy.asarray(drawn.astype(out[name].dtype))
    for name, factor in factors.items():
        out[name] = (out[name] * factor).astype(out[name].dtype)
    return out
```

```python
from contextlib import ExitStack

import numpy as np

import concourse.bass as bass
from concourse import mybir

F32 = mybir.dt.float32
F32R = mybir.dt.float32r
BF16 = mybir.dt.bfloat16
ACT = mybir.ActivationFunctionType
ALU = mybir.AluOpType
AX = mybir.AxisListType

P = 128
D_MODEL = 1024
KT = D_MODEL // P
SEQ = 1024
DEC_BATCH, DEC_SEQ, PAST = 8, 16, 128
NPT = SEQ // P
NT = NPT + 1
TOK = NT * P
HEADS, NOPE, ROPE, VDIM = 8, 128, 64, 128
Q_LORA, KV_LORA = 512, 256
QT, CT = Q_LORA // P, KV_LORA // P
MLA_IN = Q_LORA + KV_LORA + ROPE
SB_HEADS, SB_DIM = 16, 64
D_FF = 4 * D_MODEL
EPS = 1e-6
THETA = 10000.0
CHUNK = 64
MLA_SCALE = float((NOPE + ROPE) ** -0.5)
SB_SCALE = float(SB_DIM ** -0.5)
MASKED = -1e30
KEYS = PAST + DEC_SEQ
GQ = 2 * P


def semaphores(nc, names):
    return {n: nc.alloc_semaphore(n) for n in names.split()}


def f32(ap):
    return ap.bitcast(F32)


def product(pe, out, w, m, start, stop):
    pe.matmul(out, w[0], m[0], start=start, stop=False)
    pe.matmul(out, w[0], m[1], start=False, stop=False)
    return pe.matmul(out, w[1], m[0], start=False, stop=stop)


def swap_halves(ap, heads):
    return ap.rearrange("p (h i c) -> p h i c", h=heads, i=2)[:, :, ::-1, :]


class Signal:

    def __init__(self, nc, name, credit=0):
        self.sem, self.credit = nc.alloc_semaphore(name), credit

    def start(self, engine):
        engine.sem_inc(self.sem, self.credit)

    def wait(self, engine, count):
        engine.wait_ge(self.sem, count + self.credit)


def mla_input_stage(nc, io, scratch):
    with nc.cleanup_on_exit(), ExitStack() as ctx:
        def sb(name, shape, dt=F32):
            return ctx.enter_context(nc.sbuf_tensor(name, shape, dt))

        x_in = [sb(f"a_x{u}", [P, D_MODEL]) for u in range(2)]
        square_junk = sb("a_junk", [P, D_MODEL])
        xn = sb("a_xn", [P, D_MODEL])
        gain_x = sb("a_gain_x", [P, D_MODEL])
        gain_q = sb("a_gain_q", [P, Q_LORA])
        gain_kv = sb("a_gain_kv", [P, KV_LORA])
        cos_t = sb("a_cos", [P, NT, ROPE])
        sin_t = sb("a_sin", [P, NT, ROPE])
        h_t = [[sb(f"a_h{u}{s}", [P, KT, P], F32R) for s in "hl"] for u in range(2)]
        w_raw = [sb(f"a_wraw{u}", [P, MLA_IN]) for u in range(2)]
        w_in = [sb(f"a_win{s}", [P, KT, MLA_IN], F32R) for s in "hl"]
        w_qr = [sb(f"a_wqr{s}", [P, QT, HEADS * ROPE], F32R) for s in "hl"]
        cq = sb("a_cq", [P, Q_LORA])
        ckv = [sb(f"a_ckv{u}", [P, KV_LORA]) for u in range(2)]
        kr = [sb(f"a_kr{u}", [P, 2 * ROPE]) for u in range(2)]
        kr_cos = sb("a_krc", [P, ROPE])
        kr_sin = sb("a_krs", [P, ROPE])
        qr = sb("a_qr", [P, HEADS * 2 * ROPE])
        qr_cos = sb("a_qrc", [P, HEADS * ROPE])
        qr_sin = sb("a_qrs", [P, HEADS * ROPE])
        qr_stack = [sb(f"a_qrst{u}", [P, HEADS, P], F32R) for u in range(2)]
        sums = sb("a_sums", [P, NT, 3])
        means = sb("a_means", [P, NT, 3])
        rs = sb("a_rs", [P, NT, 3])
        half = sb("a_half", [P, 1])
        bank = ctx.enter_context(nc.psum_tensor("a_ps", [P, 8, 512], F32))
        xt, a1, a2, cqt, ckt, qrp = (bank[:, 0:2, :], bank[:, 2, :], bank[:, 3, :], bank[:, 4, :],
                                     bank[:, 5, :], bank[:, 6, :])

        s = semaphores(nc, """a_const a_x0 a_x1 a_w0 a_w1 a_w_hi a_w_lo a_half a_sq a_mean a_rs a_xn a_xt
            a_h_hi a_h_lo a_a1 a_a2 a_cq_sq a_cq_mean a_cq_rs a_kv_sq a_kv_mean a_kv_rs a_cq a_ckv
            a_kr_mul a_kr a_cqt a_ckt a_cq_hi a_cq_lo a_ck_hi a_ck_lo a_qr a_qr_mul a_qrot a_qrt
            a_qrt_hi a_qrt_lo a_st0 a_st1 a_stq0 a_stq1""")
        cqT, ckvT, krT = io["cqT"], io["ckvT"], io["krT"]
        ident = io["ident"]
        NW = KT + QT
        x_rows = [io["x_prompt"][0, t * P:(t + 1) * P, :] for t in range(NPT)]
        x_rows.append(io["x_sample"].rearrange("b s d -> (b s) d"))
        N_CONST = 9

        block = ctx.enter_context(nc.Block())

        @block.sync
        def _(sp):
            def load_x(t):
                if t >= 2:
                    sp.wait_ge(s["a_xn"], t - 1)
                sp.dma_start(x_in[t % 2][:], x_rows[t]).then_inc(s[f"a_x{t % 2}"], 16)

            def load_w(n):
                if n >= 2:
                    sp.wait_ge(s["a_w_lo"], n - 1)
                if n < KT:
                    dst, src = w_raw[n % 2][:], io["mla_w_in"][0, n * P:(n + 1) * P, :]
                else:
                    k = n - KT
                    src = io["mla_w_qb"][0, k * P:(k + 1) * P, :].rearrange(
                        "p (h c) -> p h c", h=HEADS)[:, :, NOPE:]
                    dst = w_raw[n % 2][:, 0:HEADS * ROPE].rearrange("p (h c) -> p h c", h=HEADS)
                sp.dma_start(dst, src).then_inc(s[f"a_w{n % 2}"], 16)

            load_x(0)
            for dst, src in (
                    (gain_x[:], io["norm_mix"][0:1, :].broadcast_to([P, D_MODEL])),
                    (ident[:], io["ident_dram"]),
                    (gain_q[:], io["mla_g_q"][0:1, :].broadcast_to([P, Q_LORA])),
                    (gain_kv[:], io["mla_g_kv"][0:1, :].broadcast_to([P, KV_LORA])),
                    (cos_t[:], io["cos_dram"]), (sin_t[:], io["sin_dram"]),
                    (io["ident16"][:], io["ident16_dram"]), (io["chunk_mask"][:], io["chunk_mask_dram"]),
                    (io["causal_mask"][:], io["causal_mask_dram"])):
                sp.dma_start(dst, src).then_inc(s["a_const"], 16)
            load_x(1)
            for n in range(NW):
                load_w(n)

            def store(t):
                sp.wait_ge(s["a_ckv"], t + 1)
                c_out = io["new_p_ckv"][0, 0, t * P:(t + 1) * P, :] if t < NPT else \
                    io["new_s_ckv"][0].rearrange("b s d -> (b s) d")
                sp.dma_start(c_out, ckv[t % 2][:]).then_inc(s[f"a_st{t % 2}"], 16)
                sp.wait_ge(s["a_kr"], t + 1)
                k_out = io["new_p_krope"][0, 0, t * P:(t + 1) * P, :] if t < NPT else \
                    io["new_s_krope"][0].rearrange("b s d -> (b s) d")
                sp.dma_start(k_out, kr[t % 2][:, 0:ROPE]).then_inc(s[f"a_st{t % 2}"], 16)

            def store_q(t):
                sp.wait_ge(s["a_qrt_lo"], 2 * (t + 1))
                sp.dma_start(scratch["qr"][:, :, t * P:(t + 1) * P].rearrange("h p c -> p h c"),
                             f32(qr_stack[t % 2][:])).then_inc(s[f"a_stq{t % 2}"], 16)

            for t in range(NT):
                if t + 2 < NT:
                    load_x(t + 2)
                store(t)
                if t >= 1:
                    store_q(t - 1)
            store_q(NT - 1)
            for u in range(2):
                uses = (NT + 1 - u) // 2
                sp.wait_ge(s[f"a_st{u}"], 32 * uses)
                sp.wait_ge(s[f"a_stq{u}"], 16 * uses)

        @block.scalar
        def _(act):
            def squares(t):
                act.wait_ge(s[f"a_x{t % 2}"], 16 * (t // 2 + 1))
                if t >= 1:
                    act.wait_ge(s["a_sq"], t)
                act.activation(square_junk[:], x_in[t % 2][:], ACT.Square,
                               accum_out=sums[:, t, 0:1]).then_inc(s["a_sq"], 1)

            def h_hi(t):
                for b in range(2):
                    act.wait_ge(s["a_xt"], 2 * t + b + 1)
                    if t >= 2:
                        act.wait_ge(s["a_a2"], t - 1)
                    act.copy(h_t[t % 2][0][:, 4 * b:4 * b + 4, :], xt[:, b, :].rearrange(
                        "p (k c) -> p k c", k=4)).then_inc(s["a_h_hi"], 1)

            def latents_hi(t):
                act.wait_ge(s["a_cqt"], t + 1)
                act.copy(cqT[0][:, :, t * P:(t + 1) * P],
                         cqt.rearrange("p (k c) -> p k c", k=QT)).then_inc(s["a_cq_hi"], 1)
                act.wait_ge(s["a_ckt"], t + 1)
                act.copy(ckvT[0][:, :, t * P:(t + 1) * P],
                         ckt[:, 0:CT * P].rearrange("p (k c) -> p k c", k=CT)).then_inc(s["a_ck_hi"], 1)
                act.copy(krT[0][:, t * P:(t + 1) * P], ckt[:, CT * P:CT * P + P]).then_inc(s["a_ck_hi"], 1)

            def q_rope_hi(t):
                for b in range(2):
                    act.wait_ge(s["a_qrt"], 2 * t + b + 1)
                    if t >= 2:
                        act.wait_ge(s[f"a_stq{t % 2}"], 16 * (t // 2))
                    act.copy(qr_stack[t % 2][:, 4 * b:4 * b + 4, :], bank[:, 4 + b, :].rearrange(
                        "p (k c) -> p k c", k=4)).then_inc(s["a_qrt_hi"], 1)

            squares(0)
            squares(1)
            for n in range(NW):
                act.wait_ge(s[f"a_w{n % 2}"], 16 * (n // 2 + 1))
                dst = w_in[0][:, n, :] if n < KT else w_qr[0][:, n - KT, :]
                act.copy(dst, w_raw[n % 2][:, 0:dst.shape[1]]).then_inc(s["a_w_hi"], 1)
                if n == 1:
                    h_hi(0)
            for t in range(NT + 1):
                if t + 2 < NT:
                    squares(t + 2)
                if t + 1 < NT:
                    h_hi(t + 1)
                if t >= 1:
                    latents_hi(t - 1)
                if t < NT:
                    act.wait_ge(s["a_a1"], t + 1)
                    act.wait_ge(s["a_sq"], min(t + 3, NT))
                    if t >= 1:
                        act.wait_ge(s["a_kv_sq"], t)
                    act.activation(square_junk[:, 0:Q_LORA], a1, ACT.Square,
                                   accum_out=sums[:, t, 1:2]).then_inc(s["a_cq_sq"], 1)
                    act.wait_ge(s["a_a2"], t + 1)
                    act.wait_ge(s["a_cq_sq"], t + 1)
                    act.activation(square_junk[:, 0:KV_LORA], a2[:, 0:KV_LORA], ACT.Square,
                                   accum_out=sums[:, t, 2:3]).then_inc(s["a_kv_sq"], 1)
                if t >= 1:
                    q_rope_hi(t - 1)

        @block.gpsimd
        def _(pool):
            pool.memset(half[:], -0.5).then_inc(s["a_half"], 1)
            pool.wait_ge(s["a_half"], 1)

            def inverse_rms(t, kind, n, squared, mean, done):
                pool.wait_ge(s[squared], t + 1)
                pool.tensor_scalar(means[:, t, kind:kind + 1], sums[:, t, kind:kind + 1], 1.0 / n, EPS,
                                   ALU.mult, ALU.add).then_inc(s[mean], 1)
                pool.wait_ge(s[mean], t + 1)
                pool.tensor_tensor(rs[:, t, kind:kind + 1], means[:, t, kind:kind + 1], half[:],
                                   ALU.pow).then_inc(s[done], 1)

            inverse_rms(0, 0, D_MODEL, "a_sq", "a_mean", "a_rs")
            inverse_rms(1, 0, D_MODEL, "a_sq", "a_mean", "a_rs")
            for t in range(NT):
                if t + 2 < NT:
                    inverse_rms(t + 2, 0, D_MODEL, "a_sq", "a_mean", "a_rs")
                inverse_rms(t, 1, Q_LORA, "a_cq_sq", "a_cq_mean", "a_cq_rs")
                inverse_rms(t, 2, KV_LORA, "a_kv_sq", "a_kv_mean", "a_kv_rs")

        @block.vector
        def _(dve):
            def normalise_x(t):
                dve.wait_ge(s["a_rs"], t + 1)
                if t >= 1:
                    dve.wait_ge(s["a_xt"], 2 * t)
                dve.scalar_tensor_tensor(out=xn[:], in0=x_in[t % 2][:], scalar=rs[:, t, 0:1],
                                         in1=gain_x[:], op0=ALU.mult, op1=ALU.mult).then_inc(s["a_xn"], 1)

            def h_lo(t):
                for b in range(2):
                    dve.wait_ge(s["a_h_hi"], 2 * t + b + 1)
                    dst = [h_t[t % 2][i][:, 4 * b:4 * b + 4, :] for i in range(2)]
                    dve.tensor_tensor(dst[1], xt[:, b, :].rearrange("p (k c) -> p k c", k=4),
                                      f32(dst[0]), ALU.subtract).then_inc(s["a_h_lo"], 1)

            def latents_lo(t):
                cols = slice(t * P, (t + 1) * P)
                dve.wait_ge(s["a_cq_hi"], t + 1)
                dve.tensor_tensor(cqT[1][:, :, cols], cqt.rearrange("p (k c) -> p k c", k=QT),
                                  f32(cqT[0][:, :, cols]), ALU.subtract).then_inc(s["a_cq_lo"], 1)
                dve.wait_ge(s["a_ck_hi"], 2 * (t + 1))
                dve.tensor_tensor(ckvT[1][:, :, cols], ckt[:, 0:CT * P].rearrange("p (k c) -> p k c", k=CT),
                                  f32(ckvT[0][:, :, cols]), ALU.subtract).then_inc(s["a_ck_lo"], 1)
                dve.tensor_tensor(krT[1][:, cols], ckt[:, CT * P:CT * P + P],
                                  f32(krT[0][:, cols]), ALU.subtract).then_inc(s["a_ck_lo"], 1)

            def rotate(out, parts, src, heads, t, mul_sem, done_sem, waits):
                for sem, v in waits:
                    dve.wait_ge(s[sem], v)
                table = [x[:, t:t + 1, :].rearrange("p o (i c) -> p o i c", i=2).broadcast_to(
                    [P, heads, 2, ROPE // 2]) for x in (cos_t[:], sin_t[:])]
                view = [x.rearrange("p (h i c) -> p h i c", h=heads, i=2) for x in (*parts, src)]
                dve.tensor_tensor(view[0], view[2], table[0], ALU.mult).then_inc(s[mul_sem], 1)
                dve.tensor_tensor(view[1], swap_halves(src, heads), table[1],
                                  ALU.mult).then_inc(s[mul_sem], 1)
                dve.wait_ge(s[mul_sem], 2 * (t + 1))
                twice = [x.rearrange("p (h o c) -> p h o c", h=heads, o=1).broadcast_to(
                    [P, heads, 2, ROPE]) for x in parts]
                dve.tensor_tensor(out.rearrange("p (h i c) -> p h i c", h=heads, i=2), *twice,
                                  ALU.add).then_inc(s[done_sem], 1)

            def q_rope_lo(t):
                for b in range(2):
                    dve.wait_ge(s["a_qrt_hi"], 2 * t + b + 1)
                    low = qr_stack[t % 2][ROPE:P, 4 * b:4 * b + 4, :]
                    dve.tensor_tensor(low, bank[ROPE:P, 4 + b, :].rearrange("p (k c) -> p k c", k=4),
                                      f32(low), ALU.subtract).then_inc(s["a_qrt_lo"], 1)

            dve.wait_ge(s["a_const"], 16 * N_CONST)
            normalise_x(0)
            for n in range(NW):
                dve.wait_ge(s["a_w_hi"], n + 1)
                hi, lo = (w_in[0][:, n, :], w_in[1][:, n, :]) if n < KT else \
                    (w_qr[0][:, n - KT, :], w_qr[1][:, n - KT, :])
                dve.tensor_tensor(lo, w_raw[n % 2][:, 0:lo.shape[1]], f32(hi),
                                  ALU.subtract).then_inc(s["a_w_lo"], 1)
                if n == 2:
                    h_lo(0)
                    normalise_x(1)
            for t in range(NT + 1):
                if t + 1 < NT:
                    h_lo(t + 1)
                if t + 2 < NT:
                    normalise_x(t + 2)
                if t >= 1:
                    latents_lo(t - 1)
                if t < NT:
                    dve.wait_ge(s["a_cq_rs"], t + 1)
                    if t >= 1:
                        dve.wait_ge(s["a_cqt"], t)
                    dve.scalar_tensor_tensor(out=cq[:], in0=a1, scalar=rs[:, t, 1:2], in1=gain_q[:],
                                             op0=ALU.mult, op1=ALU.mult).then_inc(s["a_cq"], 1)
                if t >= 1:
                    waits = [("a_qr", t)]
                    if t >= 2:
                        waits += [("a_qrot", t - 1), ("a_qrt", 2 * (t - 1))]
                    rotate(qr[:], (qr_cos[:], qr_sin[:]), qrp, HEADS, t - 1, "a_qr_mul", "a_qrot", waits)
                if t < NT:
                    dve.wait_ge(s["a_kv_rs"], t + 1)
                    if t >= 2:
                        dve.wait_ge(s[f"a_st{t % 2}"], 32 * (t // 2))
                        dve.wait_ge(s["a_ckt"], t - 1)
                    dve.scalar_tensor_tensor(out=ckv[t % 2][:], in0=a2[:, 0:KV_LORA],
                                             scalar=rs[:, t, 2:3], in1=gain_kv[:],
                                             op0=ALU.mult, op1=ALU.mult).then_inc(s["a_ckv"], 1)
                    waits = [("a_kr", t)] if t >= 1 else []
                    rotate(kr[t % 2][:], (kr_cos[:], kr_sin[:]), a2[:, KV_LORA:KV_LORA + ROPE], 1, t,
                           "a_kr_mul", "a_kr", waits)
                if t >= 1:
                    q_rope_lo(t - 1)

        @block.tensor
        def _(pe):
            def transpose_x(t):
                pe.wait_ge(s["a_xn"], t + 1)
                for b in range(2):
                    if t >= 1:
                        pe.wait_ge(s["a_h_lo"], 2 * (t - 1) + b + 1)
                    for k in range(4):
                        last = pe.transpose(xt[:, b, k * P:(k + 1) * P],
                                            xn[:, (4 * b + k) * P:(4 * b + k + 1) * P], ident[:])
                    last.then_inc(s["a_xt"], 1)

            def transpose_latents(t):
                pe.wait_ge(s["a_cq"], t + 1)
                if t >= 1:
                    pe.wait_ge(s["a_qrt_lo"], 2 * t)
                for k in range(QT):
                    last = pe.transpose(cqt[:, k * P:(k + 1) * P], cq[:, k * P:(k + 1) * P], ident[:])
                last.then_inc(s["a_cqt"], 1)
                pe.wait_ge(s["a_ckv"], t + 1)
                pe.wait_ge(s["a_kr"], t + 1)
                for k in range(CT):
                    pe.transpose(ckt[:, k * P:(k + 1) * P], ckv[t % 2][:, k * P:(k + 1) * P], ident[:])
                pe.transpose(ckt[:, CT * P:CT * P + P], kr[t % 2][:], ident[:]).then_inc(s["a_ckt"], 1)

            def rotary_queries(t):
                pe.wait_ge(s["a_cq_lo"], t + 1)
                if t >= 1:
                    pe.wait_ge(s["a_qrot"], t)
                for k in range(QT):
                    last = product(pe, qrp, [c[:, k, t * P:(t + 1) * P] for c in cqT],
                                   [w[:, k, :] for w in w_qr], k == 0, k == QT - 1)
                last.then_inc(s["a_qr"], 1)

            def transpose_rotary(t):
                pe.wait_ge(s["a_qrot"], t + 1)
                pe.wait_ge(s["a_ck_lo"], 2 * (t + 1))
                for b in range(2):
                    for k in range(4):
                        h = 4 * b + k
                        last = pe.transpose(bank[:, 4 + b, k * P:(k + 1) * P],
                                            qr[:, h * P:(h + 1) * P], ident[:])
                    last.then_inc(s["a_qrt"], 1)

            def project(t, out, c0, c1, done, emptied):
                for sem, v in emptied:
                    pe.wait_ge(s[sem], v)
                pe.wait_ge(s["a_h_lo"], 2 * (t + 1))
                for k in range(KT):
                    if t == 0:
                        pe.wait_ge(s["a_w_lo"], k + 1)
                    last = product(pe, out[:, 0:c1 - c0], [h[:, k, :] for h in h_t[t % 2]],
                                   [w[:, k, c0:c1] for w in w_in], k == 0, k == KT - 1)
                last.then_inc(s[done], 1)

            pe.wait_ge(s["a_const"], 16 * N_CONST)
            transpose_x(0)
            for t in range(NT + 1):
                if t + 1 < NT:
                    transpose_x(t + 1)
                if t >= 1:
                    transpose_latents(t - 1)
                if t < NT:
                    project(t, a1, 0, Q_LORA, "a_a1", [("a_cq", t)] if t else [])
                if t == 1:
                    pe.wait_ge(s["a_w_lo"], NW)
                if t >= 1:
                    rotary_queries(t - 1)
                if t < NT:
                    project(t, a2, Q_LORA, MLA_IN, "a_a2", [("a_kr", t)] if t else [])
                if t >= 1:
                    transpose_rotary(t - 1)


def score_columns(q):
    used = (q + 1) * P
    keys = max(used, 2 * P)
    first = P if keys == 640 else 0
    chunks, at = [], first
    while at < first + keys:
        end = min(512 * (at // 512 + 1), first + keys)
        chunks.append((at, end - at, at - first))
        at = end
    return first, chunks, used


def transpose_tasks(n):
    q = n % NPT
    order = [(q, 0)] + [(k, k + 1) for k in range(q)] if q % 2 else [(k, k + 1) for k in range(q + 1)]
    return [order[i:i + 4] for i in range(0, len(order), 4)]


def tasks_before(n):
    return sum(len(transpose_tasks(m)) for m in range(n))


STEPS = 2 * NPT
T_TASKS = tasks_before(STEPS)
GROUPS = STEPS // 2


def mla_attention_stage(nc, io, scratch):
    PAIRS = HEADS // 2
    Q_TASKS, K_TASKS, V_TASKS = 2 * 3, 2 * 2, NPT // 2
    PROJ = Q_TASKS + K_TASKS + V_TASKS
    WEIGHTS_AT = 6
    with nc.cleanup_on_exit(), ExitStack() as ctx:
        def sb(name, shape, dt=F32):
            return ctx.enter_context(nc.sbuf_tensor(name, shape, dt))

        wq_raw = sb("b_wq_raw", [P, QT, 2, NOPE])
        wkv_raw = sb("b_wkv_raw", [P, CT, 2, NOPE + VDIM])
        wq = [sb(f"b_wq{s}", [P, QT, 2, NOPE], F32R) for s in "hl"]
        wkv = [sb(f"b_wkv{s}", [P, CT, 2, NOPE + VDIM], F32R) for s in "hl"]
        qn = [sb(f"b_qn{s}", [P, 2, TOK], F32R) for s in "hl"]
        kn = [sb(f"b_kn{s}", [P, 2, SEQ], F32R) for s in "hl"]
        v = [sb(f"b_v{s}", [P, NPT, 2 * VDIM], F32R) for s in "hl"]
        qr = sb("b_qr", [P, 2, SEQ], F32R)
        prob = [sb(f"b_p{u}", [P, SEQ]) for u in range(3)]
        pt = [[sb(f"b_pt{u}{s}", [P, NPT, GQ], F32R) for s in "hl"] for u in range(2)]
        o_st = [sb(f"b_o{u}", [P, GQ]) for u in range(2)]
        stat = sb("b_stat", [P, STEPS, 4])
        bank = ctx.enter_context(nc.psum_tensor("b_ps", [P, 8, 512], F32))
        score = [bank[:, 2 * u:2 * u + 2, :].rearrange("p b c -> p (b c)") for u in range(2)]
        cqT, ckvT, krT, ident = io["cqT"], io["ckvT"], io["krT"], io["ident"]

        def signal(name, credit=0):
            return Signal(nc, name, credit)

        wq_in, wkv_in, qr_in = signal("b_wq_in"), signal("b_wkv_in"), signal("b_qr_in")
        w_hi, w_lo = signal("b_w_hi"), signal("b_w_lo")
        proj = signal("b_proj", 1)
        proj_hi, proj_lo = signal("b_proj_hi"), signal("b_proj_lo", 4)
        q_smp_done = signal("b_q_smp")
        s_done = signal("b_s")
        nmax, nbias = signal("b_nmax", 1), signal("b_nbias")
        exp_done = signal("b_exp", 2)
        recip, normed = signal("b_recip"), signal("b_normed")
        t_done, t_hi, t_lo = signal("b_t"), signal("b_t_hi"), signal("b_t_lo", 3)
        zero_done = signal("b_zero")
        pv_done, o_done = signal("b_pv", 2), signal("b_o", 1)
        o_out = [signal(f"b_o_out{u}", 16) for u in range(2)]

        def task_bank(m):
            return bank[:, 4 + m % 3, :]

        def pairs(engine, body):
            with engine.Fori(0, PAIRS - 1) as i:
                body(i, False)
            body(PAIRS - 1, True)

        block = ctx.enter_context(nc.Block())

        @block.sync
        def _(sp):
            def load_weights(i):
                for a in range(2):
                    sp.dma_start(wq_raw[:, :, a, :], io["mla_w_qb"][0].rearrange(
                        "(k p) (h c) -> p k h c", p=P, h=HEADS)[:, :, 2 * i + a, 0:NOPE]).then_inc(wq_in.sem, 16)
                sp.dma_start(wkv_raw[:].rearrange("p k a c -> p k (a c)"),
                             io["mla_w_kvb"][0].rearrange("(k p) n -> p k n", p=P)[
                    :, :, bass.ds(i * 2 * (NOPE + VDIM), 2 * (NOPE + VDIM))]).then_inc(wkv_in.sem, 16)

            def load_rotary(i):
                sp.dma_start(f32(qr[:]), scratch["qr"][bass.ds(2 * i, 2), :, 0:SEQ].rearrange(
                    "h p c -> p h c")).then_inc(qr_in.sem, 16)

            def store(i, g):
                o_done.wait(sp, i * GROUPS + g + 1)
                cols = slice((g % 4) * GQ, (g % 4 + 1) * GQ)
                sp.dma_start(scratch["oT"][2 * i + g // 4, :, cols], o_st[g % 2][:]).then_inc(
                    o_out[g % 2].sem, 16)

            for x in o_out:
                x.start(sp)
            load_weights(0)
            load_rotary(0)
            w_lo.wait(sp, 2)
            load_weights(1)

            def body(i, more_weights, more_pairs):
                for g in range(GROUPS - 1):
                    store(i, g)
                if more_weights:
                    w_lo.wait(sp, 2 * (i + 2))
                    load_weights(i + 2)
                if more_pairs:
                    s_done.wait(sp, STEPS * (i + 1))
                    load_rotary(i + 1)
                store(i, GROUPS - 1)

            with sp.Fori(0, PAIRS - 2) as i:
                body(i, True, True)
            body(PAIRS - 2, False, True)
            body(PAIRS - 1, False, False)
            for x in o_out:
                x.wait(sp, 16 * PAIRS * GROUPS // 2)

        @block.scalar
        def _(act):
            exp_done.start(act)
            o_done.start(act)

            def weights_hi(i):
                wq_in.wait(act, 32 * (i + 1))
                act.copy(wq[0][:], wq_raw[:]).then_inc(w_hi.sem, 1)
                wkv_in.wait(act, 16 * (i + 1))
                act.copy(wkv[0][:], wkv_raw[:]).then_inc(w_hi.sem, 1)

            def body(i, last):
                def project_hi(n):
                    proj.wait(act, PROJ * i + n + 1)
                    ps = bank[:, 4 + n % 4, :]
                    if n < Q_TASKS:
                        a, c = n // 3, n % 3
                        act.copy(qn[0][:, a, c * 384:(c + 1) * 384], ps[:, 0:384]).then_inc(proj_hi.sem, 1)
                        if c == 2:
                            act.copy(io["q_smp"][:, 2 * i + a, :], ps[:, 256:384]).then_inc(q_smp_done.sem, 1)
                    elif n < Q_TASKS + K_TASKS:
                        a, c = (n - Q_TASKS) // 2, (n - Q_TASKS) % 2
                        act.copy(kn[0][:, a, c * 512:(c + 1) * 512], ps).then_inc(proj_hi.sem, 1)
                    else:
                        t = 2 * (n - Q_TASKS - K_TASKS)
                        act.copy(v[0][:, t:t + 2, :], ps.rearrange("p (t c) -> p t c", t=2)).then_inc(
                            proj_hi.sem, 1)

                def exponential(n):
                    first, _, used = score_columns(n % NPT)
                    nbias.wait(act, STEPS * i + n + 1)
                    if n >= 3:
                        t_done.wait(act, T_TASKS * i + tasks_before(n - 2))
                    act.activation(prob[n % 3][:, 0:used], score[n % 2][:, first:first + used], ACT.Exp,
                                   bias=stat[:, n, 1:2], scale=MLA_SCALE,
                                   accum_out=stat[:, n, 2:3]).then_inc(exp_done.sem, 1)

                def transposed_hi(n):
                    g, at = n // 2, (n % 2) * P
                    for j, task in enumerate(transpose_tasks(n)):
                        m = tasks_before(n) + j
                        t_done.wait(act, T_TASKS * i + m + 1)
                        pv_done.wait(act, GROUPS * i + g - 1)
                        s0 = task[0][1]
                        act.copy(pt[g % 2][0][:, s0:s0 + len(task), at:at + P],
                                 task_bank(m)[:, 0:len(task) * P].rearrange(
                                     "p (s c) -> p s c", c=P)).then_inc(t_hi.sem, 1)

                def output(g):
                    pv_done.wait(act, GROUPS * i + g + 1)
                    o_out[g % 2].wait(act, 16 * (GROUPS // 2 * i + g // 2))
                    act.copy(o_st[g % 2][:], bank[:, 7, 0:GQ]).then_inc(o_done.sem, 1)

                for n in range(Q_TASKS + K_TASKS):
                    project_hi(n)
                exponential(0)
                for n in range(Q_TASKS + K_TASKS, PROJ):
                    project_hi(n)
                exponential(1)
                for n in range(STEPS):
                    if n + 2 < STEPS:
                        exponential(n + 2)
                    if n == WEIGHTS_AT and not last:
                        weights_hi(i + 1)
                    transposed_hi(n)
                    if n % 2 == 0 and n >= 2:
                        output(n // 2 - 1)
                output(GROUPS - 1)

            weights_hi(0)
            pairs(act, body)

        @block.vector
        def _(dve):
            nmax.start(dve)
            proj_lo.start(dve)
            t_lo.start(dve)
            for u in range(2):
                for x in pt[u]:
                    dve.memset(f32(x[:, 0, 0:P]), 0.0).then_inc(zero_done.sem, 1)

            def weights_lo(i):
                w_hi.wait(dve, 2 * i + 1)
                dve.tensor_tensor(wq[1][:], wq_raw[:], f32(wq[0][:]), ALU.subtract).then_inc(w_lo.sem, 1)
                w_hi.wait(dve, 2 * i + 2)
                dve.tensor_tensor(wkv[1][:], wkv_raw[:], f32(wkv[0][:]), ALU.subtract).then_inc(w_lo.sem, 1)

            def body(i, last):
                def project_lo(n):
                    proj_hi.wait(dve, PROJ * i + n + 1)
                    if n < Q_TASKS and n % 3 == 2:
                        q_smp_done.wait(dve, 2 * i + n // 3 + 1)
                    ps = bank[:, 4 + n % 4, :]
                    if n < Q_TASKS:
                        a, c = n // 3, n % 3
                        out, hi, src = (*(x[:, a, c * 384:(c + 1) * 384] for x in qn[::-1]), ps[:, 0:384])
                    elif n < Q_TASKS + K_TASKS:
                        a, c = (n - Q_TASKS) // 2, (n - Q_TASKS) % 2
                        out, hi, src = (*(x[:, a, c * 512:(c + 1) * 512] for x in kn[::-1]), ps)
                    else:
                        t = 2 * (n - Q_TASKS - K_TASKS)
                        out, hi, src = (*(x[:, t:t + 2, :] for x in v[::-1]),
                                        ps.rearrange("p (t c) -> p t c", t=2))
                    dve.tensor_tensor(out, src, f32(hi), ALU.subtract).then_inc(proj_lo.sem, 1)

                def maximum(n):
                    first, _, used = score_columns(n % NPT)
                    s_done.wait(dve, STEPS * i + n + 1)
                    exp_done.wait(dve, STEPS * i + n - 1)
                    dve.tensor_reduce(stat[:, n, 0:1], score[n % 2][:, first:first + used], AX.X, ALU.max,
                                      negate=True).then_inc(nmax.sem, 1)
                    nmax.wait(dve, STEPS * i + n + 1)
                    dve.tensor_scalar(stat[:, n, 1:2], stat[:, n, 0:1], MLA_SCALE, None,
                                      ALU.mult).then_inc(nbias.sem, 1)

                def normalise(n):
                    used = (n % NPT + 1) * P
                    exp_done.wait(dve, STEPS * i + n + 1)
                    dve.reciprocal(stat[:, n, 3:4], stat[:, n, 2:3]).then_inc(recip.sem, 1)
                    recip.wait(dve, STEPS * i + n + 1)
                    dve.tensor_scalar(prob[n % 3][:, 0:used], prob[n % 3][:, 0:used], stat[:, n, 3:4], None,
                                      ALU.mult).then_inc(normed.sem, 1)

                def transposed_lo(n):
                    g, at = n // 2, (n % 2) * P
                    for j, task in enumerate(transpose_tasks(n)):
                        m = tasks_before(n) + j
                        t_hi.wait(dve, T_TASKS * i + m + 1)
                        s0 = task[0][1]
                        hi, lo = (x[:, s0:s0 + len(task), at:at + P] for x in pt[g % 2])
                        dve.tensor_tensor(lo, task_bank(m)[:, 0:len(task) * P].rearrange(
                            "p (s c) -> p s c", c=P), f32(hi), ALU.subtract).then_inc(t_lo.sem, 1)

                for n in range(Q_TASKS + K_TASKS):
                    project_lo(n)
                maximum(0)
                maximum(1)
                for n in range(Q_TASKS + K_TASKS, PROJ):
                    project_lo(n)
                maximum(2)
                normalise(0)
                for n in range(STEPS):
                    if n + 3 < STEPS:
                        maximum(n + 3)
                    if n + 1 < STEPS:
                        normalise(n + 1)
                    if n == WEIGHTS_AT and not last:
                        weights_lo(i + 1)
                    transposed_lo(n)

            weights_lo(0)
            pairs(dve, body)

        @block.tensor
        def _(pe):
            proj.start(pe)
            pv_done.start(pe)

            def body(i, last):
                def project(n):
                    proj_lo.wait(pe, PROJ * i + n - 3)
                    ps = bank[:, 4 + n % 4, :]
                    if n < Q_TASKS:
                        a, c = n // 3, n % 3
                        for k in range(QT):
                            last = product(pe, ps[:, 0:384], [w[:, k, a, :] for w in wq],
                                           [x[:, k, c * 384:(c + 1) * 384] for x in cqT], k == 0, k == QT - 1)
                    elif n < Q_TASKS + K_TASKS:
                        a, c = (n - Q_TASKS) // 2, (n - Q_TASKS) % 2
                        for k in range(CT):
                            last = product(pe, ps, [w[:, k, a, 0:NOPE] for w in wkv],
                                           [x[:, k, c * 512:(c + 1) * 512] for x in ckvT], k == 0, k == CT - 1)
                    else:
                        for j in range(2):
                            t = 2 * (n - Q_TASKS - K_TASKS) + j
                            for k in range(CT):
                                last = product(pe, ps[:, j * GQ:(j + 1) * GQ],
                                               [x[:, k, t * P:(t + 1) * P] for x in ckvT],
                                               [w[:, k, :, NOPE:] for w in wkv], k == 0, k == CT - 1)
                    last.then_inc(proj.sem, 1)

                def scores(n):
                    a, q = n // NPT, n % NPT
                    tile = slice(q * P, (q + 1) * P)
                    exp_done.wait(pe, STEPS * i + n - 1)
                    first, chunks, used = score_columns(q)
                    for at, width, key in chunks:
                        out = score[n % 2][:, at:at + width]
                        keys = slice(key, key + width)
                        product(pe, out, [x[:, a, tile] for x in qn], [x[:, a, keys] for x in kn], True, False)
                        pe.matmul(out, qr[:, a, tile], krT[0][:, keys], start=False, stop=False)
                        last_chunk = (at, width, key) == chunks[-1]
                        last = pe.matmul(out, qr[:, a, tile], krT[1][:, keys], start=False, stop=not last_chunk)
                    end = first + used
                    last = pe.matmul(score[n % 2][:, end - P:end], io["ident16"][:], io["chunk_mask"][:],
                                     start=False, stop=True)
                    last.then_inc(s_done.sem, 1)

                def transposes(n):
                    normed.wait(pe, STEPS * i + n + 1)
                    for j, task in enumerate(transpose_tasks(n)):
                        m = tasks_before(n) + j
                        t_lo.wait(pe, T_TASKS * i + m - 2)
                        for c, (k, _) in enumerate(task):
                            last = pe.transpose(task_bank(m)[:, c * P:(c + 1) * P],
                                                prob[n % 3][:, k * P:(k + 1) * P], ident[:])
                        last.then_inc(t_done.sem, 1)

                def values(g):
                    a, last_q = g // 4, 2 * (g % 4) + 1
                    t_lo.wait(pe, T_TASKS * i + tasks_before(2 * g + 2))
                    o_done.wait(pe, GROUPS * i + g)
                    order = [(last_q, 0)] + [(k, k + 1) for k in range(last_q)]
                    for k, slot in order:
                        last = product(pe, bank[:, 7, 0:GQ],
                                       [x[:, k, a * VDIM:(a + 1) * VDIM] for x in v],
                                       [x[:, slot, :] for x in pt[g % 2]], k == last_q, k == last_q - 1)
                    last.then_inc(pv_done.sem, 1)

                t_lo.wait(pe, T_TASKS * i)
                o_done.wait(pe, GROUPS * i)
                w_lo.wait(pe, 2 * (i + 1))
                for n in range(Q_TASKS + K_TASKS):
                    project(n)
                proj_lo.wait(pe, PROJ * i + Q_TASKS + K_TASKS)
                qr_in.wait(pe, 16 * (i + 1))
                scores(0)
                scores(1)
                for n in range(Q_TASKS + K_TASKS, PROJ):
                    project(n)
                proj_lo.wait(pe, PROJ * (i + 1))
                zero_done.wait(pe, 4)
                scores(2)
                for n in range(STEPS):
                    if n + 3 < STEPS:
                        scores(n + 3)
                    transposes(n)
                    if n % 2 == 0 and n >= 2:
                        values(n // 2 - 1)
                values(GROUPS - 1)

            pairs(pe, body)


def mla_sample_stage(nc, io, scratch):
    assert (PAST + DEC_SEQ - 1) // CHUNK <= PAST // CHUNK
    with nc.cleanup_on_exit(), ExitStack() as ctx:
        def sb(name, shape, dt=F32):
            return ctx.enter_context(nc.sbuf_tensor(name, shape, dt))

        def signal(name, credit=0):
            return Signal(nc, name, credit)

        w_kvb = sb("c_wkvb", [P, CT, HEADS, NOPE + VDIM])
        wkT = sb("c_wkT", [P, HEADS, CT, P])
        cache_c = sb("c_cache_c", [P, DEC_BATCH, KV_LORA])
        cache_r = sb("c_cache_r", [P, DEC_BATCH, 2, ROPE])
        new_c = sb("c_new_c", [DEC_SEQ, DEC_BATCH, KV_LORA])
        qr_in = sb("c_qr_in", [P, HEADS, P])
        qr = sb("c_qr", [P, DEC_BATCH, HEADS, DEC_SEQ])
        qa = sb("c_qa", [P, CT, DEC_BATCH, HEADS, DEC_SEQ])
        keysT = [sb(f"c_keysT{u}", [P, CT + 1, KEYS]) for u in range(2)]
        prob = [sb(f"c_p{u}", [P, KEYS]) for u in range(2)]
        pT = [sb(f"c_pT{u}", [P, 2, P]) for u in range(2)]
        latent = sb("c_latent", [P, CT, HEADS, P])
        o_all = sb("c_o", [P, HEADS, P])
        stat = sb("c_stat", [P, DEC_BATCH, 4])
        bank = ctx.enter_context(nc.psum_tensor("c_ps", [P, 8, 512], F32))
        q_smp, ckvT, krT, ident = io["q_smp"], io["ckvT"], io["krT"], io["ident"]
        SMP = slice(SEQ, TOK)

        w_in, cache_in, qr_loaded, qr_ready = (signal(f"c_{n}") for n in ("w", "cache", "qrl", "qrr"))
        wt_done, wt_out, qa_done, qa_out = (signal(f"c_{n}") for n in ("wt", "wto", "qad", "qao"))
        kt_done, kt_past, kt_new = (signal(f"c_{n}") for n in ("kt", "ktp", "ktn"))
        s_done, nmax, nbias, exp_done = (signal(f"c_{n}") for n in ("s", "nm", "nb", "e"))
        recip, normed, t_done, t_out = (signal(f"c_{n}") for n in ("rc", "nd", "t", "to"))
        pv_done, lat_out, o_done, o_out, stored = (signal(f"c_{n}") for n in ("pv", "lo", "o", "oo", "st"))

        block = ctx.enter_context(nc.Block())

        @block.sync
        def _(sp):
            sp.dma_start(w_kvb[:].rearrange("p k h c -> p k (h c)"),
                         io["mla_w_kvb"][0].rearrange("(k p) n -> p k n", p=P)).then_inc(w_in.sem, 16)
            sp.dma_start(qr_in[:], scratch["qr"][:, :, SMP].rearrange("h p c -> p h c")).then_inc(
                qr_loaded.sem, 16)
            for dst, src in ((cache_c[:], io["cache_mla_ckv"][0].rearrange("b s c -> s b c")),
                             (cache_r[:, :, 0, :], io["cache_mla_krope"][0].rearrange("b s c -> s b c")),
                             (cache_r[:, :, 1, :], io["cache_mla_krope"][0].rearrange("b s c -> s b c")),
                             (new_c[:], io["new_s_ckv"][0].rearrange("b s c -> s b c"))):
                sp.dma_start(dst, src).then_inc(cache_in.sem, 16)
            o_out.wait(sp, 2)
            sp.dma_start(scratch["oT"][:, :, SMP].rearrange("h p c -> p h c"), o_all[:]).then_inc(
                stored.sem, 16)
            stored.wait(sp, 16)

        @block.scalar
        def _(act):
            for j in range(4):
                wt_done.wait(act, j + 1)
                act.copy(wkT[:, 2 * j:2 * j + 2, :, :], bank[:, j, :].rearrange(
                    "p (h k c) -> p h k c", h=2, k=CT)).then_inc(wt_out.sem, 1)
            for j in range(4):
                qa_done.wait(act, j + 1)
                act.copy(qa[:, j // 2, :, 4 * (j % 2):4 * (j % 2) + 4, :],
                         bank[:, 4 + j, :].rearrange("p (h b q) -> p b h q", h=4, b=DEC_BATCH)).then_inc(
                             qa_out.sem, 1)

            def past_keys(b):
                kt_done.wait(act, b + 1)
                if b >= 2:
                    s_done.wait(act, b - 1)
                act.copy(keysT[b % 2][:, :, 0:PAST], bank[:, b % 2, 0:3 * PAST].rearrange(
                    "p (k c) -> p k c", k=CT + 1)).then_inc(kt_past.sem, 1)

            past_keys(0)
            for b in range(DEC_BATCH):
                if b + 1 < DEC_BATCH:
                    past_keys(b + 1)
                nbias.wait(act, b + 1)
                if b >= 2:
                    t_done.wait(act, b - 1)
                act.activation(prob[b % 2][:], bank[:, 2 + b % 2, 0:KEYS], ACT.Exp, bias=stat[:, b, 1:2],
                               scale=MLA_SCALE, accum_out=stat[:, b, 2:3]).then_inc(exp_done.sem, 1)
                t_done.wait(act, b + 1)
                if b >= 2:
                    pv_done.wait(act, b - 1)
                act.copy(pT[b % 2][:, 0, :], bank[:, 4 + b % 2, 0:P]).then_inc(t_out.sem, 1)
                act.copy(pT[b % 2][0:DEC_SEQ, 1, :], bank[0:DEC_SEQ, 4 + b % 2, P:2 * P]).then_inc(
                    t_out.sem, 1)
                pv_done.wait(act, b + 1)
                act.copy(latent[:, :, :, b * DEC_SEQ:(b + 1) * DEC_SEQ],
                         bank[:, 6 + b % 2, 0:CT * P].rearrange("p (k h q) -> p k h q", k=CT, h=HEADS)).then_inc(
                             lat_out.sem, 1)
            for j in range(2):
                o_done.wait(act, j + 1)
                act.copy(o_all[:, 4 * j:4 * j + 4, :], bank[:, 4 + j, :].rearrange(
                    "p (h c) -> p h c", h=4)).then_inc(o_out.sem, 1)

        @block.vector
        def _(dve):
            qr_loaded.wait(dve, 16)
            dve.tensor_copy(qr[:].rearrange("p b h q -> p h b q"),
                            qr_in[:].rearrange("p h (b q) -> p h b q", b=DEC_BATCH)).then_inc(qr_ready.sem, 1)

            def new_keys(b):
                cols = slice(SEQ + b * DEC_SEQ, SEQ + (b + 1) * DEC_SEQ)
                if b >= 2:
                    s_done.wait(dve, b - 1)
                dve.tensor_tensor(keysT[b % 2][:, 0:CT, PAST:KEYS], f32(ckvT[0][:, :, cols]),
                                  f32(ckvT[1][:, :, cols]), ALU.add).then_inc(kt_new.sem, 1)
                dve.tensor_tensor(keysT[b % 2][:, CT, PAST:KEYS], f32(krT[0][:, cols]),
                                  f32(krT[1][:, cols]), ALU.add).then_inc(kt_new.sem, 1)

            new_keys(0)
            for b in range(DEC_BATCH):
                if b + 1 < DEC_BATCH:
                    new_keys(b + 1)
                s_done.wait(dve, b + 1)
                dve.tensor_reduce(stat[:, b, 0:1], bank[:, 2 + b % 2, 0:KEYS], AX.X, ALU.max,
                                  negate=True).then_inc(nmax.sem, 1)
                nmax.wait(dve, b + 1)
                dve.tensor_scalar(stat[:, b, 1:2], stat[:, b, 0:1], MLA_SCALE, None,
                                  ALU.mult).then_inc(nbias.sem, 1)
                exp_done.wait(dve, b + 1)
                dve.reciprocal(stat[:, b, 3:4], stat[:, b, 2:3]).then_inc(recip.sem, 1)
                recip.wait(dve, b + 1)
                dve.tensor_scalar(prob[b % 2][:], prob[b % 2][:], stat[:, b, 3:4], None,
                                  ALU.mult).then_inc(normed.sem, 1)

        @block.tensor
        def _(pe):
            w_in.wait(pe, 16)
            for j in range(4):
                for h in range(2):
                    for k in range(CT):
                        at = (h * CT + k) * P
                        last = pe.transpose(bank[:, j, at:at + P], w_kvb[:, k, 2 * j + h, 0:NOPE], ident[:])
                last.then_inc(wt_done.sem, 1)
            for j in range(4):
                k = j // 2
                wt_out.wait(pe, 4)
                for c in range(4):
                    h = 4 * (j % 2) + c
                    last = pe.matmul(bank[:, 4 + j, c * P:(c + 1) * P], wkT[:, h, k, :], q_smp[:, h, :],
                                     start=True, stop=True)
                last.then_inc(qa_done.sem, 1)

            def keys(b):
                if b >= 2:
                    kt_past.wait(pe, b - 1)
                for k in range(CT):
                    pe.transpose(bank[:, b % 2, k * P:(k + 1) * P], cache_c[:, b, k * P:(k + 1) * P], ident[:])
                pe.transpose(bank[:, b % 2, CT * P:(CT + 1) * P],
                             cache_r[:, b, :, :].rearrange("p i c -> p (i c)"), ident[:]).then_inc(kt_done.sem, 1)

            def scores(b):
                kt_past.wait(pe, b + 1)
                kt_new.wait(pe, 2 * (b + 1))
                if b >= 2:
                    exp_done.wait(pe, b - 1)
                stationary = [qa[:, 0, b, :, :], qa[:, 1, b, :, :], qr[:, b, :, :]]
                for k, w in enumerate(stationary):
                    last = pe.matmul(bank[:, 2 + b % 2, 0:KEYS], w.rearrange("p h q -> p (h q)"),
                                     keysT[b % 2][:, k, :], start=k == 0, stop=k == CT)
                last.then_inc(s_done.sem, 1)

            cache_in.wait(pe, 64)
            keys(0)
            qa_out.wait(pe, 4)
            qr_ready.wait(pe, 1)
            scores(0)
            for b in range(DEC_BATCH):
                if b + 1 < DEC_BATCH:
                    keys(b + 1)
                    scores(b + 1)
                normed.wait(pe, b + 1)
                if b >= 2:
                    t_out.wait(pe, 2 * (b - 1))
                pe.transpose(bank[:, 4 + b % 2, 0:P], prob[b % 2][:, 0:PAST], ident[:])
                pe.transpose(bank[0:DEC_SEQ, 4 + b % 2, P:2 * P], prob[b % 2][:, PAST:KEYS],
                             ident[:]).then_inc(t_done.sem, 1)
                t_out.wait(pe, 2 * (b + 1))
                if b >= 2:
                    lat_out.wait(pe, b - 1)
                for k in range(CT):
                    out = bank[:, 6 + b % 2, k * P:(k + 1) * P]
                    pe.matmul(out, cache_c[:, b, k * P:(k + 1) * P], pT[b % 2][:, 0, :], start=True, stop=False)
                    last = pe.matmul(out, new_c[:, b, k * P:(k + 1) * P], pT[b % 2][0:DEC_SEQ, 1, :],
                                     start=False, stop=True)
                last.then_inc(pv_done.sem, 1)
            lat_out.wait(pe, DEC_BATCH)
            t_out.wait(pe, 2 * DEC_BATCH)
            for j in range(2):
                for c in range(4):
                    h = 4 * j + c
                    for k in range(CT):
                        last = pe.matmul(bank[:, 4 + j, c * P:(c + 1) * P], w_kvb[:, k, h, NOPE:],
                                         latent[:, k, h, :], start=k == 0, stop=k == CT - 1)
                last.then_inc(o_done.sem, 1)


class NormToFeatures:

    def __init__(self, nc, ctx, name, x, gain, xn, junk, h_t, bank, ident):
        self.x, self.gain, self.xn, self.junk, self.h_t, self.bank = x, gain, xn, junk, h_t, bank
        self.ident = ident
        self.stat = ctx.enter_context(nc.sbuf_tensor(f"{name}_stat", [P, NT, 3], F32))
        self.half = ctx.enter_context(nc.sbuf_tensor(f"{name}_half", [P, 1], F32))
        self.squared, self.mean, self.rs, self.normed, self.turned, self.hi, self.lo, self.half_set = (
            Signal(nc, f"{name}_{n}") for n in ("sq", "mean", "rs", "xn", "xt", "hi", "lo", "half"))

    def act_squares(self, act, t):
        if t >= 1:
            self.squared.wait(act, t)
        act.activation(self.junk[:], self.x[:, t, :], ACT.Square,
                       accum_out=self.stat[:, t, 0:1]).then_inc(self.squared.sem, 1)

    def pool_start(self, pool):
        pool.memset(self.half[:], -0.5).then_inc(self.half_set.sem, 1)
        self.half_set.wait(pool, 1)

    def pool_inverse_rms(self, pool, t):
        self.squared.wait(pool, t + 1)
        pool.tensor_scalar(self.stat[:, t, 1:2], self.stat[:, t, 0:1], 1.0 / D_MODEL, EPS,
                           ALU.mult, ALU.add).then_inc(self.mean.sem, 1)
        self.mean.wait(pool, t + 1)
        pool.tensor_tensor(self.stat[:, t, 2:3], self.stat[:, t, 1:2], self.half[:],
                           ALU.pow).then_inc(self.rs.sem, 1)

    def dve_scale(self, dve, t):
        self.rs.wait(dve, t + 1)
        if t >= 2:
            self.turned.wait(dve, 2 * (t - 1))
        dve.scalar_tensor_tensor(out=self.xn[t % 2][:], in0=self.x[:, t, :], scalar=self.stat[:, t, 2:3],
                                 in1=self.gain[:], op0=ALU.mult, op1=ALU.mult).then_inc(self.normed.sem, 1)

    def pe_transposes(self, pe, t):
        self.normed.wait(pe, t + 1)
        for b in range(2):
            if t >= 2:
                self.lo.wait(pe, 2 * (t - 2) + b + 1)
            for c in range(4):
                k = 4 * b + c
                last = pe.transpose(self.bank[:, 2 * (t % 2) + b, c * P:(c + 1) * P],
                                    self.xn[t % 2][:, k * P:(k + 1) * P], self.ident[:])
            last.then_inc(self.turned.sem, 1)

    def _bank(self, t, b):
        return self.bank[:, 2 * (t % 2) + b, :].rearrange("p (k c) -> p k c", k=4)

    def act_hi(self, act, t):
        for b in range(2):
            self.turned.wait(act, 2 * t + b + 1)
            act.copy(self.h_t[0][:, 4 * b:4 * b + 4, t * P:(t + 1) * P], self._bank(t, b)).then_inc(
                self.hi.sem, 1)

    def dve_lo(self, dve, t):
        for b in range(2):
            self.hi.wait(dve, 2 * t + b + 1)
            hi, lo = (h[:, 4 * b:4 * b + 4, t * P:(t + 1) * P] for h in self.h_t)
            dve.tensor_tensor(lo, self._bank(t, b), f32(hi), ALU.subtract).then_inc(self.lo.sem, 1)


def output_and_mlp_stage(nc, io, scratch, layer, w_o, load_x):
    CH = 4
    CHUNKS = D_FF // (CH * P)
    GROUP = TOK // 3
    HALVES = 2
    DOWN = NT * HALVES
    O_PIECES = ((0, 1), (1, 3), (3, 6), (6, 9))
    x = io["x"]
    with nc.cleanup_on_exit(), ExitStack() as ctx:
        name = f"m{layer}"

        def sb(n, shape, dt=F32, stack=ctx):
            return stack.enter_context(nc.sbuf_tensor(f"{name}_{n}", shape, dt))

        def signal(n, credit=0):
            return Signal(nc, f"{name}_{n}", credit)

        def split(n, shape, stack=ctx):
            hi = sb(f"{n}h", shape, F32R, stack)
            with ExitStack() as before:
                raw = sb(f"{n}r", shape, F32, before)
            return raw, (hi, sb(f"{n}l", shape, F32R, stack))

        o_raw, h_t = split("h", [P, KT, TOK])
        w_o_t = [split(f"dn{u}", [P, D_MODEL]) for u in range(CH)]
        w_dn = [w for _, w in w_o_t]
        with ExitStack() as early:
            w_o_t += [split(f"wo{u}", [P, D_MODEL], early) for u in range(CH, KT)]
            gain = sb("gain", [P, D_MODEL], stack=early)
        u_t = [sb(f"u{s}", [P, CH, TOK], F32R) for s in "hl"]
        w_up = [[sb(f"up0{s}", [P, KT, P], F32R) for s in "hl"]]
        with ExitStack() as early:
            xn = [sb(f"xn{u}", [P, D_MODEL], stack=early) for u in range(2)]
        w_up.append([sb(f"up1{s}", [P, KT, P], F32R) for s in "hl"])
        up_raw = sb("up_raw", [P, KT, P])
        dn_raw = sb("dn_raw", [P, D_MODEL])
        with ExitStack() as early:
            junk = sb("junk", [P, D_MODEL], BF16, early)
        relu = [sb(f"relu{u}", [P, GROUP]) for u in range(2)]
        sq = [sb(f"sq{u}", [P, GROUP]) for u in range(2)]
        bank = ctx.enter_context(nc.psum_tensor(f"{name}_ps", [P, 8, 512], F32))
        norm = NormToFeatures(nc, ctx, f"{name}n", x, gain, xn, junk, h_t, bank, io["ident"])

        x_in, gain_in = signal("x"), signal("gain")
        w_in, o_in = [signal(f"w{k}") for k in range(KT)], [signal(f"o{g}") for g in range(len(O_PIECES))]
        w_hi, w_lo = signal("whi"), [signal("wlo_pool"), signal("wlo_dve")]
        o_hi, o_lo = signal("ohi"), signal("olo")
        up_in, up_hi, up_lo = signal("upin"), signal("uphi"), signal("uplo", 1)
        dn_in, dn_hi, dn_lo = signal("dnin"), signal("dnhi"), signal("dnlo", 1)
        up_done, dn_done = signal("up", 4), signal("dn", 1)
        relu_done, sq_done, u_hi, u_lo = signal("relu", 4), signal("sq", 2), signal("uhi"), signal("ulo", 2)
        added = signal("add", 3)

        block = ctx.enter_context(nc.Block())

        @block.sync
        def _(sp):
            def load_w_o(k):
                sp.dma_start(w_o_t[k][0][:], w_o[k * P:(k + 1) * P, :]).then_inc(w_in[k].sem, 16)

            def load_outputs(g):
                a, b = (t * P for t in O_PIECES[g])
                sp.dma_start(o_raw[:, :, a:b], scratch["oT"][:, :, a:b].rearrange(
                    "k p c -> p k c")).then_inc(o_in[g].sem, 16)

            load_w_o(0)
            load_outputs(0)
            for k in range(1, KT):
                load_w_o(k)
            load_outputs(1)
            if load_x:
                sp.dma_start(x[:, 0:NPT, :], io["x_prompt"][0].rearrange("(t p) d -> p t d", p=P)).then_inc(
                    x_in.sem, 16)
                sp.dma_start(x[:, NPT, :], io["x_sample"].rearrange("b s d -> (b s) d")).then_inc(x_in.sem, 16)
            sp.dma_start(gain[:], io["norm_mlp"][layer:layer + 1, :].broadcast_to([P, D_MODEL])).then_inc(
                gain_in.sem, 16)
            for g in range(2, len(O_PIECES)):
                load_outputs(g)
            up_rows = io["mlp_w_up"][layer].rearrange("(k p) f -> p k f", p=P)
            down_rows = io["mlp_w_down"][layer].rearrange("(f p) d -> f p d", p=P)
            with sp.Fori(0, CHUNKS) as c:
                for j in range(CH):
                    up_lo.wait(sp, CH * c + j)
                    sp.dma_start(up_raw[:], up_rows[:, :, bass.ds((CH * c + j) * P, P)]).then_inc(up_in.sem, 16)
                    dn_lo.wait(sp, CH * c + j)
                    sp.dma_start(dn_raw[:], down_rows[CH * c + j]).then_inc(dn_in.sem, 16)

        @block.scalar
        def _(act):
            relu_done.start(act)

            def output_hi(t):
                g = [a <= t < b for a, b in O_PIECES].index(True)
                cols = slice(t * P, (t + 1) * P)
                o_in[g].wait(act, 16)
                act.copy(h_t[0][:, :, cols], o_raw[:, :, cols]).then_inc(o_hi.sem, 1)

            for k in range(KT):
                w_in[k].wait(act, 16)
                act.copy(w_o_t[k][1][0][:], w_o_t[k][0][:]).then_inc(w_hi.sem, 1)
                if k == 0:
                    output_hi(0)
            for t in range(1, NT):
                output_hi(t)
            for t in range(NT + 1):
                if t < NT:
                    added.wait(act, HALVES * (t + 1))
                    norm.act_squares(act, t)
                if t >= 1:
                    norm.act_hi(act, t - 1)
            norm.turned.wait(act, 2 * NT)
            with act.Fori(0, CHUNKS) as c:
                def up_split(j):
                    up_in.wait(act, 16 * (CH * c + j + 1))
                    up_done.wait(act, 3 * (CH * c + j) - 3)
                    act.copy(w_up[j % 2][0][:], up_raw[:]).then_inc(up_hi.sem, 1)

                up_split(0)
                up_split(1)
                for j in range(CH):
                    dn_in.wait(act, 16 * (CH * c + j + 1))
                    dn_done.wait(act, DOWN + DOWN * c)
                    act.copy(w_dn[j][0][:], dn_raw[:]).then_inc(dn_hi.sem, 1)
                    for g in range(3):
                        n = 3 * j + g
                        up_done.wait(act, 12 * c + n + 1)
                        sq_done.wait(act, 12 * c + n - 1)
                        act.activation(relu[n % 2][:], bank[:, (n + 2) % 4, 0:GROUP], ACT.Relu).then_inc(
                            relu_done.sem, 1)
                        relu_done.wait(act, 12 * c + n + 1)
                        act.activation(u_t[0][:, j, g * GROUP:(g + 1) * GROUP], relu[n % 2][:],
                                       ACT.Square).then_inc(u_hi.sem, 1)
                    if j + 2 < CH:
                        up_split(j + 2)

        @block.gpsimd
        def _(pool):
            up_lo.start(pool)
            dn_lo.start(pool)
            norm.pool_start(pool)
            for k in range(0, KT, 2):
                w_hi.wait(pool, k + 1)
                raw, (hi, lo) = w_o_t[k]
                pool.tensor_tensor(lo[:], raw[:], f32(hi[:]), ALU.subtract).then_inc(w_lo[0].sem, 1)
            for t in range(NT):
                norm.pool_inverse_rms(pool, t)
            with pool.Fori(0, CHUNKS) as c:
                def up_rest(j):
                    up_hi.wait(pool, CH * c + j + 1)
                    pool.tensor_tensor(w_up[j % 2][1][:], up_raw[:], f32(w_up[j % 2][0][:]),
                                       ALU.subtract).then_inc(up_lo.sem, 1)

                up_rest(0)
                up_rest(1)
                for j in range(CH):
                    dn_hi.wait(pool, CH * c + j + 1)
                    pool.tensor_tensor(w_dn[j][1][:], dn_raw[:], f32(w_dn[j][0][:]), ALU.subtract).then_inc(
                        dn_lo.sem, 1)
                    if j + 2 < CH:
                        up_rest(j + 2)

        @block.vector
        def _(dve):
            added.start(dve)
            u_lo.start(dve)
            sq_done.start(dve)

            def add(t, half, count):
                n = HALVES * t + half
                dn_done.wait(dve, count + n + 1)
                cols = slice(half * 512, (half + 1) * 512)
                dve.tensor_tensor(x[:, t, cols], bank[:, 4 + n % 3, :], x[:, t, cols], ALU.add).then_inc(
                    added.sem, 1)

            def output_lo(t):
                o_hi.wait(dve, t + 1)
                hi, lo = (h[:, :, t * P:(t + 1) * P] for h in h_t)
                dve.tensor_tensor(lo, o_raw[:, :, t * P:(t + 1) * P], f32(hi), ALU.subtract).then_inc(o_lo.sem, 1)

            output_lo(0)
            for k in range(1, KT, 2):
                w_hi.wait(dve, k + 1)
                raw, (hi, lo) = w_o_t[k]
                dve.tensor_tensor(lo[:], raw[:], f32(hi[:]), ALU.subtract).then_inc(w_lo[1].sem, 1)
            output_lo(1)
            output_lo(2)
            if load_x:
                x_in.wait(dve, 32)
            gain_in.wait(dve, 16)
            for t in range(NT + 2):
                if t < NT:
                    for half in range(HALVES):
                        add(t, half, 0)
                if t + 3 < NT:
                    output_lo(t + 3)
                if 1 <= t <= NT:
                    norm.dve_scale(dve, t - 1)
                if t >= 2:
                    norm.dve_lo(dve, t - 2)
            with dve.Fori(0, CHUNKS) as c:
                for n in range(12):
                    j, g = n // 3, n % 3
                    cols = slice(g * GROUP, (g + 1) * GROUP)
                    relu_done.wait(dve, 12 * c + n + 1)
                    u_lo.wait(dve, 12 * c + n - 1)
                    dve.tensor_tensor(sq[n % 2][:], relu[n % 2][:], relu[n % 2][:], ALU.mult).then_inc(
                        sq_done.sem, 1)
                    u_hi.wait(dve, 12 * c + n + 1)
                    sq_done.wait(dve, 12 * c + n + 1)
                    dve.tensor_tensor(u_t[1][:, j, cols], sq[n % 2][:], f32(u_t[0][:, j, cols]),
                                      ALU.subtract).then_inc(u_lo.sem, 1)
                for t in range(NT):
                    for half in range(HALVES):
                        add(t, half, DOWN + DOWN * c)

        @block.tensor
        def _(pe):
            up_done.start(pe)
            dn_done.start(pe)

            def down(t, half, w, weights, count, ready=None):
                n = HALVES * t + half
                added.wait(pe, count + n - 2)
                for j, d in enumerate(weights):
                    if ready:
                        ready(j)
                    last = product(pe, bank[:, 4 + n % 3, :], [u[:, j, t * P:(t + 1) * P] for u in w],
                                   [m[:, half * 512:(half + 1) * 512] for m in d], j == 0,
                                   j == len(weights) - 1)
                last.then_inc(dn_done.sem, 1)

            for t in range(NT):
                o_lo.wait(pe, t + 1)
                for half in range(HALVES):
                    down(t, half, h_t, [w for _, w in w_o_t], 0,
                         (lambda k: w_lo[k % 2].wait(pe, k // 2 + 1)) if t == half == 0 else None)
                if t >= 2:
                    norm.pe_transposes(pe, t - 2)
            norm.pe_transposes(pe, NT - 2)
            norm.pe_transposes(pe, NT - 1)
            with pe.Fori(0, CHUNKS) as c:
                for n in range(12):
                    j, g = n // 3, n % 3
                    relu_done.wait(pe, 12 * c + n - 3)
                    up_lo.wait(pe, CH * c + j + 1)
                    if j == 0:
                        norm.lo.wait(pe, 2 * (NT if g == 2 else NT - 1))
                    for k in range(KT):
                        last = product(pe, bank[:, (n + 2) % 4, 0:GROUP], [w[:, k, :] for w in w_up[j % 2]],
                                       [h[:, k, g * GROUP:(g + 1) * GROUP] for h in h_t], k == 0, k == KT - 1)
                    last.then_inc(up_done.sem, 1)
                dn_lo.wait(pe, CH * (c + 1))
                for t in range(NT):
                    u_lo.wait(pe, 12 * c + 9 + t // 3 + 1)
                    for half in range(HALVES):
                        down(t, half, u_t, w_dn, DOWN + DOWN * c)


def sb_input_stage(nc, io, scratch):
    WIDTH = 512
    GROUPS_W = 3 * D_MODEL // WIDTH
    PIECES = 4
    x = io["x"]
    with nc.cleanup_on_exit(), ExitStack() as ctx:
        def sb(name, shape, dt=F32):
            return ctx.enter_context(nc.sbuf_tensor(name, shape, dt))

        def signal(name, credit=0):
            return Signal(nc, name, credit)

        h_t = [sb(f"d_h{s}", [P, KT, TOK], F32R) for s in "hl"]
        gain = sb("d_gain", [P, D_MODEL])
        xn = [sb(f"d_xn{u}", [P, D_MODEL]) for u in range(2)]
        junk = sb("d_junk", [P, D_MODEL], BF16)
        w_raw = [sb(f"d_wraw{u}", [P, 2, WIDTH]) for u in range(2)]
        w = [[sb(f"d_w{u}{s}", [P, 2, WIDTH], F32R) for s in "hl"] for u in range(2 * PIECES)]
        stage = [sb(f"d_out{u}", [P, WIDTH]) for u in range(3)]
        bank = ctx.enter_context(nc.psum_tensor("d_ps", [P, 8, 512], F32))
        norm = NormToFeatures(nc, ctx, "dn", x, gain, xn, junk, h_t, bank, io["ident"])

        gain_in, w_in = signal("d_gain_in"), [signal(f"d_w_in{u}") for u in range(2)]
        w_hi, w_lo = signal("d_w_hi"), signal("d_w_lo")
        done, copied, stored = signal("d_done"), signal("d_copied"), [signal(f"d_st{u}") for u in range(3)]
        TASKS = GROUPS_W * NT

        block = ctx.enter_context(nc.Block())

        @block.sync
        def _(sp):
            sp.dma_start(gain[:], io["norm_mix"][1:2, :].broadcast_to([P, D_MODEL])).then_inc(gain_in.sem, 16)

            def load(n):
                g, j = n // PIECES, n % PIECES
                if n >= 2:
                    w_lo.wait(sp, n - 1)
                sp.dma_start(w_raw[n % 2][:], io["sb_w_in"][0].rearrange("(k p) n -> p k n", p=P)[
                    :, 2 * j:2 * j + 2, g * WIDTH:(g + 1) * WIDTH]).then_inc(w_in[n % 2].sem, 16)

            def destination(g, t):
                kind, cols = g // 2, slice((g % 2) * WIDTH, (g % 2 + 1) * WIDTH)
                if kind == 0:
                    rows = scratch["q"]
                else:
                    rows = io[f"new_{'s' if t == NPT else 'p'}_sb_{'k' if kind == 1 else 'v'}"][0].rearrange(
                        "b s h c -> (b s) (h c)")
                    t = 0 if t == NPT else t
                return rows[t * P:(t + 1) * P, cols]

            for n in range(PIECES + 2):
                load(n)
            for n in range(TASKS):
                copied.wait(sp, n + 1)
                sp.dma_start(destination(n // NT, n % NT), stage[n % 3][:]).then_inc(stored[n % 3].sem, 16)
                piece = (n // NT + 1) * PIECES + n % NT + 2
                if n % NT < PIECES and piece < GROUPS_W * PIECES:
                    load(piece)
            for u in range(3):
                stored[u].wait(sp, 16 * TASKS // 3)

        @block.scalar
        def _(act):
            def weights_hi(n):
                w_in[n % 2].wait(act, 16 * (n // 2 + 1))
                g = n // PIECES
                if g >= 2:
                    done.wait(act, NT * (g - 1))
                act.copy(w[n % (2 * PIECES)][0][:], w_raw[n % 2][:]).then_inc(w_hi.sem, 1)

            for t in range(2):
                norm.act_squares(act, t)
                weights_hi(2 * t)
                weights_hi(2 * t + 1)
            for t in range(2):
                norm.act_squares(act, t + 2)
                norm.act_hi(act, t)
            for n in range(TASKS):
                g, t = n // NT, n % NT
                if t < PIECES and g + 1 < GROUPS_W:
                    weights_hi((g + 1) * PIECES + t)
                if n + 4 < NT:
                    norm.act_squares(act, n + 4)
                if n + 2 < NT:
                    norm.act_hi(act, n + 2)
                done.wait(act, n + 1)
                if n >= 3:
                    stored[n % 3].wait(act, 16 * (n // 3))
                act.copy(stage[n % 3][:], bank[:, 4 + n % 4, :]).then_inc(copied.sem, 1)

        @block.gpsimd
        def _(pool):
            norm.pool_start(pool)

            def weights_lo(n):
                w_hi.wait(pool, n + 1)
                hi, lo = w[n % (2 * PIECES)]
                pool.tensor_tensor(lo[:], w_raw[n % 2][:], f32(hi[:]), ALU.subtract).then_inc(w_lo.sem, 1)

            for t in range(2):
                norm.pool_inverse_rms(pool, t)
                weights_lo(2 * t)
                weights_lo(2 * t + 1)
            for t in range(2, 4):
                norm.pool_inverse_rms(pool, t)
            for n in range(PIECES, GROUPS_W * PIECES):
                if n == NT - 1:
                    norm.pool_inverse_rms(pool, n)
                weights_lo(n)
                if n < NT - 1:
                    norm.pool_inverse_rms(pool, n)

        @block.vector
        def _(dve):
            gain_in.wait(dve, 16)
            for t in range(NT + 1):
                if t < NT:
                    norm.dve_scale(dve, t)
                if t >= 1:
                    norm.dve_lo(dve, t - 1)

        @block.tensor
        def _(pe):
            norm.pe_transposes(pe, 0)
            norm.pe_transposes(pe, 1)
            for n in range(TASKS):
                g, t = n // NT, n % NT
                if n >= 4:
                    copied.wait(pe, n - 3)
                if g == 0:
                    norm.lo.wait(pe, 2 * (t + 1))
                w_lo.wait(pe, PIECES * (g + 1))
                for k in range(KT):
                    piece = w[(g % 2) * PIECES + k // 2]
                    last = product(pe, bank[:, 4 + n % 4, :], [h[:, k, t * P:(t + 1) * P] for h in h_t],
                                   [m[:, k % 2, :] for m in piece], k == 0, k == KT - 1)
                last.then_inc(done.sem, 1)
                if g == 0 and t + 2 < NT:
                    norm.pe_transposes(pe, t + 2)


class SbSchedule:
    PAIRS = SB_HEADS // 2
    PAIR_STEPS = 2 * NPT
    STEPS = 2 * PAIR_STEPS
    PREPARE_TASKS = [(kind, a, 4 * half, 4) for kind in range(2) for a in range(2) for half in range(2)]
    PREPARE_TASKS[-1:] = [(1, 1, 4, 2), (1, 1, 6, 2)]
    PREPARE = len(PREPARE_TASKS)
    PREPARE_AT = (0, 1, 2, 4, 5, 6, 8, 9, 10)
    VALUES_AT = 4
    UNITS, GROUPS = STEPS // 2, STEPS // 4
    AHEAD = 3
    ORDER = (0, 1, 2, 3)
    VALUES_LAG = 1
    OUTPUT_LAG = 2

    @staticmethod
    def where(n):
        m = n % SbSchedule.PAIR_STEPS
        return n // SbSchedule.PAIR_STEPS % 2, m // 2 % 2, 2 * SbSchedule.ORDER[m // 4] + m % 2

    @classmethod
    def tasks(cls, n, last):
        pair, _, q = cls.where(n)
        out = [("weights", t) for t in transpose_tasks(q)]
        m = n % cls.PAIR_STEPS
        if m in cls.PREPARE_AT and not (last and pair == 1):
            out.append(("prepare", cls.PREPARE_AT.index(m)))
        return out

    @classmethod
    def before(cls, n, last=False):
        return sum(len(cls.tasks(m, last)) for m in range(n))


def sb_attention_stage(nc, io, scratch):
    S = SbSchedule
    BODIES = S.PAIRS // 2
    TASKS = S.before(S.STEPS)
    with nc.cleanup_on_exit(), ExitStack() as ctx:
        def sb(name, shape, dt=F32):
            return ctx.enter_context(nc.sbuf_tensor(name, shape, dt))

        def signal(name, credit=0):
            return Signal(nc, name, credit)

        raw = [sb(f"e_raw_{x}", [P, NPT, 2, 2, SB_DIM]) for x in "qk"]
        v_raw = sb("e_raw_v", [P, NPT, 2, SB_DIM])
        q_st = [sb(f"e_q{u}", [P, 2, SEQ], F32R) for u in range(2)]
        k_tt = [[sb(f"e_k{u}{s}", [P, 2, SEQ], F32R) for s in "hl"] for u in range(2)]
        v = [[sb(f"e_v{u}{s}", [P, NPT, 3 * SB_DIM], F32R) for s in "hl"] for u in range(2)]
        keep = [sb(f"e_u{u}", [P, SEQ]) for u in range(2)]
        take = [sb(f"e_b{u}", [P, SEQ]) for u in range(4)]
        rest = [sb(f"e_r{u}", [P, SEQ + 1]) for u in range(2)]
        pt = [[sb(f"e_pt{u}{s}", [P, NPT, GQ], F32R) for s in "hl"] for u in range(2)]
        o_st = [sb(f"e_o{u}", [P, GQ]) for u in range(2)]
        zero = sb("e_zero", [P, 1])
        bank = ctx.enter_context(nc.psum_tensor("e_ps", [P, 8, 512], F32))
        score = [bank[:, 2 * u:2 * u + 2, :].rearrange("p b c -> p (b c)") for u in range(2)]

        raw_in = [signal(f"e_{x}_in") for x in "qk"]
        v_in, v_hi, v_lo = (signal(f"e_v_{x}") for x in ("in", "hi", "lo"))
        s_done = signal("e_s")
        kept, taken = signal("e_kept", 2), signal("e_taken", 2)
        scanned, weighted = signal("e_scan", 2), signal("e_weighted", 2)
        t_done, t_hi, t_lo = signal("e_t"), signal("e_t_hi"), signal("e_t_lo", 3)
        pv_done, o_done = signal("e_pv", 2), signal("e_o", 1)
        const_done = signal("e_const")
        o_out = [signal(f"e_o_out{u}", 16) for u in range(2)]

        def task_bank(m):
            return bank[:, 4 + m % 3, :]

        def operand(pair, index):
            kind, a, tile, tiles = S.PREPARE_TASKS[index]
            cols = slice(tile * P, (tile + tiles) * P)
            if kind == 0:
                q = q_st[pair][:, a, cols]
                return q, q[SB_DIM:P, :], slice(SB_DIM, P)
            hi, lo = (k[:, a, cols] for k in k_tt[pair])
            return hi, lo, slice(0, P)

        def bodies(engine, body):
            with engine.Fori(0, BODIES - 1) as i:
                body(i, False)
            body(BODIES - 1, True)

        block = ctx.enter_context(nc.Block())

        @block.sync
        def _(sp):
            def load_queries_keys(p):
                for x, rows in enumerate((scratch["q"][0:SEQ, :], io["new_p_sb_k"][0, 0].rearrange(
                        "s h c -> s (h c)"))):
                    src = rows.rearrange("(t p) (h c) -> p t h c", p=P, h=SB_HEADS)
                    for a in range(2):
                        for twice in range(2):
                            sp.dma_start(raw[x][:, :, a, twice, :], src[:, :, 2 * p + a, :]).then_inc(
                                raw_in[x].sem, 16)

            def load_values(p):
                sp.dma_start(v_raw[:].rearrange("p t a c -> p t (a c)"),
                             io["new_p_sb_v"][0, 0].rearrange("(t p) h c -> p t (h c)", p=P)[
                    :, :, bass.ds(p * 2 * SB_DIM, 2 * SB_DIM)]).then_inc(v_in.sem, 16)

            def store(i, g):
                o_done.wait(sp, S.GROUPS * i + g + 1)
                cols = slice(S.ORDER[g % 4] * GQ, (S.ORDER[g % 4] + 1) * GQ)
                sp.dma_start(scratch["oT"][2 * i + g // 4, :, cols], o_st[g % 2][:]).then_inc(
                    o_out[g % 2].sem, 16)

            def body(i, last):
                for pair in range(2):
                    for g in range(4):
                        store(i, 4 * pair + g)
                        if g == 1 and not (last and pair == 0) and not (last and pair == 1):
                            v_lo.wait(sp, 2 * i + pair + 2)
                            load_values(2 * i + pair + 2)
                        if g == 2 and not last:
                            t_done.wait(sp, S.PREPARE + TASKS * i + S.before(
                                pair * S.PAIR_STEPS + S.PREPARE_AT[-1] + 1))
                            load_queries_keys(2 * i + pair + 2)

            for x in o_out:
                x.start(sp)
            load_queries_keys(0)
            load_values(0)
            t_done.wait(sp, S.PREPARE)
            load_queries_keys(1)
            v_lo.wait(sp, 1)
            load_values(1)
            bodies(sp, body)
            for x in o_out:
                x.wait(sp, 16 * BODIES * S.GROUPS // 2)

        @block.scalar
        def _(act):
            kept.start(act)
            taken.start(act)
            o_done.start(act)

            def weights(i, n, last=False):
                first, _, used = score_columns(S.where(n)[2])
                z = score[n % 2][:, first:first + used]
                s_done.wait(act, S.STEPS * i + n + 1)
                scanned.wait(act, S.STEPS * i + n - 1)
                act.activation(keep[n % 2][:, 0:used], z, ACT.Sigmoid, scale=-SB_SCALE).then_inc(kept.sem, 1)
                if n >= 4:
                    t_done.wait(act, S.PREPARE + TASKS * i + S.before(n - 3, last))
                act.activation(take[n % 4][:, 0:used], z, ACT.Sigmoid, scale=SB_SCALE).then_inc(taken.sem, 1)

            def prepare_hi(pair, index, m):
                hi = operand(pair, index)[0]
                act.copy(hi, task_bank(m)[:, 0:hi.shape[1]]).then_inc(t_hi.sem, 1)

            def values_hi(p, pair):
                v_in.wait(act, 16 * (p + 1))
                pv_done.wait(act, S.UNITS // 2 * (p - 1))
                act.copy(v[pair][0][:].rearrange("p t (b c) -> p t b c", b=3)[:, :, ::2, :],
                         v_raw[:]).then_inc(v_hi.sem, 1)

            def transposed_hi(i, n, last):
                unit, at = n // 2, (n % 2) * P
                for j, (kind, task) in enumerate(S.tasks(n, last)):
                    m = S.before(n, last) + j
                    t_done.wait(act, S.PREPARE + TASKS * i + m + 1)
                    if kind == "prepare":
                        prepare_hi(1 - S.where(n)[0], task, m)
                        continue
                    pv_done.wait(act, S.UNITS * i + unit - 1)
                    s0 = task[0][1]
                    act.copy(pt[unit % 2][0][:, s0:s0 + len(task), at:at + P],
                             task_bank(m)[:, 0:len(task) * P].rearrange("p (s c) -> p s c", c=P)).then_inc(
                                 t_hi.sem, 1)

            def output(i, g):
                pv_done.wait(act, S.UNITS * i + 2 * g + 2)
                o_out[g % 2].wait(act, 16 * (S.GROUPS // 2 * i + g // 2))
                act.copy(o_st[g % 2][:], bank[:, 7, 0:GQ]).then_inc(o_done.sem, 1)

            def step(i, n, last):
                if not (last and n + S.AHEAD >= S.STEPS):
                    weights(i, n + S.AHEAD, last)
                pair, m = S.where(n)[0], n % S.PAIR_STEPS
                if m == S.VALUES_AT and not (last and pair == 1):
                    values_hi(2 * i + pair + 1, 1 - pair)

            def body(i, last):
                for n in range(S.STEPS):
                    m = n + S.OUTPUT_LAG
                    if not (last and m >= S.STEPS):
                        step(i, m, last)
                    if n % 4 == 3:
                        output(i, n // 4)
                    if not (last and m >= S.STEPS):
                        transposed_hi(i, m, last)

            for m in range(S.PREPARE):
                t_done.wait(act, m + 1)
                prepare_hi(0, m, m)
            v_in.wait(act, 16)
            const_done.wait(act, 4)
            act.copy(v[0][0][:].rearrange("p t (b c) -> p t b c", b=3)[:, :, ::2, :],
                     v_raw[:]).then_inc(v_hi.sem, 1)
            for n in range(S.AHEAD):
                weights(0, n)
            for n in range(S.OUTPUT_LAG):
                step(0, n, False)
                transposed_hi(0, n, False)
            bodies(act, body)

        @block.gpsimd
        def _(pool):
            weighted.start(pool)

            def weigh(i, n):
                used = (S.where(n)[2] + 1) * P
                scanned.wait(pool, S.STEPS * i + n + 1)
                taken.wait(pool, S.STEPS * i + n + 1)
                b = take[n % 4][:, 0:used]
                pool.tensor_tensor(b, b, rest[n % 2][:, SEQ - used + 1:SEQ + 1], ALU.mult).then_inc(
                    weighted.sem, 1)

            def body(i, last):
                for n in range(S.STEPS):
                    if not (last and n + S.AHEAD >= S.STEPS):
                        weigh(i, n + S.AHEAD)

            for n in range(S.AHEAD):
                weigh(0, n)
            bodies(pool, body)

        @block.vector
        def _(dve):
            scanned.start(dve)
            t_lo.start(dve)
            for x in (*v[0], *v[1]):
                dve.memset(f32(x[:, :, SB_DIM:2 * SB_DIM]), 0.0).then_inc(const_done.sem, 1)
            for x in (*pt[0], *pt[1]):
                dve.memset(f32(x[:, 0, 0:P]), 0.0).then_inc(const_done.sem, 1)
            for x in rest:
                dve.memset(x[:, SEQ:SEQ + 1], 1.0).then_inc(const_done.sem, 1)
            dve.memset(zero[:], 0.0).then_inc(const_done.sem, 1)
            const_done.wait(dve, 11)

            def scan(i, n):
                used = (S.where(n)[2] + 1) * P
                kept.wait(dve, S.STEPS * i + n + 1)
                weighted.wait(dve, S.STEPS * i + n - 1)
                dve.tensor_tensor_scan(rest[n % 2][:, SEQ - used:SEQ][:, ::-1], keep[n % 2][:, 0:used][:, ::-1],
                                       zero[:].broadcast_to([P, used]), 1.0, ALU.mult, ALU.add).then_inc(
                                           scanned.sem, 1)

            def prepare_lo(pair, index, m):
                hi, lo, rows = operand(pair, index)
                dve.tensor_tensor(lo, task_bank(m)[rows, 0:hi.shape[1]], f32(hi[rows, :]), ALU.subtract).then_inc(
                    t_lo.sem, 1)

            def values_lo(p, pair):
                v_hi.wait(dve, p + 1)
                hi, lo = (x[:].rearrange("p t (b c) -> p t b c", b=3)[:, :, ::2, :] for x in v[pair])
                dve.tensor_tensor(lo, v_raw[:], f32(hi), ALU.subtract).then_inc(v_lo.sem, 1)

            def transposed_lo(i, n, last):
                unit, at = n // 2, (n % 2) * P
                for j, (kind, task) in enumerate(S.tasks(n, last)):
                    m = S.before(n, last) + j
                    t_hi.wait(dve, S.PREPARE + TASKS * i + m + 1)
                    if kind == "prepare":
                        prepare_lo(1 - S.where(n)[0], task, m)
                        continue
                    s0 = task[0][1]
                    hi, lo = (x[:, s0:s0 + len(task), at:at + P] for x in pt[unit % 2])
                    dve.tensor_tensor(lo, task_bank(m)[:, 0:len(task) * P].rearrange(
                        "p (s c) -> p s c", c=P), f32(hi), ALU.subtract).then_inc(t_lo.sem, 1)

            def body(i, last):
                for n in range(S.STEPS):
                    if not (last and n + S.AHEAD >= S.STEPS):
                        scan(i, n + S.AHEAD)
                    pair, m = S.where(n)[0], n % S.PAIR_STEPS
                    if m == S.VALUES_AT and not (last and pair == 1):
                        values_lo(2 * i + pair + 1, 1 - pair)
                    transposed_lo(i, n, last)

            for m in range(S.PREPARE):
                t_hi.wait(dve, m + 1)
                prepare_lo(0, m, m)
            values_lo(0, 0)
            for n in range(S.AHEAD):
                scan(0, n)
            bodies(dve, body)

        @block.tensor
        def _(pe):
            pv_done.start(pe)
            ident = io["ident"]

            def scores(i, n):
                pair, a, q = S.where(n)
                if n % S.PAIR_STEPS == 0:
                    last_task = S.before((n - S.PAIR_STEPS) + S.PREPARE_AT[-1] + 1) if n else 0
                    t_lo.wait(pe, S.PREPARE + TASKS * i + last_task)
                taken.wait(pe, S.STEPS * i + n - 1)
                first, chunks, used = score_columns(q)
                for at, width, key in chunks:
                    for k in k_tt[pair]:
                        pe.matmul(score[n % 2][:, at:at + width], q_st[pair][:, a, q * P:(q + 1) * P],
                                  k[:, a, key:key + width], start=k is k_tt[pair][0],
                                  stop=k is k_tt[pair][1] and key + width < used)
                end = first + used
                pe.matmul(score[n % 2][:, end - P:end], io["ident16"][:], io["causal_mask"][:, 0:P],
                          start=False, stop=True).then_inc(s_done.sem, 1)

            def prepare(p, index, m):
                kind, a, tile, tiles = S.PREPARE_TASKS[index]
                raw_in[kind].wait(pe, 64 * (p + 1))
                for c in range(tiles):
                    last = pe.transpose(task_bank(m)[:, c * P:(c + 1) * P],
                                        raw[kind][:, tile + c, a, :, :].rearrange("p i c -> p (i c)"),
                                        ident[:])
                last.then_inc(t_done.sem, 1)

            def transposes(i, n, last):
                weighted.wait(pe, S.STEPS * i + n + 1)
                for j, (kind, task) in enumerate(S.tasks(n, last)):
                    m = S.before(n, last) + j
                    t_lo.wait(pe, S.PREPARE + TASKS * i + m - 2)
                    if kind == "prepare":
                        prepare(2 * i + n // S.PAIR_STEPS + 1, task, m)
                        continue
                    for c, (k, _) in enumerate(task):
                        t = pe.transpose(task_bank(m)[:, c * P:(c + 1) * P],
                                         take[n % 4][:, k * P:(k + 1) * P], ident[:])
                    t.then_inc(t_done.sem, 1)

            def values(i, unit, last):
                g, a, pair = unit // 2, unit % 2, unit // (S.UNITS // 2)
                last_q = 2 * S.ORDER[g % 4] + 1
                t_lo.wait(pe, S.PREPARE + TASKS * i + S.before(2 * unit + 2, last))
                if unit % (S.UNITS // 2) == 0:
                    v_lo.wait(pe, 2 * i + pair + 1)
                if a == 0:
                    o_done.wait(pe, S.GROUPS * i + g)
                order = [(last_q, 0)] + [(k, k + 1) for k in range(last_q)]
                for k, slot in order:
                    done = product(pe, bank[:, 7, 0:GQ],
                                   [x[:, k, a * SB_DIM:a * SB_DIM + P] for x in v[pair]],
                                   [x[:, slot, :] for x in pt[unit % 2]], a == 0 and k == last_q,
                                   a == 1 and k == last_q - 1)
                done.then_inc(pv_done.sem, 1)

            def step(i, n, last):
                if not (last and n + S.AHEAD + 1 >= S.STEPS):
                    scores(i, n + S.AHEAD + 1)
                if not (last and n >= S.STEPS):
                    transposes(i, n, last)

            def body(i, last):
                for n in range(S.STEPS):
                    step(i, n + S.VALUES_LAG, last)
                    if n % 2 == 1:
                        values(i, n // 2, last)

            const_done.wait(pe, 11)
            for m in range(S.PREPARE):
                if m >= 3:
                    t_lo.wait(pe, m - 2)
                prepare(0, m, m)
            for n in range(S.AHEAD + 1):
                scores(0, n)
            for n in range(S.VALUES_LAG):
                step(0, n, False)
            bodies(pe, body)


def sb_sample_stage(nc, io, scratch):
    PAIRS = SB_HEADS // 2
    HALF = PAIRS // 2
    STEPS = 2 * DEC_BATCH
    ROWS = 2 * DEC_SEQ
    with nc.cleanup_on_exit(), ExitStack() as ctx:
        def sb(name, shape, dt=F32):
            return ctx.enter_context(nc.sbuf_tensor(name, shape, dt))

        def signal(name, credit=0):
            return Signal(nc, name, credit)

        q_tok = sb("f_q_tok", [P, PAIRS, P])
        k_tok = sb("f_k_tok", [P, PAIRS, P])
        cache_k = sb("f_ck", [P, DEC_BATCH, PAIRS, P])
        cache_v = sb("f_cv", [P, DEC_BATCH, PAIRS, P])
        new_v = sb("f_nv", [DEC_SEQ, DEC_BATCH, PAIRS, P])
        q_z = sb("f_qz", [P, DEC_BATCH, PAIRS, P])
        new_kT = sb("f_nkT", [P, PAIRS, P])
        keysT = [sb(f"f_kT{u}", [P, PAIRS, KEYS]) for u in range(2)]
        keep = [sb(f"f_u{u}", [P, KEYS]) for u in range(2)]
        take = [sb(f"f_b{u}", [P, KEYS]) for u in range(2)]
        rest = [sb(f"f_r{u}", [P, KEYS + 1]) for u in range(2)]
        wT = [sb(f"f_wT{u}", [P, 2, P]) for u in range(2)]
        o_all = sb("f_o", [P, PAIRS, P])
        zero = sb("f_zero", [P, 1])
        bank = ctx.enter_context(nc.psum_tensor("f_ps", [P, 8, 512], F32))
        SMP = slice(SEQ, TOK)

        tok_in, new_v_in = signal("f_tok"), signal("f_nv_in")
        cache_in = [signal(f"f_c{b}") for b in range(DEC_BATCH)]
        zeroed, const_done = signal("f_zeroed"), signal("f_const")
        qt_done, q_out, nk_out = signal("f_qt"), signal("f_qo"), signal("f_nko")
        kt_done, kt_past, kt_new = signal("f_kt"), signal("f_ktp"), signal("f_ktn")
        s_done, kept, taken = signal("f_s"), signal("f_kept"), signal("f_taken")
        scanned, weighted = signal("f_scan"), signal("f_weighted")
        t_done, t_out, pv_done, o_out, stored = (signal(f"f_{n}") for n in ("t", "to", "pv", "oo", "st"))

        block = ctx.enter_context(nc.Block())

        @block.sync
        def _(sp):
            sp.dma_start(q_tok[:].rearrange("p a c -> p (a c)"), scratch["q"][SMP, :]).then_inc(tok_in.sem, 16)
            sp.dma_start(k_tok[:].rearrange("p a c -> p (a c)"),
                         io["new_s_sb_k"][0].rearrange("b s h c -> (b s) (h c)")).then_inc(tok_in.sem, 16)
            for b in range(DEC_BATCH):
                for dst, src in ((cache_k, "cache_sb_k"), (cache_v, "cache_sb_v")):
                    sp.dma_start(dst[:, b, :, :].rearrange("p a c -> p (a c)"),
                                 io[src][0, b].rearrange("s h c -> s (h c)")).then_inc(cache_in[b].sem, 16)
                if b == 0:
                    sp.dma_start(new_v[:].rearrange("p b a c -> p b (a c)"),
                                 io["new_s_sb_v"][0].rearrange("b s h c -> s b (h c)")).then_inc(
                                     new_v_in.sem, 16)
            o_out.wait(sp, 2 * STEPS)
            sp.dma_start(scratch["oT"][:, :, SMP].rearrange("h p c -> p h c"), o_all[:]).then_inc(
                stored.sem, 16)
            stored.wait(sp, 16)

        @block.gpsimd
        def _(pool):
            pool.memset(q_z[:, 0:DEC_BATCH // 2], 0.0).then_inc(zeroed.sem, 1)

        @block.scalar
        def _(act):
            zeroed.wait(act, 2)
            for j in range(2):
                qt_done.wait(act, j + 1)
                for c in range(HALF):
                    for a in range(2):
                        rows, at = slice(a * SB_DIM, (a + 1) * SB_DIM), (2 * c + a) * DEC_SEQ
                        act.copy(q_z[rows, :, j * HALF + c, at:at + DEC_SEQ],
                                 bank[rows, j, c * P:(c + 1) * P].rearrange("p (b q) -> p b q", b=DEC_BATCH)
                                 ).then_inc(q_out.sem, 1)

            def past_keys(b):
                for j in range(2):
                    kt_done.wait(act, 2 * b + j + 1)
                    if b >= 2:
                        s_done.wait(act, 2 * (b - 1))
                    act.copy(keysT[b % 2][:, j * HALF:(j + 1) * HALF, 0:PAST], bank[:, j, :].rearrange(
                        "p (a c) -> p a c", a=HALF)).then_inc(kt_past.sem, 1)

            def sigmoids(n):
                z = bank[:, 2 + n % 2, 0:KEYS]
                s_done.wait(act, n + 1)
                if n >= 2:
                    scanned.wait(act, n - 1)
                    t_done.wait(act, n - 1)
                act.activation(keep[n % 2][:], z, ACT.Sigmoid, scale=-SB_SCALE).then_inc(kept.sem, 1)
                act.activation(take[n % 2][:], z, ACT.Sigmoid, scale=SB_SCALE).then_inc(taken.sem, 1)

            past_keys(0)
            sigmoids(0)
            for n in range(STEPS):
                b = n // 2
                if n % 2 == 0 and b + 1 < DEC_BATCH:
                    past_keys(b + 1)
                if n + 1 < STEPS:
                    sigmoids(n + 1)
                t_done.wait(act, n + 1)
                if n >= 2:
                    pv_done.wait(act, n - 1)
                act.copy(wT[n % 2][:, 0, :], bank[:, 4 + n % 2, 0:P]).then_inc(t_out.sem, 1)
                act.copy(wT[n % 2][0:DEC_SEQ, 1, :], bank[0:DEC_SEQ, 4 + n % 2, P:2 * P]).then_inc(t_out.sem, 1)

        @block.vector
        def _(dve):
            dve.memset(q_z[:, DEC_BATCH // 2:], 0.0).then_inc(zeroed.sem, 1)
            for x in rest:
                dve.memset(x[:, KEYS:KEYS + 1], 1.0).then_inc(const_done.sem, 1)
            dve.memset(zero[:], 0.0).then_inc(const_done.sem, 1)
            const_done.wait(dve, 3)
            for j in range(2):
                qt_done.wait(dve, 3 + j)
                dve.tensor_copy(new_kT[:, j * HALF:(j + 1) * HALF, :], bank[:, 2 + j, :].rearrange(
                    "p (a c) -> p a c", a=HALF)).then_inc(nk_out.sem, 1)
            nk_out.wait(dve, 2)

            def new_keys(b):
                if b >= 2:
                    s_done.wait(dve, 2 * (b - 1))
                dve.tensor_copy(keysT[b % 2][:, :, PAST:KEYS],
                                new_kT[:, :, b * DEC_SEQ:(b + 1) * DEC_SEQ]).then_inc(kt_new.sem, 1)

            def output(n):
                b, half = n // 2, n % 2
                pv_done.wait(dve, n + 1)
                for a in range(2):
                    rows = slice(a * SB_DIM, (a + 1) * SB_DIM)
                    dve.tensor_copy(
                        o_all[rows, half * HALF:(half + 1) * HALF, b * DEC_SEQ:(b + 1) * DEC_SEQ],
                        bank[rows, 6 + n % 2, 0:HALF * ROWS].rearrange("p (c i q) -> p c i q", c=HALF, i=2)[
                            :, :, a, :]).then_inc(o_out.sem, 1)

            new_keys(0)
            for n in range(STEPS):
                b = n // 2
                if n % 2 == 0 and b + 1 < DEC_BATCH:
                    new_keys(b + 1)
                kept.wait(dve, n + 1)
                if n >= 2:
                    weighted.wait(dve, n - 1)
                dve.tensor_tensor_scan(rest[n % 2][:, 0:KEYS][:, ::-1], keep[n % 2][:][:, ::-1],
                                       zero[:].broadcast_to([P, KEYS]), 1.0, ALU.mult, ALU.add).then_inc(
                                           scanned.sem, 1)
                scanned.wait(dve, n + 1)
                taken.wait(dve, n + 1)
                dve.tensor_tensor(take[n % 2][:], take[n % 2][:], rest[n % 2][:, 1:KEYS + 1],
                                  ALU.mult).then_inc(weighted.sem, 1)
                if n >= 1:
                    output(n - 1)
            output(STEPS - 1)

        @block.tensor
        def _(pe):
            ident = io["ident"]
            tok_in.wait(pe, 32)
            for x, src in enumerate((q_tok, k_tok)):
                for j in range(2):
                    for c in range(HALF):
                        last = pe.transpose(bank[:, 2 * x + j, c * P:(c + 1) * P], src[:, j * HALF + c, :],
                                            ident[:])
                    last.then_inc(qt_done.sem, 1)

            def keys(b):
                cache_in[b].wait(pe, 32)
                for j in range(2):
                    if b == 0:
                        q_out.wait(pe, 2 * HALF * (j + 1))
                    else:
                        kt_past.wait(pe, 2 * b - 1 + j)
                    for c in range(HALF):
                        last = pe.transpose(bank[:, j, c * P:(c + 1) * P], cache_k[:, b, j * HALF + c, :],
                                            ident[:])
                    last.then_inc(kt_done.sem, 1)

            def scores(n):
                b, half = n // 2, n % 2
                kt_past.wait(pe, 2 * b + half + 1)
                kt_new.wait(pe, b + 1)
                if n >= 2:
                    taken.wait(pe, n - 1)
                z = bank[:, 2 + n % 2, 0:KEYS]
                for c in range(HALF):
                    pair = half * HALF + c
                    pe.matmul(z, q_z[:, b, pair, :], keysT[b % 2][:, pair, :], start=c == 0, stop=False)
                pe.matmul(z[:, PAST:KEYS], io["ident16"][:], io["causal_mask"][:, P:P + DEC_SEQ],
                          start=False, stop=True).then_inc(s_done.sem, 1)

            def transposes(n):
                weighted.wait(pe, n + 1)
                if n >= 2:
                    t_out.wait(pe, 2 * (n - 1))
                pe.transpose(bank[:, 4 + n % 2, 0:P], take[n % 2][:, 0:PAST], ident[:])
                pe.transpose(bank[0:DEC_SEQ, 4 + n % 2, P:2 * P], take[n % 2][:, PAST:KEYS],
                             ident[:]).then_inc(t_done.sem, 1)

            def values(n):
                b, half = n // 2, n % 2
                t_out.wait(pe, 2 * (n + 1))
                if n >= 2:
                    o_out.wait(pe, 2 * (n - 1))
                for c in range(HALF):
                    pair, cols = half * HALF + c, slice(c * ROWS, (c + 1) * ROWS)
                    out = bank[:, 6 + n % 2, cols]
                    pe.matmul(out, cache_v[:, b, pair, :], wT[n % 2][:, 0, cols], start=True, stop=False)
                    last = pe.matmul(out, new_v[:, b, pair, :], wT[n % 2][0:DEC_SEQ, 1, cols],
                                     start=False, stop=True)
                last.then_inc(pv_done.sem, 1)

            keys(0)
            nk_out.wait(pe, 2)
            scores(0)
            for n in range(STEPS):
                if n % 2 == 0 and n // 2 + 1 < DEC_BATCH:
                    keys(n // 2 + 1)
                if n + 1 < STEPS:
                    scores(n + 1)
                transposes(n)
                if n == 0:
                    new_v_in.wait(pe, 16)
                if n >= 1:
                    values(n - 1)
            values(STEPS - 1)


def final_norm_stage(nc, io):
    x = io["x"]
    with nc.cleanup_on_exit(), ExitStack() as ctx:
        def sb(name, shape, dt=F32):
            return ctx.enter_context(nc.sbuf_tensor(name, shape, dt))

        gain = sb("g_gain", [P, D_MODEL])
        junk = sb("g_junk", [P, D_MODEL], BF16)
        y = sb("g_y", [P, NT, D_MODEL])
        stat = sb("g_stat", [P, NT, 3])
        half = sb("g_half", [P, 1])
        gain_in, squared, mean, rs, half_set, y_done, stored = (
            Signal(nc, f"g_{n}") for n in ("gain_in", "sq", "mean", "rs", "half_set", "yd", "st"))
        block = ctx.enter_context(nc.Block())

        @block.sync
        def _(sp):
            sp.dma_start(gain[:], io["norm_final"].rearrange("(o d) -> o d", o=1).broadcast_to(
                [P, D_MODEL])).then_inc(gain_in.sem, 16)
            for t in range(NT):
                y_done.wait(sp, t + 1)
                rows = io["y_prompt"][0, t * P:(t + 1) * P, :] if t < NPT else \
                    io["y_sample"].rearrange("b s d -> (b s) d")
                sp.dma_start(rows, y[:, t, :]).then_inc(stored.sem, 16)
            stored.wait(sp, 16 * NT)

        @block.scalar
        def _(act):
            for t in range(NT):
                if t >= 1:
                    squared.wait(act, t)
                act.activation(junk[:], x[:, t, :], ACT.Square, accum_out=stat[:, t, 0:1]).then_inc(
                    squared.sem, 1)

        @block.gpsimd
        def _(pool):
            pool.memset(half[:], -0.5).then_inc(half_set.sem, 1)
            half_set.wait(pool, 1)
            for t in range(NT):
                squared.wait(pool, t + 1)
                pool.tensor_scalar(stat[:, t, 1:2], stat[:, t, 0:1], 1.0 / D_MODEL, EPS,
                                   ALU.mult, ALU.add).then_inc(mean.sem, 1)
                mean.wait(pool, t + 1)
                pool.tensor_tensor(stat[:, t, 2:3], stat[:, t, 1:2], half[:], ALU.pow).then_inc(rs.sem, 1)

        @block.vector
        def _(dve):
            gain_in.wait(dve, 16)
            for t in range(NT):
                rs.wait(dve, t + 1)
                dve.scalar_tensor_tensor(out=y[:, t, :], in0=x[:, t, :], scalar=stat[:, t, 2:3],
                                         in1=gain[:], op0=ALU.mult, op1=ALU.mult).then_inc(y_done.sem, 1)


def build(nc, io):
    with ExitStack() as ctx:
        def sb(name, shape, dt=F32):
            return ctx.enter_context(nc.sbuf_tensor(name, shape, dt))

        io["ident"] = sb("ident", [P, P])
        io["ident16"] = sb("ident16", [P, P], BF16)
        io["chunk_mask"] = sb("chunk_mask", [P, P], BF16)
        io["causal_mask"] = sb("causal_mask", [P, P + DEC_SEQ], BF16)
        scratch = {
            "qr": nc.dram_tensor("scratch_qr", (HEADS, P, TOK), F32, kind="Internal").ap(),
            "oT": nc.dram_tensor("scratch_oT", (KT, P, TOK), F32, kind="Internal").ap(),
        }
        scratch["q"] = nc.dram_tensor("scratch_q", (TOK, D_MODEL), F32, kind="Internal").ap()
        with ExitStack() as mla:
            io["cqT"] = [mla.enter_context(nc.sbuf_tensor(f"cqT{s}", [P, QT, TOK], F32R)) for s in "hl"]
            io["ckvT"] = [mla.enter_context(nc.sbuf_tensor(f"ckvT{s}", [P, CT, TOK], F32R)) for s in "hl"]
            io["krT"] = [mla.enter_context(nc.sbuf_tensor(f"krT{s}", [P, TOK], F32R)) for s in "hl"]
            mla_input_stage(nc, io, scratch)
            io["q_smp"] = mla.enter_context(nc.sbuf_tensor("q_smp", [P, HEADS, P], F32))
            mla_attention_stage(nc, io, scratch)
            mla_sample_stage(nc, io, scratch)
        io["x"] = sb("x", [P, NT, D_MODEL])
        output_and_mlp_stage(nc, io, scratch, 0, io["mla_w_o"][0], True)
        sb_input_stage(nc, io, scratch)
        sb_attention_stage(nc, io, scratch)
        sb_sample_stage(nc, io, scratch)
        output_and_mlp_stage(nc, io, scratch, 1, io["sb_w_o"][0], False)
        final_norm_stage(nc, io)


_INS = ["x_prompt", "x_sample", "cache_mla_ckv", "cache_mla_krope", "cache_sb_k", "cache_sb_v",
        "norm_mix", "norm_mlp", "norm_final", "mla_w_in", "mla_g_q", "mla_w_qb", "mla_g_kv",
        "mla_w_kvb", "mla_w_o", "sb_w_in", "sb_w_o", "mlp_w_up", "mlp_w_down"]
_OUTS = [("y_prompt", (1, SEQ, D_MODEL)), ("y_sample", (DEC_BATCH, DEC_SEQ, D_MODEL)),
         ("new_p_ckv", (1, 1, SEQ, KV_LORA)), ("new_p_krope", (1, 1, SEQ, ROPE)),
         ("new_p_sb_k", (1, 1, SEQ, SB_HEADS, SB_DIM)), ("new_p_sb_v", (1, 1, SEQ, SB_HEADS, SB_DIM)),
         ("new_s_ckv", (1, DEC_BATCH, DEC_SEQ, KV_LORA)), ("new_s_krope", (1, DEC_BATCH, DEC_SEQ, ROPE)),
         ("new_s_sb_k", (1, DEC_BATCH, DEC_SEQ, SB_HEADS, SB_DIM)),
         ("new_s_sb_v", (1, DEC_BATCH, DEC_SEQ, SB_HEADS, SB_DIM))]


def shape_constants():
    half = ROPE // 2
    inv = (THETA ** (-np.arange(0, ROPE, 2) / ROPE)).astype(np.float32)
    pos = np.arange(TOK, dtype=np.float32)
    pos[SEQ:] = PAST + np.arange(P) % DEC_SEQ
    ang = (pos[:, None] * inv[None, :]).astype(np.float32).astype(np.float64)
    cos, sin = np.cos(ang).astype(np.float32), np.sin(ang).astype(np.float32)

    def by_tile(a, b):
        both = np.concatenate([a, b], axis=1).reshape(NT, P, 2 * half)
        return np.ascontiguousarray(both.transpose(1, 0, 2))

    q, k = np.arange(P)[:, None], np.arange(P)[None, :]
    bf = mybir.dt.np(BF16)
    new = np.where(np.arange(DEC_SEQ)[None, :] < q % DEC_SEQ, 0.0, MASKED)
    return {
        "cos_dram": by_tile(cos, cos), "sin_dram": by_tile(-sin, sin),
        "ident_dram": np.eye(P, dtype=np.float32), "ident16_dram": np.eye(P).astype(bf),
        "chunk_mask_dram": np.where(k // CHUNK <= q // CHUNK, 0.0, MASKED).astype(bf),
        "causal_mask_dram": np.concatenate([np.where(k < q, 0.0, MASKED), new], axis=1).astype(bf),
    }


def kernel(**inputs):
    import concourse.bacc as _bacc
    from concourse.bass_utils import run_bass_kernel_spmd as _run

    nc = _bacc.Bacc("TRN2", target_bir_lowering=False, num_devices=1)
    arrays, io = {}, {}
    for name in _INS:
        arrays[f"in_{name}"] = np.ascontiguousarray(inputs[name])
    arrays.update({f"in_{name}": a for name, a in shape_constants().items()})
    for name, a in arrays.items():
        io[name[3:]] = nc.dram_tensor(name, a.shape, mybir.dt.from_np(a.dtype), kind="ExternalInput").ap()
    for name, shape in _OUTS:
        io[name] = nc.dram_tensor(name, shape, F32, kind="ExternalOutput").ap()
    build(nc, io)
    r = _run(nc, [arrays], core_ids=[0])
    return tuple(r.results[0][name] for name, _ in _OUTS)
```

```python
from contextlib import ExitStack

import numpy as np

import concourse.bass as bass
from concourse import mybir

F32 = mybir.dt.float32
F32R = mybir.dt.float32r
BF16 = mybir.dt.bfloat16
ACT = mybir.ActivationFunctionType
ALU = mybir.AluOpType
AX = mybir.AxisListType

P = 128
D_MODEL = 1024
KT = D_MODEL // P
SEQ = 1024
DEC_BATCH, DEC_SEQ, PAST = 8, 16, 128
NPT = SEQ // P
NT = NPT + 1
TOK = NT * P
HEADS, NOPE, ROPE, VDIM = 8, 128, 64, 128
Q_LORA, KV_LORA = 512, 256
QT, CT = Q_LORA // P, KV_LORA // P
MLA_IN = Q_LORA + KV_LORA + ROPE
SB_HEADS, SB_DIM = 16, 64
D_FF = 4 * D_MODEL
EPS = 1e-6
THETA = 10000.0
CHUNK = 64
MLA_SCALE = float((NOPE + ROPE) ** -0.5)
SB_SCALE = float(SB_DIM ** -0.5)
MASKED = -1e30
KEYS = PAST + DEC_SEQ
GQ = 2 * P


def semaphores(nc, names):
    return {n: nc.alloc_semaphore(n) for n in names.split()}


def f32(ap):
    return ap.bitcast(F32)


def product(pe, out, w, m, start, stop):
    pe.matmul(out, w[0], m[0], start=start, stop=False)
    pe.matmul(out, w[0], m[1], start=False, stop=False)
    return pe.matmul(out, w[1], m[0], start=False, stop=stop)


def swap_halves(ap, heads):
    return ap.rearrange("p (h i c) -> p h i c", h=heads, i=2)[:, :, ::-1, :]


class Signal:

    def __init__(self, nc, name, credit=0):
        self.sem, self.credit = nc.alloc_semaphore(name), credit

    def start(self, engine):
        engine.sem_inc(self.sem, self.credit)

    def wait(self, engine, count):
        engine.wait_ge(self.sem, count + self.credit)


def mla_input_stage(nc, io, scratch, raw):
    with nc.cleanup_on_exit(), ExitStack() as ctx:
        def sb(name, shape, dt=F32):
            return ctx.enter_context(nc.sbuf_tensor(name, shape, dt))

        x_in = [sb(f"a_x{u}", [P, D_MODEL]) for u in range(2)]
        square_junk = sb("a_junk", [P, D_MODEL])
        xn = sb("a_xn", [P, D_MODEL])
        gain_x = sb("a_gain_x", [P, D_MODEL])
        gain_q = sb("a_gain_q", [P, Q_LORA])
        gain_kv = sb("a_gain_kv", [P, KV_LORA])
        cos_t = sb("a_cos", [P, NT, ROPE])
        sin_t = sb("a_sin", [P, NT, ROPE])
        h_t = [[sb(f"a_h{u}{s}", [P, KT, P], F32R) for s in "hl"] for u in range(2)]
        w_in = sb("a_winh", [P, KT, MLA_IN], F32R)
        w_qr = sb("a_wqrh", [P, QT, HEADS * ROPE], F32R)
        with ExitStack() as before:
            w_in_raw = before.enter_context(nc.sbuf_tensor("a_winr", [P, KT, MLA_IN], F32))
            w_qr_raw = before.enter_context(nc.sbuf_tensor("a_wqrr", [P, QT, HEADS * ROPE], F32))
        w_in = [w_in, sb("a_winl", [P, KT, MLA_IN], F32R)]
        w_qr = [w_qr, sb("a_wqrl", [P, QT, HEADS * ROPE], F32R)]
        cq = sb("a_cq", [P, Q_LORA])
        ckv = [sb(f"a_ckv{u}", [P, KV_LORA]) for u in range(2)]
        kr = [sb(f"a_kr{u}", [P, 2 * ROPE]) for u in range(2)]
        kr_cos = sb("a_krc", [P, ROPE])
        kr_sin = sb("a_krs", [P, ROPE])
        qr = sb("a_qr", [P, HEADS * 2 * ROPE])
        qr_cos = sb("a_qrc", [P, HEADS * ROPE])
        qr_sin = sb("a_qrs", [P, HEADS * ROPE])
        qr_stack = [sb(f"a_qrst{u}", [P, HEADS, P], F32R) for u in range(2)]
        sums = sb("a_sums", [P, NT, 3])
        means = sb("a_means", [P, NT, 3])
        rs = sb("a_rs", [P, NT, 3])
        half = sb("a_half", [P, 1])
        bank = ctx.enter_context(nc.psum_tensor("a_ps", [P, 8, 512], F32))
        xt, a1, a2, cqt, ckt, qrp, qrt = (bank[:, 0:2, :], bank[:, 2, :], bank[:, 3, :], bank[:, 4, :],
                                          bank[:, 5, :], bank[:, 6, :], bank[:, 7, :])

        s = semaphores(nc, """a_const a_gain a_ident a_x0 a_x1 a_w_hi a_w_lo_pool a_w_lo_dve a_half a_sq a_mean a_rs a_xn a_xt
            a_h_hi a_h_lo a_a1 a_a2 a_cq_sq a_cq_mean a_cq_rs a_kv_sq a_kv_mean a_kv_rs a_cq a_ckv
            a_kr_mul a_kr a_cqt a_ckt a_cq_hi a_cq_lo a_ck_hi a_ck_lo a_qr a_qr_mul a_qrot a_qrt
            a_qrt_hi a_qrt_lo a_next_w a_st0 a_st1 a_stq0 a_stq1""")
        cqT, ckvT, krT = io["cqT"], io["ckvT"], io["krT"]
        ident = io["ident"]
        NW = KT + QT
        w_arrived = [nc.alloc_semaphore(f"a_w{n}") for n in range(NW)]
        pieces = [(w_in_raw[:, k, :], *(w[:, k, :] for w in w_in)) for k in range(KT)] + \
                 [(w_qr_raw[:, k, :], *(w[:, k, :] for w in w_qr)) for k in range(QT)]
        w_lo = [s["a_w_lo_pool"], s["a_w_lo_dve"]]
        x_rows = [io["x_prompt"][0, t * P:(t + 1) * P, :] for t in range(NPT)]
        x_rows.append(io["x_sample"].rearrange("b s d -> (b s) d"))
        N_CONST = 7

        block = ctx.enter_context(nc.Block())

        @block.sync
        def _(sp):
            def load_x(t):
                if t >= 2:
                    sp.wait_ge(s["a_xn"], t - 1)
                sp.dma_start(x_in[t % 2][:], x_rows[t]).then_inc(s[f"a_x{t % 2}"], 16)

            def load_w(n):
                if n < KT:
                    dst, src = pieces[n][0], io["mla_w_in"][0, n * P:(n + 1) * P, :]
                else:
                    k = n - KT
                    src = io["mla_w_qb"][0, k * P:(k + 1) * P, :].rearrange(
                        "p (h c) -> p h c", h=HEADS)[:, :, NOPE:]
                    dst = pieces[n][0].rearrange("p (h c) -> p h c", h=HEADS)
                sp.dma_start(dst, src).then_inc(w_arrived[n], 16)

            load_x(0)
            sp.dma_start(gain_x[:], io["norm_mix"][0:1, :].broadcast_to([P, D_MODEL])).then_inc(s["a_gain"], 16)
            sp.dma_start(ident[:], io["ident_dram"]).then_inc(s["a_ident"], 16)
            for n in range(3):
                load_w(n)
            load_x(1)
            for n in range(3, KT):
                load_w(n)
            for dst, src in (
                    (gain_q[:], io["mla_g_q"][0:1, :].broadcast_to([P, Q_LORA])),
                    (gain_kv[:], io["mla_g_kv"][0:1, :].broadcast_to([P, KV_LORA])),
                    (cos_t[:], io["cos_dram"]), (sin_t[:], io["sin_dram"]),
                    (io["ident16"][:], io["ident16_dram"]), (io["chunk_mask"][:], io["chunk_mask_dram"]),
                    (io["causal_mask"][:], io["causal_mask_dram"])):
                sp.dma_start(dst, src).then_inc(s["a_const"], 16)
            for n in range(KT, NW):
                load_w(n)

            def store(t):
                sp.wait_ge(s["a_ckv"], t + 1)
                c_out = io["new_p_ckv"][0, 0, t * P:(t + 1) * P, :] if t < NPT else \
                    io["new_s_ckv"][0].rearrange("b s d -> (b s) d")
                sp.dma_start(c_out, ckv[t % 2][:]).then_inc(s[f"a_st{t % 2}"], 16)
                sp.wait_ge(s["a_kr"], t + 1)
                k_out = io["new_p_krope"][0, 0, t * P:(t + 1) * P, :] if t < NPT else \
                    io["new_s_krope"][0].rearrange("b s d -> (b s) d")
                sp.dma_start(k_out, kr[t % 2][:, 0:ROPE]).then_inc(s[f"a_st{t % 2}"], 16)

            def store_q(t):
                sp.wait_ge(s["a_qrt_lo"], 2 * (t + 1))
                sp.dma_start(scratch["qr"][:, :, t * P:(t + 1) * P].rearrange("h p c -> p h c"),
                             f32(qr_stack[t % 2][:])).then_inc(s[f"a_stq{t % 2}"], 16)

            for t in range(NT + 2):
                if t + 2 < NT:
                    load_x(t + 2)
                if t == NT // 2:
                    load_raw_weights(sp, io, raw, 0, s["a_next_w"], s["a_next_w"])
                if t < NT:
                    store(t)
                if t >= 2:
                    store_q(t - 2)
            for u in range(2):
                uses = (NT + 1 - u) // 2
                sp.wait_ge(s[f"a_st{u}"], 32 * uses)
                sp.wait_ge(s[f"a_stq{u}"], 16 * uses)
            sp.wait_ge(s["a_next_w"], 48)

        @block.scalar
        def _(act):
            def squares(t):
                act.wait_ge(s[f"a_x{t % 2}"], 16 * (t // 2 + 1))
                if t >= 1:
                    act.wait_ge(s["a_sq"], t)
                act.activation(square_junk[:], x_in[t % 2][:], ACT.Square,
                               accum_out=sums[:, t, 0:1]).then_inc(s["a_sq"], 1)

            def h_hi(t):
                for b in range(2):
                    act.wait_ge(s["a_xt"], 2 * t + b + 1)
                    if t >= 2:
                        act.wait_ge(s["a_a2"], t - 1)
                    act.copy(h_t[t % 2][0][:, 4 * b:4 * b + 4, :], xt[:, b, :].rearrange(
                        "p (k c) -> p k c", k=4)).then_inc(s["a_h_hi"], 1)

            def latents_hi(t):
                act.wait_ge(s["a_cqt"], t + 1)
                act.copy(cqT[0][:, :, t * P:(t + 1) * P],
                         cqt.rearrange("p (k c) -> p k c", k=QT)).then_inc(s["a_cq_hi"], 1)
                act.wait_ge(s["a_ckt"], t + 1)
                act.copy(ckvT[0][:, :, t * P:(t + 1) * P],
                         ckt[:, 0:CT * P].rearrange("p (k c) -> p k c", k=CT)).then_inc(s["a_ck_hi"], 1)
                act.copy(krT[0][:, t * P:(t + 1) * P], ckt[:, CT * P:CT * P + P]).then_inc(s["a_ck_hi"], 1)

            def q_rope_hi(t, b):
                act.wait_ge(s["a_qrt"], 2 * t + b + 1)
                if t >= 2:
                    act.wait_ge(s[f"a_stq{t % 2}"], 16 * (t // 2))
                act.copy(qr_stack[t % 2][:, 4 * b:4 * b + 4, :], qrt.rearrange(
                    "p (k c) -> p k c", k=4)).then_inc(s["a_qrt_hi"], 1)

            def weights_hi(n):
                act.wait_ge(w_arrived[n], 16)
                raw, hi, _ = pieces[n]
                act.copy(hi, raw).then_inc(s["a_w_hi"], 1)

            squares(0)
            for n in range(2):
                weights_hi(n)
            h_hi(0)
            for n in range(2, 4):
                weights_hi(n)
            squares(1)
            for n in range(4, NW):
                weights_hi(n)
            for t in range(NT + 2):
                if t + 1 < NT:
                    h_hi(t + 1)
                if t + 2 < NT:
                    squares(t + 2)
                if t < NT:
                    act.wait_ge(s["a_a1"], t + 1)
                    act.wait_ge(s["a_sq"], min(t + 3, NT))
                    if t >= 1:
                        act.wait_ge(s["a_kv_sq"], t)
                    act.activation(square_junk[:, 0:Q_LORA], a1, ACT.Square,
                                   accum_out=sums[:, t, 1:2]).then_inc(s["a_cq_sq"], 1)
                if t >= 2:
                    q_rope_hi(t - 2, 0)
                if 1 <= t <= NT:
                    latents_hi(t - 1)
                if t < NT:
                    act.wait_ge(s["a_a2"], t + 1)
                    act.wait_ge(s["a_cq_sq"], t + 1)
                    act.activation(square_junk[:, 0:KV_LORA], a2[:, 0:KV_LORA], ACT.Square,
                                   accum_out=sums[:, t, 2:3]).then_inc(s["a_kv_sq"], 1)
                if t >= 2:
                    q_rope_hi(t - 2, 1)

        @block.gpsimd
        def _(pool):
            pool.memset(half[:], -0.5).then_inc(s["a_half"], 1)
            pool.wait_ge(s["a_half"], 1)

            def inverse_rms(t, kind, n, squared, mean, done):
                pool.wait_ge(s[squared], t + 1)
                pool.tensor_scalar(means[:, t, kind:kind + 1], sums[:, t, kind:kind + 1], 1.0 / n, EPS,
                                   ALU.mult, ALU.add).then_inc(s[mean], 1)
                pool.wait_ge(s[mean], t + 1)
                pool.tensor_tensor(rs[:, t, kind:kind + 1], means[:, t, kind:kind + 1], half[:],
                                   ALU.pow).then_inc(s[done], 1)

            def weights_rest(n):
                pool.wait_ge(s["a_w_hi"], n + 1)
                raw, hi, lo = pieces[n]
                pool.tensor_tensor(lo, raw, f32(hi), ALU.subtract).then_inc(w_lo[0], 1)

            inverse_rms(0, 0, D_MODEL, "a_sq", "a_mean", "a_rs")
            weights_rest(0)
            weights_rest(2)
            inverse_rms(1, 0, D_MODEL, "a_sq", "a_mean", "a_rs")
            for n in range(4, NW, 2):
                weights_rest(n)
            for t in range(NT):
                if t + 2 < NT:
                    inverse_rms(t + 2, 0, D_MODEL, "a_sq", "a_mean", "a_rs")
                inverse_rms(t, 1, Q_LORA, "a_cq_sq", "a_cq_mean", "a_cq_rs")
                inverse_rms(t, 2, KV_LORA, "a_kv_sq", "a_kv_mean", "a_kv_rs")

        @block.vector
        def _(dve):
            def normalise_x(t):
                dve.wait_ge(s["a_rs"], t + 1)
                if t >= 1:
                    dve.wait_ge(s["a_xt"], 2 * t)
                dve.scalar_tensor_tensor(out=xn[:], in0=x_in[t % 2][:], scalar=rs[:, t, 0:1],
                                         in1=gain_x[:], op0=ALU.mult, op1=ALU.mult).then_inc(s["a_xn"], 1)

            def h_lo(t):
                for b in range(2):
                    dve.wait_ge(s["a_h_hi"], 2 * t + b + 1)
                    dst = [h_t[t % 2][i][:, 4 * b:4 * b + 4, :] for i in range(2)]
                    dve.tensor_tensor(dst[1], xt[:, b, :].rearrange("p (k c) -> p k c", k=4),
                                      f32(dst[0]), ALU.subtract).then_inc(s["a_h_lo"], 1)

            def latents_lo(t):
                cols = slice(t * P, (t + 1) * P)
                dve.wait_ge(s["a_cq_hi"], t + 1)
                dve.tensor_tensor(cqT[1][:, :, cols], cqt.rearrange("p (k c) -> p k c", k=QT),
                                  f32(cqT[0][:, :, cols]), ALU.subtract).then_inc(s["a_cq_lo"], 1)
                dve.wait_ge(s["a_ck_hi"], 2 * (t + 1))
                dve.tensor_tensor(ckvT[1][:, :, cols], ckt[:, 0:CT * P].rearrange("p (k c) -> p k c", k=CT),
                                  f32(ckvT[0][:, :, cols]), ALU.subtract).then_inc(s["a_ck_lo"], 1)
                dve.tensor_tensor(krT[1][:, cols], ckt[:, CT * P:CT * P + P],
                                  f32(krT[0][:, cols]), ALU.subtract).then_inc(s["a_ck_lo"], 1)

            def rotate(out, parts, src, heads, t, mul_sem, done_sem, waits):
                for sem, v in waits:
                    dve.wait_ge(s[sem], v)
                table = [x[:, t:t + 1, :].rearrange("p o (i c) -> p o i c", i=2).broadcast_to(
                    [P, heads, 2, ROPE // 2]) for x in (cos_t[:], sin_t[:])]
                view = [x.rearrange("p (h i c) -> p h i c", h=heads, i=2) for x in (*parts, src)]
                dve.tensor_tensor(view[0], view[2], table[0], ALU.mult).then_inc(s[mul_sem], 1)
                dve.tensor_tensor(view[1], swap_halves(src, heads), table[1],
                                  ALU.mult).then_inc(s[mul_sem], 1)
                dve.wait_ge(s[mul_sem], 2 * (t + 1))
                twice = [x.rearrange("p (h o c) -> p h o c", h=heads, o=1).broadcast_to(
                    [P, heads, 2, ROPE]) for x in parts]
                dve.tensor_tensor(out.rearrange("p (h i c) -> p h i c", h=heads, i=2), *twice,
                                  ALU.add).then_inc(s[done_sem], 1)

            def q_rope_lo(t, b):
                dve.wait_ge(s["a_qrt_hi"], 2 * t + b + 1)
                low = qr_stack[t % 2][ROPE:P, 4 * b:4 * b + 4, :]
                dve.tensor_tensor(low, qrt[ROPE:P, :].rearrange("p (k c) -> p k c", k=4),
                                  f32(low), ALU.subtract).then_inc(s["a_qrt_lo"], 1)

            def weights_rest(n):
                dve.wait_ge(s["a_w_hi"], n + 1)
                raw, hi, lo = pieces[n]
                dve.tensor_tensor(lo, raw, f32(hi), ALU.subtract).then_inc(w_lo[1], 1)

            dve.wait_ge(s["a_gain"], 16)
            normalise_x(0)
            weights_rest(1)
            h_lo(0)
            weights_rest(3)
            normalise_x(1)
            for n in range(5, NW, 2):
                weights_rest(n)
            dve.wait_ge(s["a_const"], 16 * N_CONST)
            for t in range(NT + 2):
                if t + 1 < NT:
                    h_lo(t + 1)
                if t + 2 < NT:
                    normalise_x(t + 2)
                if t < NT:
                    dve.wait_ge(s["a_cq_rs"], t + 1)
                    if t >= 1:
                        dve.wait_ge(s["a_cqt"], t)
                    dve.scalar_tensor_tensor(out=cq[:], in0=a1, scalar=rs[:, t, 1:2], in1=gain_q[:],
                                             op0=ALU.mult, op1=ALU.mult).then_inc(s["a_cq"], 1)
                if t >= 2:
                    q_rope_lo(t - 2, 0)
                if 1 <= t <= NT:
                    latents_lo(t - 1)
                if t < NT:
                    dve.wait_ge(s["a_kv_rs"], t + 1)
                    if t >= 2:
                        dve.wait_ge(s[f"a_st{t % 2}"], 32 * (t // 2))
                        dve.wait_ge(s["a_ckt"], t - 1)
                    dve.scalar_tensor_tensor(out=ckv[t % 2][:], in0=a2[:, 0:KV_LORA],
                                             scalar=rs[:, t, 2:3], in1=gain_kv[:],
                                             op0=ALU.mult, op1=ALU.mult).then_inc(s["a_ckv"], 1)
                    waits = [("a_kr", t)] if t >= 1 else []
                    rotate(kr[t % 2][:], (kr_cos[:], kr_sin[:]), a2[:, KV_LORA:KV_LORA + ROPE], 1, t,
                           "a_kr_mul", "a_kr", waits)
                if t >= 2:
                    q_rope_lo(t - 2, 1)
                if 1 <= t <= NT:
                    waits = [("a_qr", t)]
                    if t >= 2:
                        waits += [("a_qrot", t - 1), ("a_qrt", 2 * (t - 1))]
                    rotate(qr[:], (qr_cos[:], qr_sin[:]), qrp, HEADS, t - 1, "a_qr_mul", "a_qrot", waits)

        @block.tensor
        def _(pe):
            def transpose_x(t):
                pe.wait_ge(s["a_xn"], t + 1)
                for b in range(2):
                    if t >= 1:
                        pe.wait_ge(s["a_h_lo"], 2 * (t - 1) + b + 1)
                    for k in range(4):
                        last = pe.transpose(xt[:, b, k * P:(k + 1) * P],
                                            xn[:, (4 * b + k) * P:(4 * b + k + 1) * P], ident[:])
                    last.then_inc(s["a_xt"], 1)

            def transpose_latents(t):
                pe.wait_ge(s["a_cq"], t + 1)
                if t >= 1:
                    pe.wait_ge(s["a_ck_lo"], 2 * t)
                for k in range(QT):
                    last = pe.transpose(cqt[:, k * P:(k + 1) * P], cq[:, k * P:(k + 1) * P], ident[:])
                last.then_inc(s["a_cqt"], 1)
                pe.wait_ge(s["a_ckv"], t + 1)
                pe.wait_ge(s["a_kr"], t + 1)
                for k in range(CT):
                    pe.transpose(ckt[:, k * P:(k + 1) * P], ckv[t % 2][:, k * P:(k + 1) * P], ident[:])
                pe.transpose(ckt[:, CT * P:CT * P + P], kr[t % 2][:], ident[:]).then_inc(s["a_ckt"], 1)

            def rotary_queries(t):
                pe.wait_ge(s["a_cq_lo"], t + 1)
                if t >= 1:
                    pe.wait_ge(s["a_qrot"], t)
                for k in range(QT):
                    last = product(pe, qrp, [c[:, k, t * P:(t + 1) * P] for c in cqT],
                                   [w[:, k, :] for w in w_qr], k == 0, k == QT - 1)
                last.then_inc(s["a_qr"], 1)

            def transpose_rotary(t, b):
                pe.wait_ge(s["a_qrot"], t + 1)
                if 2 * t + b >= 1:
                    pe.wait_ge(s["a_qrt_lo"], 2 * t + b)
                for k in range(4):
                    h = 4 * b + k
                    last = pe.transpose(qrt[:, k * P:(k + 1) * P], qr[:, h * P:(h + 1) * P], ident[:])
                last.then_inc(s["a_qrt"], 1)

            def project(t, out, c0, c1, done, emptied):
                for sem, v in emptied:
                    pe.wait_ge(s[sem], v)
                pe.wait_ge(s["a_h_lo"], 2 * (t + 1))
                for k in range(KT):
                    if t == 0:
                        pe.wait_ge(w_lo[k % 2], k // 2 + 1)
                    last = product(pe, out[:, 0:c1 - c0], [h[:, k, :] for h in h_t[t % 2]],
                                   [w[:, k, c0:c1] for w in w_in], k == 0, k == KT - 1)
                last.then_inc(s[done], 1)

            pe.wait_ge(s["a_ident"], 16)
            transpose_x(0)
            for t in range(NT + 2):
                if t + 1 < NT:
                    transpose_x(t + 1)
                if t < NT:
                    project(t, a1, 0, Q_LORA, "a_a1", [("a_cq", t)] if t else [])
                if t >= 2:
                    transpose_rotary(t - 2, 0)
                if 1 <= t <= NT:
                    transpose_latents(t - 1)
                if t < NT:
                    project(t, a2, Q_LORA, MLA_IN, "a_a2", [("a_kr", t)] if t else [])
                if t >= 2:
                    transpose_rotary(t - 2, 1)
                if t == 1:
                    for w in w_lo:
                        pe.wait_ge(w, NW // 2)
                if 1 <= t <= NT:
                    rotary_queries(t - 1)


def score_columns(q):
    used = (q + 1) * P
    keys = max(used, 2 * P)
    first = P if keys == 640 else 0
    chunks, at = [], first
    while at < first + keys:
        end = min(512 * (at // 512 + 1), first + keys)
        chunks.append((at, end - at, at - first))
        at = end
    return first, chunks, used


def transpose_tasks(n):
    q = n % NPT
    order = [(q, 0)] + [(k, k + 1) for k in range(q)] if q % 2 else [(k, k + 1) for k in range(q + 1)]
    return [order[i:i + 4] for i in range(0, len(order), 4)]


def tasks_before(n):
    return sum(len(transpose_tasks(m)) for m in range(n))


STEPS = 2 * NPT
T_TASKS = tasks_before(STEPS)
GROUPS = STEPS // 2


def raw_weights(nc, ctx):
    return [ctx.enter_context(nc.sbuf_tensor(f"raw_{n}", shape, F32)) for n, shape in (
        ("wq", [P, QT, 2, NOPE]), ("wkv", [P, CT, 2, NOPE + VDIM]))]


def load_raw_weights(sp, io, raw, i, wq_in, wkv_in):
    for a in range(2):
        sp.dma_start(raw[0][:, :, a, :], io["mla_w_qb"][0].rearrange(
            "(k p) (h c) -> p k h c", p=P, h=HEADS)[:, :, 2 * i + a, 0:NOPE]).then_inc(wq_in, 16)
    sp.dma_start(raw[1][:].rearrange("p k a c -> p k (a c)"), io["mla_w_kvb"][0].rearrange(
        "(k p) n -> p k n", p=P)[:, :, bass.ds(i * 2 * (NOPE + VDIM), 2 * (NOPE + VDIM))]).then_inc(wkv_in, 16)


def mla_attention_stage(nc, io, scratch, raw):
    PAIRS = HEADS // 2
    Q_TASKS, K_TASKS, V_TASKS = 2 * 3, 2 * 2, NPT // 2
    PROJ = Q_TASKS + K_TASKS + V_TASKS
    QK = Q_TASKS + K_TASKS
    WEIGHTS_AT = 6
    TAIL = {13: (0, 1), 14: (2, 3), 15: (4, 5, 6, 7), 16: (8, 9)}
    with nc.cleanup_on_exit(), ExitStack() as ctx:
        def sb(name, shape, dt=F32):
            return ctx.enter_context(nc.sbuf_tensor(name, shape, dt))

        wq_raw, wkv_raw = raw
        wq = [sb(f"b_wq{s}", [P, QT, 2, NOPE], F32R) for s in "hl"]
        wkv = [sb(f"b_wkv{s}", [P, CT, 2, NOPE + VDIM], F32R) for s in "hl"]
        qn = [sb(f"b_qn{s}", [P, 2, TOK], F32R) for s in "hl"]
        kn = [sb(f"b_kn{s}", [P, 2, SEQ], F32R) for s in "hl"]
        v = [sb(f"b_v{s}", [P, NPT, 2 * VDIM], F32R) for s in "hl"]
        qr = sb("b_qr", [P, 2, SEQ], F32R)
        prob = [sb(f"b_p{u}", [P, SEQ]) for u in range(3)]
        pt = [[sb(f"b_pt{u}{s}", [P, NPT, GQ], F32R) for s in "hl"] for u in range(2)]
        o_st = [sb(f"b_o{u}", [P, GQ]) for u in range(2)]
        stat = sb("b_stat", [P, STEPS, 4])
        bank = ctx.enter_context(nc.psum_tensor("b_ps", [P, 8, 512], F32))
        score = [bank[:, 2 * u:2 * u + 2, :].rearrange("p b c -> p (b c)") for u in range(2)]
        cqT, ckvT, krT, ident = io["cqT"], io["ckvT"], io["krT"], io["ident"]

        def signal(name, credit=0):
            return Signal(nc, name, credit)

        wq_in, wkv_in, qr_in = signal("b_wq_in"), signal("b_wkv_in"), signal("b_qr_in")
        w_hi, w_lo = signal("b_w_hi"), signal("b_w_lo")
        proj = signal("b_proj", 1)
        proj_hi, proj_lo = signal("b_proj_hi"), signal("b_proj_lo", 4)
        q_smp_done = signal("b_q_smp")
        s_done = signal("b_s")
        nmax, nbias = signal("b_nmax", 1), signal("b_nbias")
        exp_done = signal("b_exp", 2)
        recip, normed = signal("b_recip"), signal("b_normed")
        t_done, t_hi, t_lo = signal("b_t"), signal("b_t_hi"), signal("b_t_lo", 3)
        zero_done = signal("b_zero")
        pv_done, o_done = signal("b_pv", 2), signal("b_o", 1)
        o_out = [signal(f"b_o_out{u}", 16) for u in range(2)]

        def task_bank(m):
            return bank[:, 4 + m % 3, :]

        def project_bank(n):
            return bank[:, n % 4 if n < QK else 4 + n % 3, :]

        def pairs(engine, body):
            with engine.Fori(0, PAIRS - 1) as i:
                body(i, False)
            body(PAIRS - 1, True)

        block = ctx.enter_context(nc.Block())

        @block.sync
        def _(sp):
            def load_weights(i):
                load_raw_weights(sp, io, raw, i, wq_in.sem, wkv_in.sem)

            def load_rotary(i):
                sp.dma_start(f32(qr[:]), scratch["qr"][bass.ds(2 * i, 2), :, 0:SEQ].rearrange(
                    "h p c -> p h c")).then_inc(qr_in.sem, 16)

            def store(i, g):
                o_done.wait(sp, i * GROUPS + g + 1)
                cols = slice((g % 4) * GQ, (g % 4 + 1) * GQ)
                sp.dma_start(scratch["oT"][2 * i + g // 4, :, cols], o_st[g % 2][:]).then_inc(
                    o_out[g % 2].sem, 16)

            for x in o_out:
                x.start(sp)
            sp.sem_inc(wq_in.sem, 32)
            sp.sem_inc(wkv_in.sem, 16)
            load_rotary(0)
            w_lo.wait(sp, 2)
            load_weights(1)

            def body(i, more_weights, more_pairs):
                for g in range(GROUPS - 1):
                    store(i, g)
                if more_weights:
                    w_lo.wait(sp, 2 * (i + 2))
                    load_weights(i + 2)
                if more_pairs:
                    s_done.wait(sp, STEPS * (i + 1))
                    load_rotary(i + 1)
                store(i, GROUPS - 1)

            with sp.Fori(0, PAIRS - 2) as i:
                body(i, True, True)
            body(PAIRS - 2, False, True)
            body(PAIRS - 1, False, False)
            for x in o_out:
                x.wait(sp, 16 * PAIRS * GROUPS // 2)

        @block.scalar
        def _(act):
            exp_done.start(act)
            o_done.start(act)

            def project_hi(i, n):
                proj.wait(act, PROJ * i + n + 1)
                ps = project_bank(n)
                if n < Q_TASKS:
                    a, c = n // 3, n % 3
                    act.copy(qn[0][:, a, c * 384:(c + 1) * 384], ps[:, 0:384]).then_inc(proj_hi.sem, 1)
                    if c == 2:
                        act.copy(io["q_smp"][:, 2 * i + a, :], ps[:, 256:384]).then_inc(q_smp_done.sem, 1)
                elif n < Q_TASKS + K_TASKS:
                    a, c = (n - Q_TASKS) // 2, (n - Q_TASKS) % 2
                    act.copy(kn[0][:, a, c * 512:(c + 1) * 512], ps).then_inc(proj_hi.sem, 1)
                else:
                    t = 2 * (n - Q_TASKS - K_TASKS)
                    act.copy(v[0][:, t:t + 2, :], ps.rearrange("p (t c) -> p t c", t=2)).then_inc(
                        proj_hi.sem, 1)

            def weights_hi(i):
                wq_in.wait(act, 32 * (i + 1))
                act.copy(wq[0][:], wq_raw[:]).then_inc(w_hi.sem, 1)
                wkv_in.wait(act, 16 * (i + 1))
                act.copy(wkv[0][:], wkv_raw[:]).then_inc(w_hi.sem, 1)

            def body(i, last):
                def exponential(n):
                    first, _, used = score_columns(n % NPT)
                    nbias.wait(act, STEPS * i + n + 1)
                    if n >= 3:
                        t_done.wait(act, T_TASKS * i + tasks_before(n - 2))
                    act.activation(prob[n % 3][:, 0:used], score[n % 2][:, first:first + used], ACT.Exp,
                                   bias=stat[:, n, 1:2], scale=MLA_SCALE,
                                   accum_out=stat[:, n, 2:3]).then_inc(exp_done.sem, 1)

                def transposed_hi(n):
                    g, at = n // 2, (n % 2) * P
                    for j, task in enumerate(transpose_tasks(n)):
                        m = tasks_before(n) + j
                        t_done.wait(act, T_TASKS * i + m + 1)
                        pv_done.wait(act, GROUPS * i + g - 1)
                        s0 = task[0][1]
                        act.copy(pt[g % 2][0][:, s0:s0 + len(task), at:at + P],
                                 task_bank(m)[:, 0:len(task) * P].rearrange(
                                     "p (s c) -> p s c", c=P)).then_inc(t_hi.sem, 1)

                def output(g):
                    pv_done.wait(act, GROUPS * i + g + 1)
                    o_out[g % 2].wait(act, 16 * (GROUPS // 2 * i + g // 2))
                    act.copy(o_st[g % 2][:], bank[:, 7, 0:GQ]).then_inc(o_done.sem, 1)

                exponential(0)
                project_hi(i, QK)
                exponential(1)
                for n in range(QK + 1, PROJ):
                    project_hi(i, n)
                for n in range(STEPS):
                    if n + 2 < STEPS:
                        exponential(n + 2)
                    if n == WEIGHTS_AT and not last:
                        weights_hi(i + 1)
                    transposed_hi(n)
                    if n % 2 == 0 and n >= 2:
                        output(n // 2 - 1)
                    for m in TAIL.get(n, ()) if not last else ():
                        project_hi(i + 1, m)
                output(GROUPS - 1)
                for m in TAIL[STEPS] if not last else ():
                    project_hi(i + 1, m)

            weights_hi(0)
            for n in range(QK):
                project_hi(0, n)
            pairs(act, body)

        @block.vector
        def _(dve):
            nmax.start(dve)
            proj_lo.start(dve)
            t_lo.start(dve)
            for u in range(2):
                for x in pt[u]:
                    dve.memset(f32(x[:, 0, 0:P]), 0.0).then_inc(zero_done.sem, 1)

            def project_lo(i, n):
                proj_hi.wait(dve, PROJ * i + n + 1)
                if n < Q_TASKS and n % 3 == 2:
                    q_smp_done.wait(dve, 2 * i + n // 3 + 1)
                ps = project_bank(n)
                if n < Q_TASKS:
                    a, c = n // 3, n % 3
                    out, hi, src = (*(x[:, a, c * 384:(c + 1) * 384] for x in qn[::-1]), ps[:, 0:384])
                elif n < Q_TASKS + K_TASKS:
                    a, c = (n - Q_TASKS) // 2, (n - Q_TASKS) % 2
                    out, hi, src = (*(x[:, a, c * 512:(c + 1) * 512] for x in kn[::-1]), ps)
                else:
                    t = 2 * (n - Q_TASKS - K_TASKS)
                    out, hi, src = (*(x[:, t:t + 2, :] for x in v[::-1]),
                                    ps.rearrange("p (t c) -> p t c", t=2))
                dve.tensor_tensor(out, src, f32(hi), ALU.subtract).then_inc(proj_lo.sem, 1)

            def weights_lo(i):
                w_hi.wait(dve, 2 * i + 1)
                dve.tensor_tensor(wq[1][:], wq_raw[:], f32(wq[0][:]), ALU.subtract).then_inc(w_lo.sem, 1)
                w_hi.wait(dve, 2 * i + 2)
                dve.tensor_tensor(wkv[1][:], wkv_raw[:], f32(wkv[0][:]), ALU.subtract).then_inc(w_lo.sem, 1)

            def body(i, last):
                def maximum(n):
                    first, _, used = score_columns(n % NPT)
                    s_done.wait(dve, STEPS * i + n + 1)
                    exp_done.wait(dve, STEPS * i + n - 1)
                    dve.tensor_reduce(stat[:, n, 0:1], score[n % 2][:, first:first + used], AX.X, ALU.max,
                                      negate=True).then_inc(nmax.sem, 1)
                    nmax.wait(dve, STEPS * i + n + 1)
                    dve.tensor_scalar(stat[:, n, 1:2], stat[:, n, 0:1], MLA_SCALE, None,
                                      ALU.mult).then_inc(nbias.sem, 1)

                def normalise(n):
                    used = (n % NPT + 1) * P
                    exp_done.wait(dve, STEPS * i + n + 1)
                    dve.reciprocal(stat[:, n, 3:4], stat[:, n, 2:3]).then_inc(recip.sem, 1)
                    recip.wait(dve, STEPS * i + n + 1)
                    dve.tensor_scalar(prob[n % 3][:, 0:used], prob[n % 3][:, 0:used], stat[:, n, 3:4], None,
                                      ALU.mult).then_inc(normed.sem, 1)

                def transposed_lo(n):
                    g, at = n // 2, (n % 2) * P
                    for j, task in enumerate(transpose_tasks(n)):
                        m = tasks_before(n) + j
                        t_hi.wait(dve, T_TASKS * i + m + 1)
                        s0 = task[0][1]
                        hi, lo = (x[:, s0:s0 + len(task), at:at + P] for x in pt[g % 2])
                        dve.tensor_tensor(lo, task_bank(m)[:, 0:len(task) * P].rearrange(
                            "p (s c) -> p s c", c=P), f32(hi), ALU.subtract).then_inc(t_lo.sem, 1)

                maximum(0)
                maximum(1)
                project_lo(i, QK)
                normalise(0)
                for n in range(QK + 1, PROJ):
                    project_lo(i, n)
                maximum(2)
                for n in range(STEPS):
                    if n + 3 < STEPS:
                        maximum(n + 3)
                    if n + 1 < STEPS:
                        normalise(n + 1)
                    if n == WEIGHTS_AT and not last:
                        weights_lo(i + 1)
                    transposed_lo(n)
                    for m in TAIL.get(n, ()) if not last else ():
                        project_lo(i + 1, m)
                for m in TAIL[STEPS] if not last else ():
                    project_lo(i + 1, m)

            weights_lo(0)
            for n in range(QK):
                project_lo(0, n)
            pairs(dve, body)

        @block.tensor
        def _(pe):
            proj.start(pe)
            pv_done.start(pe)

            def project(i, n, first=False):
                if n < 4 and not first:
                    exp_done.wait(pe, STEPS * i + n // 2 - 1)
                elif n >= 4:
                    proj_lo.wait(pe, PROJ * i + n - 3 if n < QK else PROJ * i + max(n - 2, QK))
                ps = project_bank(n)
                if n < Q_TASKS:
                    a, c = n // 3, n % 3
                    for k in range(QT):
                        last = product(pe, ps[:, 0:384], [w[:, k, a, :] for w in wq],
                                       [x[:, k, c * 384:(c + 1) * 384] for x in cqT], k == 0, k == QT - 1)
                elif n < Q_TASKS + K_TASKS:
                    a, c = (n - Q_TASKS) // 2, (n - Q_TASKS) % 2
                    for k in range(CT):
                        last = product(pe, ps, [w[:, k, a, 0:NOPE] for w in wkv],
                                       [x[:, k, c * 512:(c + 1) * 512] for x in ckvT], k == 0, k == CT - 1)
                else:
                    for j in range(2):
                        t = 2 * (n - Q_TASKS - K_TASKS) + j
                        for k in range(CT):
                            last = product(pe, ps[:, j * GQ:(j + 1) * GQ],
                                           [x[:, k, t * P:(t + 1) * P] for x in ckvT],
                                           [w[:, k, :, NOPE:] for w in wkv], k == 0, k == CT - 1)
                last.then_inc(proj.sem, 1)

            def body(i, is_last):
                def scores(n):
                    a, q = n // NPT, n % NPT
                    tile = slice(q * P, (q + 1) * P)
                    exp_done.wait(pe, STEPS * i + n - 1)
                    first, chunks, used = score_columns(q)
                    for at, width, key in chunks:
                        out = score[n % 2][:, at:at + width]
                        keys = slice(key, key + width)
                        product(pe, out, [x[:, a, tile] for x in qn], [x[:, a, keys] for x in kn], True, False)
                        pe.matmul(out, qr[:, a, tile], krT[0][:, keys], start=False, stop=False)
                        last_chunk = (at, width, key) == chunks[-1]
                        last = pe.matmul(out, qr[:, a, tile], krT[1][:, keys], start=False, stop=not last_chunk)
                    end = first + used
                    last = pe.matmul(score[n % 2][:, end - P:end], io["ident16"][:], io["chunk_mask"][:],
                                     start=False, stop=True)
                    last.then_inc(s_done.sem, 1)

                def transposes(n):
                    normed.wait(pe, STEPS * i + n + 1)
                    for j, task in enumerate(transpose_tasks(n)):
                        m = tasks_before(n) + j
                        t_lo.wait(pe, T_TASKS * i + m - 2)
                        for c, (k, _) in enumerate(task):
                            last = pe.transpose(task_bank(m)[:, c * P:(c + 1) * P],
                                                prob[n % 3][:, k * P:(k + 1) * P], ident[:])
                        last.then_inc(t_done.sem, 1)

                def values(g):
                    a, last_q = g // 4, 2 * (g % 4) + 1
                    t_lo.wait(pe, T_TASKS * i + tasks_before(2 * g + 2))
                    o_done.wait(pe, GROUPS * i + g)
                    order = [(last_q, 0)] + [(k, k + 1) for k in range(last_q)]
                    for k, slot in order:
                        last = product(pe, bank[:, 7, 0:GQ],
                                       [x[:, k, a * VDIM:(a + 1) * VDIM] for x in v],
                                       [x[:, slot, :] for x in pt[g % 2]], k == last_q, k == last_q - 1)
                    last.then_inc(pv_done.sem, 1)

                proj_lo.wait(pe, PROJ * i + QK)
                qr_in.wait(pe, 16 * (i + 1))
                scores(0)
                scores(1)
                t_lo.wait(pe, T_TASKS * i)
                for n in range(QK, PROJ):
                    project(i, n)
                proj_lo.wait(pe, PROJ * (i + 1))
                zero_done.wait(pe, 4)
                scores(2)
                for n in range(STEPS):
                    if n + 3 < STEPS:
                        scores(n + 3)
                    transposes(n)
                    if n % 2 == 0 and n >= 2:
                        values(n // 2 - 1)
                    if n == min(TAIL) and not is_last:
                        w_lo.wait(pe, 2 * (i + 2))
                    for m in TAIL.get(n, ()) if not is_last else ():
                        project(i + 1, m)
                values(GROUPS - 1)
                for m in TAIL[STEPS] if not is_last else ():
                    project(i + 1, m)

            w_lo.wait(pe, 2)
            for n in range(QK):
                project(0, n, True)

            pairs(pe, body)


def mla_sample_stage(nc, io, scratch):
    assert (PAST + DEC_SEQ - 1) // CHUNK <= PAST // CHUNK
    with nc.cleanup_on_exit(), ExitStack() as ctx:
        def sb(name, shape, dt=F32):
            return ctx.enter_context(nc.sbuf_tensor(name, shape, dt))

        def signal(name, credit=0):
            return Signal(nc, name, credit)

        w_kvb = sb("c_wkvb", [P, CT, HEADS, NOPE + VDIM])
        wkT = sb("c_wkT", [P, HEADS, CT, P])
        cache_c = sb("c_cache_c", [P, DEC_BATCH, KV_LORA])
        cache_r = sb("c_cache_r", [P, DEC_BATCH, 2, ROPE])
        new_c = sb("c_new_c", [DEC_SEQ, DEC_BATCH, KV_LORA])
        qr_in = sb("c_qr_in", [P, HEADS, P])
        qr = sb("c_qr", [P, DEC_BATCH, HEADS, DEC_SEQ])
        qa = sb("c_qa", [P, CT, DEC_BATCH, HEADS, DEC_SEQ])
        keysT = [sb(f"c_keysT{u}", [P, CT + 1, KEYS]) for u in range(2)]
        prob = [sb(f"c_p{u}", [P, KEYS]) for u in range(2)]
        pT = [sb(f"c_pT{u}", [P, 2, P]) for u in range(2)]
        latent = sb("c_latent", [P, CT, HEADS, P])
        o_all = sb("c_o", [P, HEADS, P])
        stat = sb("c_stat", [P, DEC_BATCH, 4])
        bank = ctx.enter_context(nc.psum_tensor("c_ps", [P, 8, 512], F32))
        q_smp, ckvT, krT, ident = io["q_smp"], io["ckvT"], io["krT"], io["ident"]
        SMP = slice(SEQ, TOK)

        cache_in, qr_loaded, qr_ready = (signal(f"c_{n}") for n in ("cache", "qrl", "qrr"))
        w_in = [signal(f"c_w{j}") for j in range(4)]
        wt_done, wt_out, qa_done, qa_out = (signal(f"c_{n}") for n in ("wt", "wto", "qad", "qao"))
        kt_done, kt_past, kt_new = (signal(f"c_{n}") for n in ("kt", "ktp", "ktn"))
        s_done, nmax, nbias, exp_done = (signal(f"c_{n}") for n in ("s", "nm", "nb", "e"))
        recip, normed, t_done, t_out = (signal(f"c_{n}") for n in ("rc", "nd", "t", "to"))
        pv_done, lat_out, o_done, o_out, stored = (signal(f"c_{n}") for n in ("pv", "lo", "o", "oo", "st"))

        block = ctx.enter_context(nc.Block())

        @block.sync
        def _(sp):
            for j in range(4):
                cols = slice(2 * j * (NOPE + VDIM), 2 * (j + 1) * (NOPE + VDIM))
                sp.dma_start(w_kvb[:, :, 2 * j:2 * j + 2, :].rearrange("p k h c -> p k (h c)"),
                             io["mla_w_kvb"][0].rearrange("(k p) n -> p k n", p=P)[:, :, cols]).then_inc(
                                 w_in[j].sem, 16)
            sp.dma_start(qr_in[:], scratch["qr"][:, :, SMP].rearrange("h p c -> p h c")).then_inc(
                qr_loaded.sem, 16)
            for dst, src in ((cache_c[:], io["cache_mla_ckv"][0].rearrange("b s c -> s b c")),
                             (cache_r[:, :, 0, :], io["cache_mla_krope"][0].rearrange("b s c -> s b c")),
                             (cache_r[:, :, 1, :], io["cache_mla_krope"][0].rearrange("b s c -> s b c")),
                             (new_c[:], io["new_s_ckv"][0].rearrange("b s c -> s b c"))):
                sp.dma_start(dst, src).then_inc(cache_in.sem, 16)
            o_out.wait(sp, 2)
            sp.dma_start(scratch["oT"][:, :, SMP].rearrange("h p c -> p h c"), o_all[:]).then_inc(
                stored.sem, 16)
            stored.wait(sp, 16)

        @block.scalar
        def _(act):
            for j in range(4):
                wt_done.wait(act, j + 1)
                act.copy(wkT[:, 2 * j:2 * j + 2, :, :], bank[:, j, :].rearrange(
                    "p (h k c) -> p h k c", h=2, k=CT)).then_inc(wt_out.sem, 1)
            for j in range(4):
                qa_done.wait(act, j + 1)
                act.copy(qa[:, j // 2, :, 4 * (j % 2):4 * (j % 2) + 4, :],
                         bank[:, 4 + j, :].rearrange("p (h b q) -> p b h q", h=4, b=DEC_BATCH)).then_inc(
                             qa_out.sem, 1)

            def past_keys(b):
                kt_done.wait(act, b + 1)
                if b >= 2:
                    s_done.wait(act, b - 1)
                act.copy(keysT[b % 2][:, :, 0:PAST], bank[:, b % 2, 0:3 * PAST].rearrange(
                    "p (k c) -> p k c", k=CT + 1)).then_inc(kt_past.sem, 1)

            def exponential(b):
                nbias.wait(act, b + 1)
                if b >= 2:
                    t_done.wait(act, b - 1)
                act.activation(prob[b % 2][:], bank[:, 2 + b % 2, 0:KEYS], ACT.Exp, bias=stat[:, b, 1:2],
                               scale=MLA_SCALE, accum_out=stat[:, b, 2:3]).then_inc(exp_done.sem, 1)

            def latents(b):
                pv_done.wait(act, b + 1)
                act.copy(latent[:, :, :, b * DEC_SEQ:(b + 1) * DEC_SEQ],
                         bank[:, 6 + b % 2, 0:CT * P].rearrange("p (k h q) -> p k h q", k=CT, h=HEADS)).then_inc(
                             lat_out.sem, 1)

            past_keys(0)
            past_keys(1)
            exponential(0)
            for b in range(DEC_BATCH):
                if b + 2 < DEC_BATCH:
                    past_keys(b + 2)
                if b + 1 < DEC_BATCH:
                    exponential(b + 1)
                t_done.wait(act, b + 1)
                if b >= 2:
                    pv_done.wait(act, b - 1)
                act.copy(pT[b % 2][:, 0, :], bank[:, 4 + b % 2, 0:P]).then_inc(t_out.sem, 1)
                act.copy(pT[b % 2][0:DEC_SEQ, 1, :], bank[0:DEC_SEQ, 4 + b % 2, P:2 * P]).then_inc(
                    t_out.sem, 1)
                if b >= 1:
                    latents(b - 1)
            latents(DEC_BATCH - 1)
            for j in range(2):
                o_done.wait(act, j + 1)
                act.copy(o_all[:, 4 * j:4 * j + 4, :], bank[:, 4 + j, :].rearrange(
                    "p (h c) -> p h c", h=4)).then_inc(o_out.sem, 1)

        @block.vector
        def _(dve):
            qr_loaded.wait(dve, 16)
            dve.tensor_copy(qr[:].rearrange("p b h q -> p h b q"),
                            qr_in[:].rearrange("p h (b q) -> p h b q", b=DEC_BATCH)).then_inc(qr_ready.sem, 1)

            def new_keys(b):
                cols = slice(SEQ + b * DEC_SEQ, SEQ + (b + 1) * DEC_SEQ)
                if b >= 2:
                    s_done.wait(dve, b - 1)
                dve.tensor_tensor(keysT[b % 2][:, 0:CT, PAST:KEYS], f32(ckvT[0][:, :, cols]),
                                  f32(ckvT[1][:, :, cols]), ALU.add).then_inc(kt_new.sem, 1)
                dve.tensor_tensor(keysT[b % 2][:, CT, PAST:KEYS], f32(krT[0][:, cols]),
                                  f32(krT[1][:, cols]), ALU.add).then_inc(kt_new.sem, 1)

            def softmax(b):
                s_done.wait(dve, b + 1)
                dve.tensor_reduce(stat[:, b, 0:1], bank[:, 2 + b % 2, 0:KEYS], AX.X, ALU.max,
                                  negate=True).then_inc(nmax.sem, 1)
                nmax.wait(dve, b + 1)
                dve.tensor_scalar(stat[:, b, 1:2], stat[:, b, 0:1], MLA_SCALE, None,
                                  ALU.mult).then_inc(nbias.sem, 1)
                exp_done.wait(dve, b + 1)
                dve.reciprocal(stat[:, b, 3:4], stat[:, b, 2:3]).then_inc(recip.sem, 1)
                recip.wait(dve, b + 1)
                dve.tensor_scalar(prob[b % 2][:], prob[b % 2][:], stat[:, b, 3:4], None,
                                  ALU.mult).then_inc(normed.sem, 1)

            new_keys(0)
            new_keys(1)
            for b in range(DEC_BATCH):
                softmax(b)
                if b + 2 < DEC_BATCH:
                    new_keys(b + 2)

        @block.tensor
        def _(pe):
            for j in range(4):
                w_in[j].wait(pe, 16)
                for h in range(2):
                    for k in range(CT):
                        at = (h * CT + k) * P
                        last = pe.transpose(bank[:, j, at:at + P], w_kvb[:, k, 2 * j + h, 0:NOPE], ident[:])
                last.then_inc(wt_done.sem, 1)
            for j in range(4):
                k = j // 2
                wt_out.wait(pe, 4)
                for c in range(4):
                    h = 4 * (j % 2) + c
                    last = pe.matmul(bank[:, 4 + j, c * P:(c + 1) * P], wkT[:, h, k, :], q_smp[:, h, :],
                                     start=True, stop=True)
                last.then_inc(qa_done.sem, 1)

            def keys(b):
                if b >= 2:
                    kt_past.wait(pe, b - 1)
                for k in range(CT):
                    pe.transpose(bank[:, b % 2, k * P:(k + 1) * P], cache_c[:, b, k * P:(k + 1) * P], ident[:])
                pe.transpose(bank[:, b % 2, CT * P:(CT + 1) * P],
                             cache_r[:, b, :, :].rearrange("p i c -> p (i c)"), ident[:]).then_inc(kt_done.sem, 1)

            def scores(b):
                kt_past.wait(pe, b + 1)
                kt_new.wait(pe, 2 * (b + 1))
                if b >= 2:
                    exp_done.wait(pe, b - 1)
                stationary = [qa[:, 0, b, :, :], qa[:, 1, b, :, :], qr[:, b, :, :]]
                for k, w in enumerate(stationary):
                    last = pe.matmul(bank[:, 2 + b % 2, 0:KEYS], w.rearrange("p h q -> p (h q)"),
                                     keysT[b % 2][:, k, :], start=k == 0, stop=k == CT)
                last.then_inc(s_done.sem, 1)

            def transposes(b):
                normed.wait(pe, b + 1)
                if b >= 2:
                    t_out.wait(pe, 2 * (b - 1))
                pe.transpose(bank[:, 4 + b % 2, 0:P], prob[b % 2][:, 0:PAST], ident[:])
                pe.transpose(bank[0:DEC_SEQ, 4 + b % 2, P:2 * P], prob[b % 2][:, PAST:KEYS],
                             ident[:]).then_inc(t_done.sem, 1)

            def values(b):
                t_out.wait(pe, 2 * (b + 1))
                if b >= 2:
                    lat_out.wait(pe, b - 1)
                for k in range(CT):
                    out = bank[:, 6 + b % 2, k * P:(k + 1) * P]
                    pe.matmul(out, cache_c[:, b, k * P:(k + 1) * P], pT[b % 2][:, 0, :], start=True, stop=False)
                    last = pe.matmul(out, new_c[:, b, k * P:(k + 1) * P], pT[b % 2][0:DEC_SEQ, 1, :],
                                     start=False, stop=True)
                last.then_inc(pv_done.sem, 1)

            cache_in.wait(pe, 64)
            keys(0)
            keys(1)
            qa_out.wait(pe, 4)
            qr_ready.wait(pe, 1)
            scores(0)
            scores(1)
            for b in range(DEC_BATCH):
                if b + 2 < DEC_BATCH:
                    keys(b + 2)
                if b >= 1:
                    values(b - 1)
                if b + 2 < DEC_BATCH:
                    scores(b + 2)
                transposes(b)
            values(DEC_BATCH - 1)
            lat_out.wait(pe, DEC_BATCH)
            t_out.wait(pe, 2 * DEC_BATCH)
            for j in range(2):
                for c in range(4):
                    h = 4 * j + c
                    for k in range(CT):
                        last = pe.matmul(bank[:, 4 + j, c * P:(c + 1) * P], w_kvb[:, k, h, NOPE:],
                                         latent[:, k, h, :], start=k == 0, stop=k == CT - 1)
                last.then_inc(o_done.sem, 1)


class NormToFeatures:

    def __init__(self, nc, ctx, name, x, gain, xn, junk, h_t, bank, ident):
        self.x, self.gain, self.xn, self.junk, self.h_t, self.bank = x, gain, xn, junk, h_t, bank
        self.ident = ident
        self.stat = ctx.enter_context(nc.sbuf_tensor(f"{name}_stat", [P, NT, 3], F32))
        self.half = ctx.enter_context(nc.sbuf_tensor(f"{name}_half", [P, 1], F32))
        self.squared, self.mean, self.rs, self.normed, self.turned, self.hi, self.lo, self.half_set = (
            Signal(nc, f"{name}_{n}") for n in ("sq", "mean", "rs", "xn", "xt", "hi", "lo", "half"))

    def act_squares(self, act, t):
        if t >= 1:
            self.squared.wait(act, t)
        act.activation(self.junk[:], self.x[:, t, :], ACT.Square,
                       accum_out=self.stat[:, t, 0:1]).then_inc(self.squared.sem, 1)

    def pool_start(self, pool):
        pool.memset(self.half[:], -0.5).then_inc(self.half_set.sem, 1)
        self.half_set.wait(pool, 1)

    def pool_inverse_rms(self, pool, t):
        self.squared.wait(pool, t + 1)
        pool.tensor_scalar(self.stat[:, t, 1:2], self.stat[:, t, 0:1], 1.0 / D_MODEL, EPS,
                           ALU.mult, ALU.add).then_inc(self.mean.sem, 1)
        self.mean.wait(pool, t + 1)
        pool.tensor_tensor(self.stat[:, t, 2:3], self.stat[:, t, 1:2], self.half[:],
                           ALU.pow).then_inc(self.rs.sem, 1)

    def dve_scale(self, dve, t, stored=None):
        self.rs.wait(dve, t + 1)
        if t >= 2 and stored:
            stored[t % 2].wait(dve, 16 * (t // 2))
        elif t >= 2:
            self.turned.wait(dve, 2 * (t - 1))
        dve.scalar_tensor_tensor(out=self.xn[t % 2][:], in0=self.x[:, t, :], scalar=self.stat[:, t, 2:3],
                                 in1=self.gain[:], op0=ALU.mult, op1=ALU.mult).then_inc(self.normed.sem, 1)

    def pe_transposes(self, pe, t):
        self.normed.wait(pe, t + 1)
        for b in range(2):
            if t >= 2:
                self.lo.wait(pe, 2 * (t - 2) + b + 1)
            for c in range(4):
                k = 4 * b + c
                last = pe.transpose(self.bank[:, 2 * (t % 2) + b, c * P:(c + 1) * P],
                                    self.xn[t % 2][:, k * P:(k + 1) * P], self.ident[:])
            last.then_inc(self.turned.sem, 1)

    def _bank(self, t, b):
        return self.bank[:, 2 * (t % 2) + b, :].rearrange("p (k c) -> p k c", k=4)

    def act_hi(self, act, t):
        for b in range(2):
            self.turned.wait(act, 2 * t + b + 1)
            act.copy(self.h_t[0][:, 4 * b:4 * b + 4, t * P:(t + 1) * P], self._bank(t, b)).then_inc(
                self.hi.sem, 1)

    def dve_lo(self, dve, t):
        for b in range(2):
            self.hi.wait(dve, 2 * t + b + 1)
            hi, lo = (h[:, 4 * b:4 * b + 4, t * P:(t + 1) * P] for h in self.h_t)
            dve.tensor_tensor(lo, self._bank(t, b), f32(hi), ALU.subtract).then_inc(self.lo.sem, 1)


def tokens_split(nc, ctx, name):
    hi = ctx.enter_context(nc.sbuf_tensor(f"{name}_h", [P, KT, TOK], F32R))
    with nc.sbuf_tensor(f"{name}_raw", [P, KT, TOK], F32) as raw:
        pass
    return raw, (hi, ctx.enter_context(nc.sbuf_tensor(f"{name}_l", [P, KT, TOK], F32R)))


def output_and_mlp_stage(nc, io, scratch, layer, w_o, load_x, tokens, next_gain):
    final = layer == 1
    CH = 4
    CHUNKS = D_FF // (CH * P)
    GROUP = TOK // 3
    HALVES = 2
    DOWN = NT * HALVES
    O_PIECES = ((0, 1), (1, 3), (3, 6), (6, 9))
    X_FIRST = 2
    x = io["x"]
    with nc.cleanup_on_exit(), ExitStack() as ctx:
        name = f"m{layer}"

        def sb(n, shape, dt=F32, stack=ctx):
            return stack.enter_context(nc.sbuf_tensor(f"{name}_{n}", shape, dt))

        def signal(n, credit=0):
            return Signal(nc, f"{name}_{n}", credit)

        def split(n, shape, stack=ctx):
            hi = sb(f"{n}h", shape, F32R, stack)
            with ExitStack() as before:
                raw = sb(f"{n}r", shape, F32, before)
            return raw, (hi, sb(f"{n}l", shape, F32R, stack))

        o_raw, h_t = tokens
        w_o_t = [split(f"dn{u}", [P, D_MODEL]) for u in range(CH)]
        w_dn = [w for _, w in w_o_t]
        with ExitStack() as early:
            w_o_t += [split(f"wo{u}", [P, D_MODEL], early) for u in range(CH, KT)]
            gain = sb("gain", [P, D_MODEL], stack=early)
        u_t = [sb(f"u{s}", [P, CH, TOK], F32R) for s in "hl"]
        with ExitStack() as late:
            gain_2 = sb("gain2", [P, D_MODEL], stack=late)
        w_up = [[sb(f"up0{s}", [P, KT, P], F32R) for s in "hl"]]
        with ExitStack() as early:
            xn = [sb(f"xn{u}", [P, D_MODEL], stack=early) for u in range(2)]
        w_up.append([sb(f"up1{s}", [P, KT, P], F32R) for s in "hl"])
        up_raw = sb("up_raw", [P, KT, P])
        dn_raw = sb("dn_raw", [P, D_MODEL])
        with ExitStack() as early:
            junk = sb("junk", [P, D_MODEL], BF16, early)
        relu = [sb(f"relu{u}", [P, GROUP]) for u in range(2)]
        sq = [sb(f"sq{u}", [P, GROUP]) for u in range(2)]
        bank = ctx.enter_context(nc.psum_tensor(f"{name}_ps", [P, 8, 512], F32))
        norm = NormToFeatures(nc, ctx, f"{name}n", x, gain, xn, junk, h_t, bank, io["ident"])
        norm_2 = NormToFeatures(nc, ctx, f"{name}f", x, gain_2, xn, junk, h_t, bank, io["ident"])
        y_out = [signal(f"yout{u}") for u in range(2)]

        x_in, gain_in = [signal(f"x{n}") for n in range(3)], signal("gain")
        w_in, o_in = [signal(f"w{k}") for k in range(KT)], [signal(f"o{g}") for g in range(len(O_PIECES))]
        w_hi, w_lo = signal("whi"), [signal("wlo_pool"), signal("wlo_dve")]
        o_hi, o_lo = signal("ohi"), signal("olo")
        up_in, up_hi, up_lo = signal("upin"), signal("uphi"), signal("uplo", 1)
        dn_in, dn_hi, dn_lo = signal("dnin"), signal("dnhi"), signal("dnlo", 1)
        up_done, dn_done = signal("up", 4), signal("dn", 1)
        relu_done, sq_done, u_hi, u_lo = signal("relu", 4), signal("sq", 2), signal("uhi"), signal("ulo", 2)
        added = signal("add", 3)

        def chunks(engine, body):
            with engine.Fori(0, CHUNKS - 1) as c:
                body(c, False)
            body(CHUNKS - 1, True)

        block = ctx.enter_context(nc.Block())

        @block.sync
        def _(sp):
            def load_w_o(k):
                sp.dma_start(w_o_t[k][0][:], w_o[k * P:(k + 1) * P, :]).then_inc(w_in[k].sem, 16)

            def load_outputs(g):
                a, b = (t * P for t in O_PIECES[g])
                sp.dma_start(o_raw[:, :, a:b], scratch["oT"][:, :, a:b].rearrange(
                    "k p c -> p k c")).then_inc(o_in[g].sem, 16)

            load_w_o(0)
            load_outputs(0)
            for k in range(1, KT):
                load_w_o(k)
            load_outputs(1)
            if load_x:
                rows = io["x_prompt"][0].rearrange("(t p) d -> p t d", p=P)
                sp.dma_start(x[:, 0:X_FIRST, :], rows[:, 0:X_FIRST, :]).then_inc(x_in[0].sem, 16)
            sp.dma_start(gain[:], io["norm_mlp"][layer:layer + 1, :].broadcast_to([P, D_MODEL])).then_inc(
                gain_in.sem, 16)
            for g in range(2, len(O_PIECES)):
                load_outputs(g)
                if load_x and g == 2:
                    sp.dma_start(x[:, X_FIRST:NPT, :], rows[:, X_FIRST:, :]).then_inc(x_in[1].sem, 16)
            if load_x:
                sp.dma_start(x[:, NPT, :], io["x_sample"].rearrange("b s d -> (b s) d")).then_inc(x_in[2].sem, 16)
            up_rows = io["mlp_w_up"][layer].rearrange("(k p) f -> p k f", p=P)
            down_rows = io["mlp_w_down"][layer].rearrange("(f p) d -> f p d", p=P)

            def body(c, last):
                for j in range(CH):
                    up_lo.wait(sp, CH * c + j)
                    sp.dma_start(up_raw[:], up_rows[:, :, bass.ds((CH * c + j) * P, P)]).then_inc(up_in.sem, 16)
                    dn_lo.wait(sp, CH * c + j)
                    sp.dma_start(dn_raw[:], down_rows[CH * c + j]).then_inc(dn_in.sem, 16)
                if not last:
                    return
                up_done.wait(sp, 12 * c + 9)
                sp.dma_start(gain_2[:], next_gain.broadcast_to([P, D_MODEL])).then_inc(gain_in.sem, 16)
                if final:
                    for t in range(NT):
                        norm_2.normed.wait(sp, t + 1)
                        rows = io["y_prompt"][0, t * P:(t + 1) * P, :] if t < NPT else \
                            io["y_sample"].rearrange("b s d -> (b s) d")
                        sp.dma_start(rows, xn[t % 2][:]).then_inc(y_out[t % 2].sem, 16)
                    for u in range(2):
                        y_out[u].wait(sp, 16 * ((NT + 1 - u) // 2))

            chunks(sp, body)

        @block.scalar
        def _(act):
            relu_done.start(act)

            def output_hi(t):
                g = [a <= t < b for a, b in O_PIECES].index(True)
                cols = slice(t * P, (t + 1) * P)
                o_in[g].wait(act, 16)
                act.copy(h_t[0][:, :, cols], o_raw[:, :, cols]).then_inc(o_hi.sem, 1)

            for k in range(KT):
                w_in[k].wait(act, 16)
                act.copy(w_o_t[k][1][0][:], w_o_t[k][0][:]).then_inc(w_hi.sem, 1)
                if k == 0:
                    output_hi(0)
            for t in range(1, NT):
                output_hi(t)
            for t in range(NT + 1):
                if t < NT:
                    added.wait(act, HALVES * (t + 1))
                    norm.act_squares(act, t)
                if t >= 1:
                    norm.act_hi(act, t - 1)
            norm.turned.wait(act, 2 * NT)

            def body(c, last):
                def up_split(j):
                    up_in.wait(act, 16 * (CH * c + j + 1))
                    up_done.wait(act, 3 * (CH * c + j) - 3)
                    act.copy(w_up[j % 2][0][:], up_raw[:]).then_inc(up_hi.sem, 1)

                up_split(0)
                up_split(1)
                for j in range(CH):
                    dn_in.wait(act, 16 * (CH * c + j + 1))
                    dn_done.wait(act, DOWN + DOWN * c)
                    act.copy(w_dn[j][0][:], dn_raw[:]).then_inc(dn_hi.sem, 1)
                    for g in range(3):
                        n = 3 * j + g
                        up_done.wait(act, 12 * c + n + 1)
                        sq_done.wait(act, 12 * c + n - 1)
                        act.activation(relu[n % 2][:], bank[:, (n + 2) % 4, 0:GROUP], ACT.Relu).then_inc(
                            relu_done.sem, 1)
                        relu_done.wait(act, 12 * c + n + 1)
                        act.activation(u_t[0][:, j, g * GROUP:(g + 1) * GROUP], relu[n % 2][:],
                                       ACT.Square).then_inc(u_hi.sem, 1)
                    if j + 2 < CH:
                        up_split(j + 2)
                if not last:
                    return
                for t in range(NT + 1):
                    if t < NT:
                        added.wait(act, DOWN + DOWN * c + HALVES * (t + 1))
                        norm_2.act_squares(act, t)
                    if t >= 1 and not final:
                        norm_2.act_hi(act, t - 1)

            chunks(act, body)

        @block.gpsimd
        def _(pool):
            up_lo.start(pool)
            dn_lo.start(pool)
            norm.pool_start(pool)
            norm_2.pool_start(pool)
            for k in range(0, KT, 2):
                w_hi.wait(pool, k + 1)
                raw, (hi, lo) = w_o_t[k]
                pool.tensor_tensor(lo[:], raw[:], f32(hi[:]), ALU.subtract).then_inc(w_lo[0].sem, 1)
            for t in range(NT):
                norm.pool_inverse_rms(pool, t)

            def body(c, last):
                def up_rest(j):
                    up_hi.wait(pool, CH * c + j + 1)
                    pool.tensor_tensor(w_up[j % 2][1][:], up_raw[:], f32(w_up[j % 2][0][:]),
                                       ALU.subtract).then_inc(up_lo.sem, 1)

                up_rest(0)
                up_rest(1)
                for j in range(CH):
                    dn_hi.wait(pool, CH * c + j + 1)
                    pool.tensor_tensor(w_dn[j][1][:], dn_raw[:], f32(w_dn[j][0][:]), ALU.subtract).then_inc(
                        dn_lo.sem, 1)
                    if j + 2 < CH:
                        up_rest(j + 2)
                if last:
                    for t in range(NT):
                        norm_2.pool_inverse_rms(pool, t)

            chunks(pool, body)

        @block.vector
        def _(dve):
            added.start(dve)
            u_lo.start(dve)
            sq_done.start(dve)

            def add(t, half, count):
                n = HALVES * t + half
                dn_done.wait(dve, count + n + 1)
                cols = slice(half * 512, (half + 1) * 512)
                dve.tensor_tensor(x[:, t, cols], bank[:, 4 + n % 3, :], x[:, t, cols], ALU.add).then_inc(
                    added.sem, 1)

            def output_lo(t):
                o_hi.wait(dve, t + 1)
                hi, lo = (h[:, :, t * P:(t + 1) * P] for h in h_t)
                dve.tensor_tensor(lo, o_raw[:, :, t * P:(t + 1) * P], f32(hi), ALU.subtract).then_inc(o_lo.sem, 1)

            output_lo(0)
            for k in range(1, KT, 2):
                w_hi.wait(dve, k + 1)
                raw, (hi, lo) = w_o_t[k]
                dve.tensor_tensor(lo[:], raw[:], f32(hi[:]), ALU.subtract).then_inc(w_lo[1].sem, 1)
            output_lo(1)
            output_lo(2)
            gain_in.wait(dve, 16)
            for t in range(NT + 2):
                if load_x and t in (0, X_FIRST, NPT):
                    x_in[(0, X_FIRST, NPT).index(t)].wait(dve, 16)
                if t < NT:
                    for half in range(HALVES):
                        add(t, half, 0)
                if t + 3 < NT:
                    output_lo(t + 3)
                if 1 <= t <= NT:
                    norm.dve_scale(dve, t - 1)
                if t >= 2:
                    norm.dve_lo(dve, t - 2)

            def body(c, last):
                for n in range(12):
                    j, g = n // 3, n % 3
                    cols = slice(g * GROUP, (g + 1) * GROUP)
                    relu_done.wait(dve, 12 * c + n + 1)
                    u_lo.wait(dve, 12 * c + n - 1)
                    dve.tensor_tensor(sq[n % 2][:], relu[n % 2][:], relu[n % 2][:], ALU.mult).then_inc(
                        sq_done.sem, 1)
                    u_hi.wait(dve, 12 * c + n + 1)
                    sq_done.wait(dve, 12 * c + n + 1)
                    dve.tensor_tensor(u_t[1][:, j, cols], sq[n % 2][:], f32(u_t[0][:, j, cols]),
                                      ALU.subtract).then_inc(u_lo.sem, 1)
                if last:
                    gain_in.wait(dve, 32)
                for t in range(NT + 2 if last else NT):
                    if t < NT:
                        for half in range(HALVES):
                            add(t, half, DOWN + DOWN * c)
                    if last and 1 <= t <= NT:
                        norm_2.dve_scale(dve, t - 1, y_out if final else None)
                    if last and t >= 2 and not final:
                        norm_2.dve_lo(dve, t - 2)

            chunks(dve, body)

        @block.tensor
        def _(pe):
            up_done.start(pe)
            dn_done.start(pe)

            def down(t, half, w, weights, count, ready=None):
                n = HALVES * t + half
                added.wait(pe, count + n - 2)
                for j, d in enumerate(weights):
                    if ready:
                        ready(j)
                    last = product(pe, bank[:, 4 + n % 3, :], [u[:, j, t * P:(t + 1) * P] for u in w],
                                   [m[:, half * 512:(half + 1) * 512] for m in d], j == 0,
                                   j == len(weights) - 1)
                last.then_inc(dn_done.sem, 1)

            for t in range(NT):
                o_lo.wait(pe, t + 1)
                for half in range(HALVES):
                    down(t, half, h_t, [w for _, w in w_o_t], 0,
                         (lambda k: w_lo[k % 2].wait(pe, k // 2 + 1)) if t == half == 0 else None)
                if t >= 2:
                    norm.pe_transposes(pe, t - 2)
            norm.pe_transposes(pe, NT - 2)
            norm.pe_transposes(pe, NT - 1)

            def body(c, last):
                for n in range(12):
                    j, g = n // 3, n % 3
                    relu_done.wait(pe, 12 * c + n - 3)
                    up_lo.wait(pe, CH * c + j + 1)
                    if j == 0:
                        norm.lo.wait(pe, 2 * (NT if g == 2 else NT - 1))
                    for k in range(KT):
                        done = product(pe, bank[:, (n + 2) % 4, 0:GROUP], [w[:, k, :] for w in w_up[j % 2]],
                                       [h[:, k, g * GROUP:(g + 1) * GROUP] for h in h_t], k == 0, k == KT - 1)
                    done.then_inc(up_done.sem, 1)
                dn_lo.wait(pe, CH * (c + 1))
                for t in range(NT):
                    u_lo.wait(pe, 12 * c + 9 + t // 3 + 1)
                    for half in range(HALVES):
                        down(t, half, u_t, w_dn, DOWN + DOWN * c)
                    if last and not final and t >= 2:
                        if t == 2:
                            relu_done.wait(pe, 12 * (c + 1))
                        norm_2.pe_transposes(pe, t - 2)
                if last and not final:
                    norm_2.pe_transposes(pe, NT - 2)
                    norm_2.pe_transposes(pe, NT - 1)

            chunks(pe, body)


def sb_input_stage(nc, io, scratch, h_t, pair_raw):
    WIDTH = 512
    GROUPS_W = 3 * D_MODEL // WIDTH
    PIECES = 4
    with nc.cleanup_on_exit(), ExitStack() as ctx:
        def sb(name, shape, dt=F32):
            return ctx.enter_context(nc.sbuf_tensor(name, shape, dt))

        def signal(name, credit=0):
            return Signal(nc, name, credit)

        w = []
        for u in range(2 * PIECES):
            hi = sb(f"d_w{u}h", [P, 2, WIDTH], F32R)
            with nc.sbuf_tensor(f"d_w{u}raw", [P, 2, WIDTH], F32) as raw:
                pass
            w.append((raw, hi, sb(f"d_w{u}l", [P, 2, WIDTH], F32R)))
        stage = [sb(f"d_out{u}", [P, WIDTH]) for u in range(3)]
        bank = ctx.enter_context(nc.psum_tensor("d_ps", [P, 8, 512], F32))

        w_in = [signal(f"d_w_in{u}") for u in range(2 * PIECES)]
        w_hi, w_lo = signal("d_w_hi"), [signal("d_wlo_dve"), signal("d_wlo_pool")]
        done, copied, stored = signal("d_done"), signal("d_copied"), [signal(f"d_st{u}") for u in range(3)]
        raw_in = signal("d_raw")
        TASKS = GROUPS_W * NT
        N = GROUPS_W * PIECES

        block = ctx.enter_context(nc.Block())

        @block.sync
        def _(sp):
            def load(n):
                g, j = n // PIECES, n % PIECES
                if g >= 2:
                    done.wait(sp, NT * (g - 1))
                sp.dma_start(w[n % (2 * PIECES)][0][:], io["sb_w_in"][0].rearrange("(k p) n -> p k n", p=P)[
                    :, 2 * j:2 * j + 2, g * WIDTH:(g + 1) * WIDTH]).then_inc(w_in[n % (2 * PIECES)].sem, 16)

            def destination(g, t):
                kind, cols = g // 2, slice((g % 2) * WIDTH, (g % 2 + 1) * WIDTH)
                if kind == 0:
                    rows = scratch["q"]
                else:
                    rows = io[f"new_{'s' if t == NPT else 'p'}_sb_{'k' if kind == 1 else 'v'}"][0].rearrange(
                        "b s h c -> (b s) (h c)")
                    t = 0 if t == NPT else t
                return rows[t * P:(t + 1) * P, cols]

            for n in range(2 * PIECES):
                load(n)
            for n in range(TASKS):
                copied.wait(sp, n + 1)
                sp.dma_start(destination(n // NT, n % NT), stage[n % 3][:]).then_inc(stored[n % 3].sem, 16)
                piece = (n // NT + 1) * PIECES + n % NT
                if n % NT < PIECES and 2 * PIECES <= piece < N:
                    load(piece)
                if n == TASKS - 4:
                    for u in range(3):
                        stored[u].wait(sp, 16 * (TASKS - NT) // 3)
                    for kind in range(3):
                        load_raw_heads(sp, io, scratch, pair_raw, kind, 0, raw_in.sem)
            for u in range(3):
                stored[u].wait(sp, 16 * TASKS // 3)
            raw_in.wait(sp, 16 * sum(RAW_LOADS))

        @block.scalar
        def _(act):
            def weights_hi(n):
                w_in[n % (2 * PIECES)].wait(act, 16 * (n // (2 * PIECES) + 1))
                raw, hi, _ = w[n % (2 * PIECES)]
                act.copy(hi[:], raw[:]).then_inc(w_hi.sem, 1)

            for n in range(PIECES):
                weights_hi(n)
            for n in range(TASKS):
                g, t = n // NT, n % NT
                if t >= NT - PIECES and g + 1 < GROUPS_W:
                    weights_hi((g + 1) * PIECES + t - (NT - PIECES))
                done.wait(act, n + 1)
                if n >= 3:
                    stored[n % 3].wait(act, 16 * (n // 3))
                act.copy(stage[n % 3][:], bank[:, 4 + n % 4, :]).then_inc(copied.sem, 1)

        def weights_rest(engine, n):
            w_hi.wait(engine, n + 1)
            raw, hi, lo = w[n % (2 * PIECES)]
            engine.tensor_tensor(lo[:], raw[:], f32(hi[:]), ALU.subtract).then_inc(w_lo[n % 2].sem, 1)

        @block.gpsimd
        def _(pool):
            for n in range(1, N, 2):
                weights_rest(pool, n)

        @block.vector
        def _(dve):
            for n in range(0, N, 2):
                weights_rest(dve, n)

        @block.tensor
        def _(pe):
            for n in range(TASKS):
                g, t = n // NT, n % NT
                if n >= 4:
                    copied.wait(pe, n - 3)
                for k in range(KT):
                    if t == 0 and k % 2 == 0:
                        piece = g * PIECES + k // 2
                        w_lo[piece % 2].wait(pe, piece // 2 + 1)
                    _, *piece = w[(g % 2) * PIECES + k // 2]
                    last = product(pe, bank[:, 4 + n % 4, :], [h[:, k, t * P:(t + 1) * P] for h in h_t],
                                   [m[:, k % 2, :] for m in piece], k == 0, k == KT - 1)
                last.then_inc(done.sem, 1)


class SbSchedule:
    PAIRS = SB_HEADS // 2
    PAIR_STEPS = 2 * NPT
    STEPS = 2 * PAIR_STEPS
    PREPARE_TASKS = [(kind, a, 4 * half, 4) for kind in range(2) for a in range(2) for half in range(2)]
    PREPARE_TASKS[-1:] = [(1, 1, 4, 2), (1, 1, 6, 2)]
    PREPARE = len(PREPARE_TASKS)
    PREPARE_AT = (0, 1, 2, 4, 5, 6, 8, 9, 10)
    VALUES_AT = 4
    UNITS, GROUPS = STEPS // 2, STEPS // 4
    AHEAD = 3
    VALUES_LAG = 1
    OUTPUT_LAG = 2

    @staticmethod
    def where(n):
        m = n % SbSchedule.PAIR_STEPS
        return n // SbSchedule.PAIR_STEPS % 2, m // 2 % 2, 2 * (m // 4) + m % 2

    @classmethod
    def tasks(cls, n, last):
        pair, _, q = cls.where(n)
        out = [("weights", t) for t in transpose_tasks(q)]
        m = n % cls.PAIR_STEPS
        if m in cls.PREPARE_AT and not (last and pair == 1):
            out.append(("prepare", cls.PREPARE_AT.index(m)))
        return out

    @classmethod
    def before(cls, n, last=False):
        return sum(len(cls.tasks(m, last)) for m in range(n))


def raw_heads(nc, ctx, name):
    return [ctx.enter_context(nc.sbuf_tensor(f"{name}_raw_{x}", [P, NPT, 2, n, SB_DIM], F32))
            for x, n in (("q", 2), ("k", 2), ("v", 1))]


RAW_LOADS = 4, 4, 1


def load_raw_heads(sp, io, scratch, raw, kind, p, done):
    rows = (scratch["q"][0:SEQ, :], *(io[f"new_p_sb_{x}"][0, 0].rearrange("s h c -> s (h c)") for x in "kv"))[kind]
    if kind == 2:
        sp.dma_start(raw[2][:].rearrange("p t a o c -> p t (a o c)"), rows.rearrange("(t p) n -> p t n", p=P)[
            :, :, bass.ds(p * 2 * SB_DIM, 2 * SB_DIM)]).then_inc(done, 16)
        return
    src = rows.rearrange("(t p) (h c) -> p t h c", p=P, h=SB_HEADS)
    for a in range(2):
        for twice in range(2):
            sp.dma_start(raw[kind][:, :, a, twice, :], src[:, :, 2 * p + a, :]).then_inc(done, 16)


def sb_attention_stage(nc, io, scratch, raw):
    S = SbSchedule
    BODIES = S.PAIRS // 2
    TASKS = S.before(S.STEPS)
    with nc.cleanup_on_exit(), ExitStack() as ctx:
        def sb(name, shape, dt=F32):
            return ctx.enter_context(nc.sbuf_tensor(name, shape, dt))

        def signal(name, credit=0):
            return Signal(nc, name, credit)

        q_st = [sb(f"e_q{u}", [P, 2, SEQ], F32R) for u in range(2)]
        k_tt = [[sb(f"e_k{u}{s}", [P, 2, SEQ], F32R) for s in "hl"] for u in range(2)]
        v = [[sb(f"e_v{u}{s}", [P, NPT, 3 * SB_DIM], F32R) for s in "hl"] for u in range(2)]
        raw_heads(nc, ctx, "e")
        v_raw = raw[2][:, :, :, 0, :]
        keep = [sb(f"e_u{u}", [P, SEQ]) for u in range(2)]
        take = [sb(f"e_b{u}", [P, SEQ]) for u in range(4)]
        rest = [sb(f"e_r{u}", [P, SEQ + 1]) for u in range(2)]
        pt = [[sb(f"e_pt{u}{s}", [P, NPT, GQ], F32R) for s in "hl"] for u in range(2)]
        o_st = [sb(f"e_o{u}", [P, GQ]) for u in range(2)]
        zero = sb("e_zero", [P, 1])
        bank = ctx.enter_context(nc.psum_tensor("e_ps", [P, 8, 512], F32))
        score = [bank[:, 2 * u:2 * u + 2, :].rearrange("p b c -> p (b c)") for u in range(2)]

        raw_in = [signal(f"e_{x}_in") for x in "qk"]
        v_in, v_hi, v_lo = (signal(f"e_v_{x}") for x in ("in", "hi", "lo"))
        arrived = [*raw_in, v_in]
        s_done = signal("e_s")
        kept, taken = signal("e_kept", 2), signal("e_taken", 2)
        scanned, weighted = signal("e_scan", 2), signal("e_weighted", 2)
        t_done, t_hi, t_lo = signal("e_t"), signal("e_t_hi"), signal("e_t_lo", 3)
        pv_done, o_done = signal("e_pv", 2), signal("e_o", 1)
        const_done = signal("e_const")
        o_out = [signal(f"e_o_out{u}", 16) for u in range(2)]

        def task_bank(m):
            return bank[:, 4 + m % 3, :]

        def operand(pair, index):
            kind, a, tile, tiles = S.PREPARE_TASKS[index]
            cols = slice(tile * P, (tile + tiles) * P)
            if kind == 0:
                q = q_st[pair][:, a, cols]
                return q, q[SB_DIM:P, :], slice(SB_DIM, P)
            hi, lo = (k[:, a, cols] for k in k_tt[pair])
            return hi, lo, slice(0, P)

        def bodies(engine, body):
            with engine.Fori(0, BODIES - 1) as i:
                body(i, False)
            body(BODIES - 1, True)

        block = ctx.enter_context(nc.Block())

        @block.sync
        def _(sp):
            def load_queries_keys(p):
                for kind in range(2):
                    load_raw_heads(sp, io, scratch, raw, kind, p, raw_in[kind].sem)

            def load_values(p):
                load_raw_heads(sp, io, scratch, raw, 2, p, v_in.sem)

            def store(i, g):
                o_done.wait(sp, S.GROUPS * i + g + 1)
                cols = slice((g % 4) * GQ, (g % 4 + 1) * GQ)
                sp.dma_start(scratch["oT"][2 * i + g // 4, :, cols], o_st[g % 2][:]).then_inc(
                    o_out[g % 2].sem, 16)

            def body(i, last):
                for pair in range(2):
                    for g in range(4):
                        store(i, 4 * pair + g)
                        if g == 1 and not last:
                            v_lo.wait(sp, 2 * i + pair + 2)
                            load_values(2 * i + pair + 2)
                        if g == 2 and not last:
                            t_done.wait(sp, S.PREPARE + TASKS * i + S.before(
                                pair * S.PAIR_STEPS + S.PREPARE_AT[-1] + 1))
                            load_queries_keys(2 * i + pair + 2)

            for x in o_out:
                x.start(sp)
            for x, loads in zip(arrived, RAW_LOADS):
                sp.sem_inc(x.sem, 16 * loads)
            t_done.wait(sp, S.PREPARE)
            load_queries_keys(1)
            v_lo.wait(sp, 1)
            load_values(1)
            bodies(sp, body)
            for x in o_out:
                x.wait(sp, 16 * BODIES * S.GROUPS // 2)

        @block.scalar
        def _(act):
            kept.start(act)
            taken.start(act)
            o_done.start(act)

            def weights(i, n, last=False):
                first, _, used = score_columns(S.where(n)[2])
                z = score[n % 2][:, first:first + used]
                s_done.wait(act, S.STEPS * i + n + 1)
                scanned.wait(act, S.STEPS * i + n - 1)
                act.activation(keep[n % 2][:, 0:used], z, ACT.Sigmoid, scale=-SB_SCALE).then_inc(kept.sem, 1)
                if n >= 4:
                    t_done.wait(act, S.PREPARE + TASKS * i + S.before(n - 3, last))
                act.activation(take[n % 4][:, 0:used], z, ACT.Sigmoid, scale=SB_SCALE).then_inc(taken.sem, 1)

            def prepare_hi(pair, index, m):
                hi = operand(pair, index)[0]
                act.copy(hi, task_bank(m)[:, 0:hi.shape[1]]).then_inc(t_hi.sem, 1)

            def values_hi(p, pair):
                v_in.wait(act, 16 * (p + 1))
                pv_done.wait(act, S.UNITS // 2 * (p - 1))
                act.copy(v[pair][0][:].rearrange("p t (b c) -> p t b c", b=3)[:, :, ::2, :],
                         v_raw).then_inc(v_hi.sem, 1)

            def transposed_hi(i, n, last):
                unit, at = n // 2, (n % 2) * P
                for j, (kind, task) in enumerate(S.tasks(n, last)):
                    m = S.before(n, last) + j
                    t_done.wait(act, S.PREPARE + TASKS * i + m + 1)
                    if kind == "prepare":
                        prepare_hi(1 - S.where(n)[0], task, m)
                        continue
                    pv_done.wait(act, S.UNITS * i + unit - 1)
                    s0 = task[0][1]
                    act.copy(pt[unit % 2][0][:, s0:s0 + len(task), at:at + P],
                             task_bank(m)[:, 0:len(task) * P].rearrange("p (s c) -> p s c", c=P)).then_inc(
                                 t_hi.sem, 1)

            def output(i, g):
                pv_done.wait(act, S.UNITS * i + 2 * g + 2)
                o_out[g % 2].wait(act, 16 * (S.GROUPS // 2 * i + g // 2))
                act.copy(o_st[g % 2][:], bank[:, 7, 0:GQ]).then_inc(o_done.sem, 1)

            def step(i, n, last):
                if not (last and n + S.AHEAD >= S.STEPS):
                    weights(i, n + S.AHEAD, last)
                pair, m = S.where(n)[0], n % S.PAIR_STEPS
                if m == S.VALUES_AT and not (last and pair == 1):
                    values_hi(2 * i + pair + 1, 1 - pair)

            def body(i, last):
                for n in range(S.STEPS):
                    m = n + S.OUTPUT_LAG
                    if not (last and m >= S.STEPS):
                        step(i, m, last)
                    if n % 4 == 3:
                        output(i, n // 4)
                    if not (last and m >= S.STEPS):
                        transposed_hi(i, m, last)

            for m in range(S.PREPARE):
                t_done.wait(act, m + 1)
                prepare_hi(0, m, m)
            v_in.wait(act, 16)
            const_done.wait(act, 4)
            act.copy(v[0][0][:].rearrange("p t (b c) -> p t b c", b=3)[:, :, ::2, :],
                     v_raw).then_inc(v_hi.sem, 1)
            for n in range(S.AHEAD):
                weights(0, n)
            for n in range(S.OUTPUT_LAG):
                step(0, n, False)
                transposed_hi(0, n, False)
            bodies(act, body)

        @block.gpsimd
        def _(pool):
            weighted.start(pool)

            def weigh(i, n):
                used = (S.where(n)[2] + 1) * P
                scanned.wait(pool, S.STEPS * i + n + 1)
                taken.wait(pool, S.STEPS * i + n + 1)
                b = take[n % 4][:, 0:used]
                pool.tensor_tensor(b, b, rest[n % 2][:, SEQ - used + 1:SEQ + 1], ALU.mult).then_inc(
                    weighted.sem, 1)

            def body(i, last):
                for n in range(S.STEPS):
                    if not (last and n + S.AHEAD >= S.STEPS):
                        weigh(i, n + S.AHEAD)

            for n in range(S.AHEAD):
                weigh(0, n)
            bodies(pool, body)

        @block.vector
        def _(dve):
            scanned.start(dve)
            t_lo.start(dve)
            for x in (*v[0], *v[1]):
                dve.memset(f32(x[:, :, SB_DIM:2 * SB_DIM]), 0.0).then_inc(const_done.sem, 1)
            for x in (*pt[0], *pt[1]):
                dve.memset(f32(x[:, 0, 0:P]), 0.0).then_inc(const_done.sem, 1)
            for x in rest:
                dve.memset(x[:, SEQ:SEQ + 1], 1.0).then_inc(const_done.sem, 1)
            dve.memset(zero[:], 0.0).then_inc(const_done.sem, 1)
            const_done.wait(dve, 11)

            def scan(i, n):
                used = (S.where(n)[2] + 1) * P
                kept.wait(dve, S.STEPS * i + n + 1)
                weighted.wait(dve, S.STEPS * i + n - 1)
                dve.tensor_tensor_scan(rest[n % 2][:, SEQ - used:SEQ][:, ::-1], keep[n % 2][:, 0:used][:, ::-1],
                                       zero[:].broadcast_to([P, used]), 1.0, ALU.mult, ALU.add).then_inc(
                                           scanned.sem, 1)

            def prepare_lo(pair, index, m):
                hi, lo, rows = operand(pair, index)
                dve.tensor_tensor(lo, task_bank(m)[rows, 0:hi.shape[1]], f32(hi[rows, :]), ALU.subtract).then_inc(
                    t_lo.sem, 1)

            def values_lo(p, pair):
                v_hi.wait(dve, p + 1)
                hi, lo = (x[:].rearrange("p t (b c) -> p t b c", b=3)[:, :, ::2, :] for x in v[pair])
                dve.tensor_tensor(lo, v_raw, f32(hi), ALU.subtract).then_inc(v_lo.sem, 1)

            def transposed_lo(i, n, last):
                unit, at = n // 2, (n % 2) * P
                for j, (kind, task) in enumerate(S.tasks(n, last)):
                    m = S.before(n, last) + j
                    t_hi.wait(dve, S.PREPARE + TASKS * i + m + 1)
                    if kind == "prepare":
                        prepare_lo(1 - S.where(n)[0], task, m)
                        continue
                    s0 = task[0][1]
                    hi, lo = (x[:, s0:s0 + len(task), at:at + P] for x in pt[unit % 2])
                    dve.tensor_tensor(lo, task_bank(m)[:, 0:len(task) * P].rearrange(
                        "p (s c) -> p s c", c=P), f32(hi), ALU.subtract).then_inc(t_lo.sem, 1)

            def body(i, last):
                for n in range(S.STEPS):
                    if not (last and n + S.AHEAD >= S.STEPS):
                        scan(i, n + S.AHEAD)
                    pair, m = S.where(n)[0], n % S.PAIR_STEPS
                    if m == S.VALUES_AT and not (last and pair == 1):
                        values_lo(2 * i + pair + 1, 1 - pair)
                    transposed_lo(i, n, last)

            for m in range(S.PREPARE):
                t_hi.wait(dve, m + 1)
                prepare_lo(0, m, m)
            values_lo(0, 0)
            for n in range(S.AHEAD):
                scan(0, n)
            bodies(dve, body)

        @block.tensor
        def _(pe):
            pv_done.start(pe)
            ident = io["ident"]

            def scores(i, n):
                pair, a, q = S.where(n)
                if n % S.PAIR_STEPS == 0:
                    last_task = S.before((n - S.PAIR_STEPS) + S.PREPARE_AT[-1] + 1) if n else 0
                    t_lo.wait(pe, S.PREPARE + TASKS * i + last_task)
                taken.wait(pe, S.STEPS * i + n - 1)
                first, chunks, used = score_columns(q)
                for at, width, key in chunks:
                    for k in k_tt[pair]:
                        pe.matmul(score[n % 2][:, at:at + width], q_st[pair][:, a, q * P:(q + 1) * P],
                                  k[:, a, key:key + width], start=k is k_tt[pair][0],
                                  stop=k is k_tt[pair][1] and key + width < used)
                end = first + used
                pe.matmul(score[n % 2][:, end - P:end], io["ident16"][:], io["causal_mask"][:, 0:P],
                          start=False, stop=True).then_inc(s_done.sem, 1)

            def prepare(p, index, m):
                kind, a, tile, tiles = S.PREPARE_TASKS[index]
                raw_in[kind].wait(pe, 64 * (p + 1))
                for c in range(tiles):
                    last = pe.transpose(task_bank(m)[:, c * P:(c + 1) * P],
                                        raw[kind][:, tile + c, a, :, :].rearrange("p i c -> p (i c)"),
                                        ident[:])
                last.then_inc(t_done.sem, 1)

            def transposes(i, n, last):
                weighted.wait(pe, S.STEPS * i + n + 1)
                for j, (kind, task) in enumerate(S.tasks(n, last)):
                    m = S.before(n, last) + j
                    t_lo.wait(pe, S.PREPARE + TASKS * i + m - 2)
                    if kind == "prepare":
                        prepare(2 * i + n // S.PAIR_STEPS + 1, task, m)
                        continue
                    for c, (k, _) in enumerate(task):
                        t = pe.transpose(task_bank(m)[:, c * P:(c + 1) * P],
                                         take[n % 4][:, k * P:(k + 1) * P], ident[:])
                    t.then_inc(t_done.sem, 1)

            def values(i, unit, last):
                g, a, pair = unit // 2, unit % 2, unit // (S.UNITS // 2)
                last_q = 2 * (g % 4) + 1
                t_lo.wait(pe, S.PREPARE + TASKS * i + S.before(2 * unit + 2, last))
                if unit % (S.UNITS // 2) == 0:
                    v_lo.wait(pe, 2 * i + pair + 1)
                if a == 0:
                    o_done.wait(pe, S.GROUPS * i + g)
                order = [(last_q, 0)] + [(k, k + 1) for k in range(last_q)]
                for k, slot in order:
                    done = product(pe, bank[:, 7, 0:GQ],
                                   [x[:, k, a * SB_DIM:a * SB_DIM + P] for x in v[pair]],
                                   [x[:, slot, :] for x in pt[unit % 2]], a == 0 and k == last_q,
                                   a == 1 and k == last_q - 1)
                done.then_inc(pv_done.sem, 1)

            def step(i, n, last):
                if not (last and n + S.AHEAD + 1 >= S.STEPS):
                    scores(i, n + S.AHEAD + 1)
                if not (last and n >= S.STEPS):
                    transposes(i, n, last)

            def body(i, last):
                for n in range(S.STEPS):
                    step(i, n + S.VALUES_LAG, last)
                    if n % 2 == 1:
                        values(i, n // 2, last)

            const_done.wait(pe, 11)
            for m in range(S.PREPARE):
                if m >= 3:
                    t_lo.wait(pe, m - 2)
                prepare(0, m, m)
            for n in range(S.AHEAD + 1):
                scores(0, n)
            for n in range(S.VALUES_LAG):
                step(0, n, False)
            bodies(pe, body)


def sb_sample_stage(nc, io, scratch):
    PAIRS = SB_HEADS // 2
    HALF = PAIRS // 2
    STEPS = 2 * DEC_BATCH
    ROWS = 2 * DEC_SEQ
    with nc.cleanup_on_exit(), ExitStack() as ctx:
        def sb(name, shape, dt=F32):
            return ctx.enter_context(nc.sbuf_tensor(name, shape, dt))

        def signal(name, credit=0):
            return Signal(nc, name, credit)

        q_tok = sb("f_q_tok", [P, PAIRS, P])
        k_tok = sb("f_k_tok", [P, PAIRS, P])
        cache_k = sb("f_ck", [P, DEC_BATCH, PAIRS, P])
        cache_v = sb("f_cv", [P, DEC_BATCH, PAIRS, P])
        new_v = sb("f_nv", [DEC_SEQ, DEC_BATCH, PAIRS, P])
        q_z = sb("f_qz", [P, DEC_BATCH, PAIRS, P])
        new_kT = sb("f_nkT", [P, PAIRS, P])
        keysT = [sb(f"f_kT{u}", [P, PAIRS, KEYS]) for u in range(2)]
        keep = [sb(f"f_u{u}", [P, KEYS]) for u in range(2)]
        take = [sb(f"f_b{u}", [P, KEYS]) for u in range(2)]
        rest = [sb(f"f_r{u}", [P, KEYS + 1]) for u in range(2)]
        wT = [sb(f"f_wT{u}", [P, 2, P]) for u in range(2)]
        o_all = sb("f_o", [P, PAIRS, P])
        zero = sb("f_zero", [P, 1])
        bank = ctx.enter_context(nc.psum_tensor("f_ps", [P, 8, 512], F32))
        SMP = slice(SEQ, TOK)

        tok_in, new_v_in = signal("f_tok"), signal("f_nv_in")
        cache_in = [signal(f"f_c{b}") for b in range(DEC_BATCH)]
        zeroed, const_done = signal("f_zeroed"), signal("f_const")
        qt_done, q_out, nk_out = signal("f_qt"), signal("f_qo"), signal("f_nko")
        kt_done, kt_past, kt_new = signal("f_kt"), signal("f_ktp"), signal("f_ktn")
        s_done, kept, taken = signal("f_s"), signal("f_kept"), signal("f_taken")
        scanned, weighted = signal("f_scan"), signal("f_weighted")
        t_done, t_out, pv_done, o_out, stored = (signal(f"f_{n}") for n in ("t", "to", "pv", "oo", "st"))

        block = ctx.enter_context(nc.Block())

        @block.sync
        def _(sp):
            sp.dma_start(q_tok[:].rearrange("p a c -> p (a c)"), scratch["q"][SMP, :]).then_inc(tok_in.sem, 16)
            sp.dma_start(k_tok[:].rearrange("p a c -> p (a c)"),
                         io["new_s_sb_k"][0].rearrange("b s h c -> (b s) (h c)")).then_inc(tok_in.sem, 16)
            for b in range(DEC_BATCH):
                for dst, src in ((cache_k, "cache_sb_k"), (cache_v, "cache_sb_v")):
                    sp.dma_start(dst[:, b, :, :].rearrange("p a c -> p (a c)"),
                                 io[src][0, b].rearrange("s h c -> s (h c)")).then_inc(cache_in[b].sem, 16)
                if b == 0:
                    sp.dma_start(new_v[:].rearrange("p b a c -> p b (a c)"),
                                 io["new_s_sb_v"][0].rearrange("b s h c -> s b (h c)")).then_inc(
                                     new_v_in.sem, 16)
            o_out.wait(sp, 2 * STEPS)
            sp.dma_start(scratch["oT"][:, :, SMP].rearrange("h p c -> p h c"), o_all[:]).then_inc(
                stored.sem, 16)
            stored.wait(sp, 16)

        @block.gpsimd
        def _(pool):
            pool.memset(q_z[:, 0:DEC_BATCH // 2], 0.0).then_inc(zeroed.sem, 1)

        @block.scalar
        def _(act):
            zeroed.wait(act, 2)
            for j in range(2):
                qt_done.wait(act, j + 1)
                for c in range(HALF):
                    for a in range(2):
                        rows, at = slice(a * SB_DIM, (a + 1) * SB_DIM), (2 * c + a) * DEC_SEQ
                        act.copy(q_z[rows, :, j * HALF + c, at:at + DEC_SEQ],
                                 bank[rows, j, c * P:(c + 1) * P].rearrange("p (b q) -> p b q", b=DEC_BATCH)
                                 ).then_inc(q_out.sem, 1)

            def past_keys(b):
                for j in range(2):
                    kt_done.wait(act, 2 * b + j + 1)
                    if b >= 2:
                        s_done.wait(act, 2 * (b - 1))
                    act.copy(keysT[b % 2][:, j * HALF:(j + 1) * HALF, 0:PAST], bank[:, j, :].rearrange(
                        "p (a c) -> p a c", a=HALF)).then_inc(kt_past.sem, 1)

            def sigmoids(n):
                z = bank[:, 2 + n % 2, 0:KEYS]
                s_done.wait(act, n + 1)
                if n >= 2:
                    scanned.wait(act, n - 1)
                    t_done.wait(act, n - 1)
                act.activation(keep[n % 2][:], z, ACT.Sigmoid, scale=-SB_SCALE).then_inc(kept.sem, 1)
                act.activation(take[n % 2][:], z, ACT.Sigmoid, scale=SB_SCALE).then_inc(taken.sem, 1)

            past_keys(0)
            sigmoids(0)
            for n in range(STEPS):
                b = n // 2
                if n % 2 == 0 and b + 1 < DEC_BATCH:
                    past_keys(b + 1)
                if n + 1 < STEPS:
                    sigmoids(n + 1)
                t_done.wait(act, n + 1)
                if n >= 2:
                    pv_done.wait(act, n - 1)
                act.copy(wT[n % 2][:, 0, :], bank[:, 4 + n % 2, 0:P]).then_inc(t_out.sem, 1)
                act.copy(wT[n % 2][0:DEC_SEQ, 1, :], bank[0:DEC_SEQ, 4 + n % 2, P:2 * P]).then_inc(t_out.sem, 1)

        @block.vector
        def _(dve):
            dve.memset(q_z[:, DEC_BATCH // 2:], 0.0).then_inc(zeroed.sem, 1)
            for x in rest:
                dve.memset(x[:, KEYS:KEYS + 1], 1.0).then_inc(const_done.sem, 1)
            dve.memset(zero[:], 0.0).then_inc(const_done.sem, 1)
            const_done.wait(dve, 3)
            for j in range(2):
                qt_done.wait(dve, 3 + j)
                dve.tensor_copy(new_kT[:, j * HALF:(j + 1) * HALF, :], bank[:, 2 + j, :].rearrange(
                    "p (a c) -> p a c", a=HALF)).then_inc(nk_out.sem, 1)
            nk_out.wait(dve, 2)

            def new_keys(b):
                if b >= 2:
                    s_done.wait(dve, 2 * (b - 1))
                dve.tensor_copy(keysT[b % 2][:, :, PAST:KEYS],
                                new_kT[:, :, b * DEC_SEQ:(b + 1) * DEC_SEQ]).then_inc(kt_new.sem, 1)

            def output(n):
                b, half = n // 2, n % 2
                pv_done.wait(dve, n + 1)
                for a in range(2):
                    rows = slice(a * SB_DIM, (a + 1) * SB_DIM)
                    dve.tensor_copy(
                        o_all[rows, half * HALF:(half + 1) * HALF, b * DEC_SEQ:(b + 1) * DEC_SEQ],
                        bank[rows, 6 + n % 2, 0:HALF * ROWS].rearrange("p (c i q) -> p c i q", c=HALF, i=2)[
                            :, :, a, :]).then_inc(o_out.sem, 1)

            new_keys(0)
            for n in range(STEPS):
                b = n // 2
                if n % 2 == 0 and b + 1 < DEC_BATCH:
                    new_keys(b + 1)
                kept.wait(dve, n + 1)
                if n >= 2:
                    weighted.wait(dve, n - 1)
                dve.tensor_tensor_scan(rest[n % 2][:, 0:KEYS][:, ::-1], keep[n % 2][:][:, ::-1],
                                       zero[:].broadcast_to([P, KEYS]), 1.0, ALU.mult, ALU.add).then_inc(
                                           scanned.sem, 1)
                scanned.wait(dve, n + 1)
                taken.wait(dve, n + 1)
                dve.tensor_tensor(take[n % 2][:], take[n % 2][:], rest[n % 2][:, 1:KEYS + 1],
                                  ALU.mult).then_inc(weighted.sem, 1)
                if n >= 1:
                    output(n - 1)
            output(STEPS - 1)

        @block.tensor
        def _(pe):
            ident = io["ident"]
            tok_in.wait(pe, 32)
            for x, src in enumerate((q_tok, k_tok)):
                for j in range(2):
                    for c in range(HALF):
                        last = pe.transpose(bank[:, 2 * x + j, c * P:(c + 1) * P], src[:, j * HALF + c, :],
                                            ident[:])
                    last.then_inc(qt_done.sem, 1)

            def keys(b):
                cache_in[b].wait(pe, 32)
                for j in range(2):
                    if b == 0:
                        q_out.wait(pe, 2 * HALF * (j + 1))
                    else:
                        kt_past.wait(pe, 2 * b - 1 + j)
                    for c in range(HALF):
                        last = pe.transpose(bank[:, j, c * P:(c + 1) * P], cache_k[:, b, j * HALF + c, :],
                                            ident[:])
                    last.then_inc(kt_done.sem, 1)

            def scores(n):
                b, half = n // 2, n % 2
                kt_past.wait(pe, 2 * b + half + 1)
                kt_new.wait(pe, b + 1)
                if n >= 2:
                    taken.wait(pe, n - 1)
                z = bank[:, 2 + n % 2, 0:KEYS]
                for c in range(HALF):
                    pair = half * HALF + c
                    pe.matmul(z, q_z[:, b, pair, :], keysT[b % 2][:, pair, :], start=c == 0, stop=False)
                pe.matmul(z[:, PAST:KEYS], io["ident16"][:], io["causal_mask"][:, P:P + DEC_SEQ],
                          start=False, stop=True).then_inc(s_done.sem, 1)

            def transposes(n):
                weighted.wait(pe, n + 1)
                if n >= 2:
                    t_out.wait(pe, 2 * (n - 1))
                pe.transpose(bank[:, 4 + n % 2, 0:P], take[n % 2][:, 0:PAST], ident[:])
                pe.transpose(bank[0:DEC_SEQ, 4 + n % 2, P:2 * P], take[n % 2][:, PAST:KEYS],
                             ident[:]).then_inc(t_done.sem, 1)

            def values(n):
                b, half = n // 2, n % 2
                t_out.wait(pe, 2 * (n + 1))
                if n >= 2:
                    o_out.wait(pe, 2 * (n - 1))
                for c in range(HALF):
                    pair, cols = half * HALF + c, slice(c * ROWS, (c + 1) * ROWS)
                    out = bank[:, 6 + n % 2, cols]
                    pe.matmul(out, cache_v[:, b, pair, :], wT[n % 2][:, 0, cols], start=True, stop=False)
                    last = pe.matmul(out, new_v[:, b, pair, :], wT[n % 2][0:DEC_SEQ, 1, cols],
                                     start=False, stop=True)
                last.then_inc(pv_done.sem, 1)

            keys(0)
            nk_out.wait(pe, 2)
            scores(0)
            for n in range(STEPS):
                if n % 2 == 0 and n // 2 + 1 < DEC_BATCH:
                    keys(n // 2 + 1)
                if n + 1 < STEPS:
                    scores(n + 1)
                if n == 1:
                    new_v_in.wait(pe, 16)
                if n >= 1:
                    values(n - 1)
                transposes(n)
            values(STEPS - 1)


def build(nc, io):
    with ExitStack() as ctx:
        def sb(name, shape, dt=F32):
            return ctx.enter_context(nc.sbuf_tensor(name, shape, dt))

        io["ident"] = sb("ident", [P, P])
        io["ident16"] = sb("ident16", [P, P], BF16)
        io["chunk_mask"] = sb("chunk_mask", [P, P], BF16)
        io["causal_mask"] = sb("causal_mask", [P, P + DEC_SEQ], BF16)
        scratch = {
            "qr": nc.dram_tensor("scratch_qr", (HEADS, P, TOK), F32, kind="Internal").ap(),
            "oT": nc.dram_tensor("scratch_oT", (KT, P, TOK), F32, kind="Internal").ap(),
        }
        scratch["q"] = nc.dram_tensor("scratch_q", (TOK, D_MODEL), F32, kind="Internal").ap()
        with ExitStack() as mla:
            io["cqT"] = [mla.enter_context(nc.sbuf_tensor(f"cqT{s}", [P, QT, TOK], F32R)) for s in "hl"]
            io["ckvT"] = [mla.enter_context(nc.sbuf_tensor(f"ckvT{s}", [P, CT, TOK], F32R)) for s in "hl"]
            io["krT"] = [mla.enter_context(nc.sbuf_tensor(f"krT{s}", [P, TOK], F32R)) for s in "hl"]
            raw = raw_weights(nc, mla)
            mla_input_stage(nc, io, scratch, raw)
            io["q_smp"] = mla.enter_context(nc.sbuf_tensor("q_smp", [P, HEADS, P], F32))
            mla_attention_stage(nc, io, scratch, raw)
            mla_sample_stage(nc, io, scratch)
        io["x"] = sb("x", [P, NT, D_MODEL])
        with ExitStack() as first:
            tokens = tokens_split(nc, first, "h0")
            output_and_mlp_stage(nc, io, scratch, 0, io["mla_w_o"][0], True, tokens, io["norm_mix"][1:2, :])
            with ExitStack() as pair:
                raw = raw_heads(nc, pair, "d")
                sb_input_stage(nc, io, scratch, tokens[1], raw)
        sb_attention_stage(nc, io, scratch, raw)
        sb_sample_stage(nc, io, scratch)
        tokens = tokens_split(nc, ctx, "h1")
        output_and_mlp_stage(nc, io, scratch, 1, io["sb_w_o"][0], False, tokens,
                             io["norm_final"].rearrange("(o d) -> o d", o=1))


_INS = ["x_prompt", "x_sample", "cache_mla_ckv", "cache_mla_krope", "cache_sb_k", "cache_sb_v",
        "norm_mix", "norm_mlp", "norm_final", "mla_w_in", "mla_g_q", "mla_w_qb", "mla_g_kv",
        "mla_w_kvb", "mla_w_o", "sb_w_in", "sb_w_o", "mlp_w_up", "mlp_w_down"]
_OUTS = [("y_prompt", (1, SEQ, D_MODEL)), ("y_sample", (DEC_BATCH, DEC_SEQ, D_MODEL)),
         ("new_p_ckv", (1, 1, SEQ, KV_LORA)), ("new_p_krope", (1, 1, SEQ, ROPE)),
         ("new_p_sb_k", (1, 1, SEQ, SB_HEADS, SB_DIM)), ("new_p_sb_v", (1, 1, SEQ, SB_HEADS, SB_DIM)),
         ("new_s_ckv", (1, DEC_BATCH, DEC_SEQ, KV_LORA)), ("new_s_krope", (1, DEC_BATCH, DEC_SEQ, ROPE)),
         ("new_s_sb_k", (1, DEC_BATCH, DEC_SEQ, SB_HEADS, SB_DIM)),
         ("new_s_sb_v", (1, DEC_BATCH, DEC_SEQ, SB_HEADS, SB_DIM))]


def shape_constants():
    half = ROPE // 2
    inv = (THETA ** (-np.arange(0, ROPE, 2) / ROPE)).astype(np.float32)
    pos = np.arange(TOK, dtype=np.float32)
    pos[SEQ:] = PAST + np.arange(P) % DEC_SEQ
    ang = (pos[:, None] * inv[None, :]).astype(np.float32).astype(np.float64)
    cos, sin = np.cos(ang).astype(np.float32), np.sin(ang).astype(np.float32)

    def by_tile(a, b):
        both = np.concatenate([a, b], axis=1).reshape(NT, P, 2 * half)
        return np.ascontiguousarray(both.transpose(1, 0, 2))

    q, k = np.arange(P)[:, None], np.arange(P)[None, :]
    bf = mybir.dt.np(BF16)
    new = np.where(np.arange(DEC_SEQ)[None, :] < q % DEC_SEQ, 0.0, MASKED)
    return {
        "cos_dram": by_tile(cos, cos), "sin_dram": by_tile(-sin, sin),
        "ident_dram": np.eye(P, dtype=np.float32), "ident16_dram": np.eye(P).astype(bf),
        "chunk_mask_dram": np.where(k // CHUNK <= q // CHUNK, 0.0, MASKED).astype(bf),
        "causal_mask_dram": np.concatenate([np.where(k < q, 0.0, MASKED), new], axis=1).astype(bf),
    }


def kernel(**inputs):
    import concourse.bacc as _bacc
    from concourse.bass_utils import run_bass_kernel_spmd as _run

    nc = _bacc.Bacc("TRN2", target_bir_lowering=False, num_devices=1)
    arrays, io = {}, {}
    for name in _INS:
        arrays[f"in_{name}"] = np.ascontiguousarray(inputs[name])
    arrays.update({f"in_{name}": a for name, a in shape_constants().items()})
    for name, a in arrays.items():
        io[name[3:]] = nc.dram_tensor(name, a.shape, mybir.dt.from_np(a.dtype), kind="ExternalInput").ap()
    for name, shape in _OUTS:
        io[name] = nc.dram_tensor(name, shape, F32, kind="ExternalOutput").ap()
    build(nc, io)
    r = _run(nc, [arrays], core_ids=[0])
    return tuple(r.results[0][name] for name, _ in _OUTS)
```
